# Optimizing a Trainium2 kernel written in Bass

```python
import math
import jax
import jax.numpy as jnp
from jax import lax
import numpy as np
import jax, jax.numpy as jnp

D_MODEL = 1024
BATCH = 1
SEQ = 256
DEPTH = 2

CTX_LEN = 256
GRID_W = 64
RET_HEADS = 4
RET_DK = 128
RET_DV = 128
RET_W = RET_HEADS * RET_DV
RET_CHUNK = 128
NA_HEADS = 8
NA_DH = 64
NA_W = NA_HEADS * NA_DH
NA_WIN_ROWS = 8
NA_WIN_COLS = 16
NA_ROW_BLOCK = 8
GQA_HEADS = 8
GQA_KV_HEADS = 2
GQA_DH = 64
GQA_W = GQA_HEADS * GQA_DH
GQA_KV_W = GQA_KV_HEADS * GQA_DH
Q_BLOCK = 128
ROPE_THETA = 10000.0
EPS = 1e-6
N_BRANCH = 3
IN_SPLITS = (RET_W, RET_W, RET_W, RET_W, NA_W, NA_W, NA_W, NA_W, GQA_W, GQA_KV_W, GQA_KV_W, GQA_W, N_BRANCH * D_MODEL)
IN_COLS = 4 * RET_W + 4 * NA_W + 2 * GQA_W + 2 * GQA_KV_W + N_BRANCH * D_MODEL


def rms_norm(x, w):
    xf = x.astype(jnp.float32)
    y = xf * lax.rsqrt(jnp.mean(xf * xf, axis=-1, keepdims=True) + EPS)
    return (y * w.astype(jnp.float32)).astype(x.dtype)

def heads(a, h):
    return a.reshape(a.shape[:-1] + (h, a.shape[-1] // h))

def split_cols(p):
    bounds = np.cumsum(IN_SPLITS)[:-1].tolist()
    return jnp.split(p, bounds, axis=-1)

def _flip(a, rev):
    return a[:, ::-1] if rev else a

def axial_rope(x):
    n, dh = x.shape[1], x.shape[-1]
    half = dh // 2
    quarter = half // 2
    t = jnp.arange(n)
    pos_r = (t // GRID_W).astype(jnp.float32)
    pos_c = (t % GRID_W).astype(jnp.float32)
    freqs = ROPE_THETA ** (-jnp.arange(quarter, dtype=jnp.float32) / quarter)

    def rot(xa, pos):
        ang = pos[:, None] * freqs[None, :]
        cos = jnp.cos(ang)[None, :, None, :]
        sin = jnp.sin(ang)[None, :, None, :]
        x1, x2 = xa[..., :quarter], xa[..., quarter:]
        return jnp.concatenate([x1 * cos - x2 * sin, x2 * cos + x1 * sin], axis=-1)

    xf = x.astype(jnp.float32)
    return jnp.concatenate([rot(xf[..., :half], pos_r), rot(xf[..., half:], pos_c)], axis=-1).astype(x.dtype)

def attend(q, k, v):
    s = jnp.einsum('btkgd,bskd->bkgts', q, k).astype(jnp.float32) * (q.shape[-1] ** -0.5)
    p = jax.nn.softmax(s, axis=-1)
    return jnp.einsum('bkgts,bskd->btkgd', p, v)

def ret_chunkwise(q, k, v, log_g, s0):
    b, t, h, dk = q.shape
    dv = v.shape[-1]
    c = RET_CHUNK
    n = t // c
    qc = q.reshape(b, n, c, h, dk)
    kc = k.reshape(b, n, c, h, dk)
    vc = v.reshape(b, n, c, h, dv)
    pos = jnp.arange(c, dtype=jnp.float32)
    diff = pos[:, None] - pos[None, :]
    decay = jnp.where(diff >= 0, jnp.exp(jnp.maximum(diff, 0.0)[None] * log_g[:, None, None]), 0.0)
    scores = jnp.einsum('bnihd,bnjhd->bnhij', qc, kc) * decay[None, None]
    intra = jnp.einsum('bnhij,bnjhe->bnihe', scores, vc)
    zeta = jnp.exp((c - 1 - pos)[None, :] * log_g[:, None])
    u = jnp.einsum('bnjhd,hj,bnjhe->nbhde', kc, zeta, vc)
    g_chunk = jnp.exp(c * log_g)[None, :, None, None]

    def step(s, u_n):
        return g_chunk * s + u_n, s

    s_fin, s_prev = lax.scan(step, s0, u)
    xi = jnp.exp((pos + 1.0)[None, :] * log_g[:, None])
    inter = jnp.einsum('bnihd,hi,nbhde->bnihe', qc, xi, s_prev)
    return (intra + inter).reshape(b, t, h, dv), s_fin

def ret_state(k, v, log_g):
    t = k.shape[1]
    pos = jnp.arange(t, dtype=jnp.float32)
    w = jnp.exp((t - 1 - pos)[None, :] * log_g[:, None])
    return jnp.einsum('bthd,ht,bthe->bhde', k, w, v)

def bidir_retention(q, k, v, qc, kc, vc, log_g, need_ctx):
    b, _, h, dk = q.shape
    dv = v.shape[-1]
    o_lat, o_ctx = [], []
    for d in range(2):
        rev = d == 1
        if need_ctx:
            s0 = jnp.zeros((b, h, dk, dv), jnp.float32)
            oc, s_ctx = ret_chunkwise(_flip(qc, rev), _flip(kc, rev), _flip(vc, rev), log_g[d], s0)
            o_ctx.append(_flip(oc, rev))
        else:
            s_ctx = ret_state(_flip(kc, rev), _flip(vc, rev), log_g[d])
        ol, _ = ret_chunkwise(_flip(q, rev), _flip(k, rev), _flip(v, rev), log_g[d], s_ctx)
        o_lat.append(_flip(ol, rev))
    return o_lat[0] + o_lat[1], (o_ctx[0] + o_ctx[1] if need_ctx else None)

def head_group_norm(o, w):
    mu = jnp.mean(o, axis=-1, keepdims=True)
    var = jnp.mean(jnp.square(o - mu), axis=-1, keepdims=True)
    y = (o - mu) * lax.rsqrt(var + EPS)
    return y.reshape(o.shape[0], o.shape[1], -1) * w.astype(jnp.float32)

def neighbourhood_attention(q, k, v, kc, vc, rpb, rows):
    b, n, h, dh = q.shape
    wr = min(NA_WIN_ROWS, rows)
    qcb = NA_WIN_COLS
    ncb = GRID_W // qcb
    band = 2 * qcb
    qcol = np.arange(ncb)[:, None] * qcb + np.arange(qcb)[None, :]
    cstart = np.clip(qcol - NA_WIN_COLS // 2, 0, GRID_W - NA_WIN_COLS)
    bstart = np.clip(np.arange(ncb) * qcb - NA_WIN_COLS // 2, 0, GRID_W - band)
    kcol = bstart[:, None] + np.arange(band)[None, :]
    col_ok = jnp.asarray((kcol[:, None, :] >= cstart[:, :, None]) & (kcol[:, None, :] < cstart[:, :, None] + NA_WIN_COLS))
    dc_idx = np.clip(kcol[:, None, :] - qcol[:, :, None] + NA_WIN_COLS - 1, 0, 2 * NA_WIN_COLS - 2)
    rpb_c = rpb.astype(jnp.float32)[:, :, dc_idx]

    kg = k.reshape(b, rows, GRID_W, h, dh)[:, :, kcol]
    vg = v.reshape(b, rows, GRID_W, h, dh)[:, :, kcol]
    rb = math.gcd(rows, NA_ROW_BLOCK)
    nrb = rows // rb
    qblocks = q.reshape(b, nrb, rb, ncb, qcb, h, dh).transpose(1, 0, 2, 3, 4, 5, 6)
    scale = dh ** -0.5
    n_loc = wr * band

    def block(args):
        i, qb = args
        r = i * rb + jnp.arange(rb)
        rs = jnp.clip(r - wr // 2, 0, rows - wr)
        ridx = rs[:, None] + jnp.arange(wr)[None, :]
        kb = jnp.take(kg, ridx, axis=1)
        vb = jnp.take(vg, ridx, axis=1)
        dr_idx = ridx - r[:, None] + NA_WIN_ROWS - 1
        bias = rpb_c[:, dr_idx].transpose(0, 1, 3, 4, 2, 5)
        s = jnp.einsum('brjqhd,brwjkhd->bhrjqwk', qb, kb).astype(jnp.float32) * scale + bias[None]
        s = jnp.where(col_ok[:, :, None, :], s, -jnp.inf)
        s_ctx = jnp.einsum('brjqhd,blhd->bhrjql', qb, kc).astype(jnp.float32) * scale
        s_all = jnp.concatenate([s.reshape(s.shape[:5] + (n_loc,)), s_ctx], axis=-1)
        p = jax.nn.softmax(s_all, axis=-1)
        p_loc = p[..., :n_loc].reshape(s.shape)
        p_ctx = p[..., n_loc:]
        return jnp.einsum('bhrjqwk,brwjkhd->brjqhd', p_loc, vb) + jnp.einsum('bhrjql,blhd->brjqhd', p_ctx, vc)

    o = lax.map(block, (jnp.arange(nrb), qblocks))
    return o.transpose(1, 0, 2, 3, 4, 5, 6).reshape(b, n, h * dh)

def gqa_blocks(q, k_all, v_all):
    b, n, hq, dh = q.shape
    hk = k_all.shape[2]
    nb = n // Q_BLOCK
    qb = q.reshape(b, nb, Q_BLOCK, hk, hq // hk, dh).transpose(1, 0, 2, 3, 4, 5)
    o = lax.map(lambda qi: attend(qi, k_all, v_all), qb)
    return o.transpose(1, 0, 2, 3, 4, 5).reshape(b, n, hq * dh)

def merge_branches(ret_o, na_o, gqa_o, gate_logits, w_ret_o, w_na_o, w_gqa_o, w_out):
    dt = w_out.dtype
    g_ret, g_na, g_gqa = jnp.split(jax.nn.sigmoid(gate_logits.astype(jnp.float32)), N_BRANCH, axis=-1)
    m = (g_ret * (ret_o.astype(dt) @ w_ret_o) + g_na * (na_o.astype(dt) @ w_na_o)
         + g_gqa * (gqa_o.astype(dt) @ w_gqa_o))
    return m.astype(dt) @ w_out

def hybrid_layer(x, y, c_silu, cc_silu, ada_w, ada_b, norm_w, w_in, ret_log_decay, ret_gn_w, na_rpb,
                 q_norm_w, k_norm_w, w_ret_o, w_na_o, w_gqa_o, w_out, need_ctx):
    b, n, _ = x.shape
    l = y.shape[1]
    rows = n // GRID_W
    g_grp = GQA_HEADS // GQA_KV_HEADS
    shift_x, scale_x, gate_x = jnp.split((c_silu @ ada_w + ada_b)[:, None, :], 3, axis=-1)
    shift_y, scale_y, gate_y = jnp.split(cc_silu @ ada_w + ada_b, 3, axis=-1)
    hx = rms_norm(x, norm_w) * (1.0 + scale_x) + shift_x
    hy = rms_norm(y, norm_w) * (1.0 + scale_y) + shift_y
    rq, rk, rv, rg, nq, nk, nv, ng, gq, gk, gv, gg, mg = split_cols(hx @ w_in)
    crq, crk, crv, crg, cnq, cnk, cnv, cng, cgq, cgk, cgv, cgg, cmg = split_cols(hy @ w_in)

    log_g = -jnp.exp(ret_log_decay.astype(jnp.float32))
    ksc = RET_DK ** -0.5
    o_lat, o_ctx = bidir_retention(heads(rq, RET_HEADS), heads(rk, RET_HEADS) * ksc, heads(rv, RET_HEADS),
                                   heads(crq, RET_HEADS), heads(crk, RET_HEADS) * ksc, heads(crv, RET_HEADS),
                                   log_g, need_ctx)
    ret_x = head_group_norm(o_lat, ret_gn_w) * jax.nn.silu(rg)

    kc_na = heads(cnk, NA_HEADS)
    vc_na = heads(cnv, NA_HEADS)
    na_x = neighbourhood_attention(heads(nq, NA_HEADS), heads(nk, NA_HEADS), heads(nv, NA_HEADS),
                                   kc_na, vc_na, na_rpb, rows) * jax.nn.silu(ng)

    kc_g = rms_norm(heads(cgk, GQA_KV_HEADS), k_norm_w)
    vc_g = heads(cgv, GQA_KV_HEADS)
    q_g = axial_rope(rms_norm(heads(gq, GQA_HEADS), q_norm_w))
    k_g = axial_rope(rms_norm(heads(gk, GQA_KV_HEADS), k_norm_w))
    k_all = jnp.concatenate([k_g, kc_g], axis=1)
    v_all = jnp.concatenate([heads(gv, GQA_KV_HEADS), vc_g], axis=1)
    gqa_x = gqa_blocks(q_g, k_all, v_all) * jax.nn.silu(gg)

    x = x + gate_x * merge_branches(ret_x, na_x, gqa_x, mg, w_ret_o, w_na_o, w_gqa_o, w_out)

    if need_ctx:
        ret_y = head_group_norm(o_ctx, ret_gn_w) * jax.nn.silu(crg)
        na_y = attend(heads(cnq, NA_HEADS)[:, :, :, None, :], kc_na, vc_na).reshape(b, l, NA_W) * jax.nn.silu(cng)
        qc_g = rms_norm(heads(cgq, GQA_HEADS), q_norm_w).reshape(b, l, GQA_KV_HEADS, g_grp, GQA_DH)
        gqa_y = attend(qc_g, kc_g, vc_g).reshape(b, l, GQA_W) * jax.nn.silu(cgg)
        y = y + gate_y * merge_branches(ret_y, na_y, gqa_y, cmg, w_ret_o, w_na_o, w_gqa_o, w_out)
    return x, y

def first_inputs(seed: int = 0) -> dict:
    key = jax.random.key(seed)
    ks = jax.random.split(key, 18)
    f32 = jnp.float32
    d = D_MODEL

    def nrm(k, shape, scale):
        return jax.random.normal(k, shape, f32) * scale

    decay_base = jnp.asarray(np.log(-np.log(1.0 - 2.0 ** (-5.0 - np.arange(RET_HEADS)))), f32)
    return {
        'x': nrm(ks[0], (BATCH, SEQ, d), 1.0),
        'c': nrm(ks[1], (BATCH, d), 1.0),
        'ctx': nrm(ks[2], (BATCH, CTX_LEN, d), 1.0),
        'c_ctx': nrm(ks[3], (d,), 1.0),
        'ada_w': nrm(ks[4], (DEPTH, d, 3 * d), d ** -0.5),
        'ada_b': nrm(ks[5], (DEPTH, 3 * d), 0.02),
        'norm_w': 1.0 + nrm(ks[6], (DEPTH, d), 0.02),
        'w_in': nrm(ks[7], (DEPTH, d, IN_COLS), d ** -0.5),
        'ret_log_decay': decay_base + nrm(ks[8], (DEPTH, 2, RET_HEADS), 0.1),
        'ret_gn_w': 1.0 + nrm(ks[9], (DEPTH, RET_W), 0.02),
        'na_rpb': nrm(ks[10], (DEPTH, NA_HEADS, 2 * NA_WIN_ROWS - 1, 2 * NA_WIN_COLS - 1), 0.05),
        'q_norm_w': 1.0 + nrm(ks[11], (DEPTH, GQA_DH), 0.02),
        'k_norm_w': 1.0 + nrm(ks[12], (DEPTH, GQA_DH), 0.02),
        'w_ret_o': nrm(ks[13], (DEPTH, RET_W, d), RET_W ** -0.5),
        'w_na_o': nrm(ks[14], (DEPTH, NA_W, d), NA_W ** -0.5),
        'w_gqa_o': nrm(ks[15], (DEPTH, GQA_W, d), GQA_W ** -0.5),
        'w_out': nrm(ks[16], (DEPTH, d, d), d ** -0.5),
        'final_norm_w': 1.0 + nrm(ks[17], (d,), 0.02),
    }

def first_block(x, c, ctx, c_ctx, ada_w, ada_b, norm_w, w_in, ret_log_decay, ret_gn_w, na_rpb,
              q_norm_w, k_norm_w, w_ret_o, w_na_o, w_gqa_o, w_out, final_norm_w):
    c_silu = jax.nn.silu(c)
    cc_silu = jax.nn.silu(c_ctx)
    y = ctx
    for layer in range(DEPTH):
        x, y = hybrid_layer(x, y, c_silu, cc_silu, ada_w[layer], ada_b[layer], norm_w[layer], w_in[layer],
                            ret_log_decay[layer], ret_gn_w[layer], na_rpb[layer], q_norm_w[layer], k_norm_w[layer],
                            w_ret_o[layer], w_na_o[layer], w_gqa_o[layer], w_out[layer],
                            need_ctx=layer < DEPTH - 1)
    return rms_norm(x, final_norm_w)


N_MIXERS = 2
N_A = (DEPTH + 1) // 2
N_B = DEPTH // 2
D_FF = 2816
LRU_WIDTH = D_MODEL
LRU_HEADS = 16
LRU_HEAD_DIM = LRU_WIDTH // LRU_HEADS
LRU_C = 8.0
CONV_WIDTH = 4
SG_WIDTH = D_MODEL
SG_HEADS = 8
SG_HEAD_DIM = SG_WIDTH // SG_HEADS
CHUNK = 128
NORM_EPS = 1e-6


def rms_norm_2(x, g):
    xf = x.astype(jnp.float32)
    y = xf * lax.rsqrt(jnp.mean(xf * xf, axis=-1, keepdims=True) + NORM_EPS)
    return (y * g.astype(jnp.float32)).astype(x.dtype)

def swiglu(x, w_in, w_out):
    g, u = jnp.split(x @ w_in, 2, axis=-1)
    return (jax.nn.silu(g) * u) @ w_out

def causal_depthwise_conv(x, w, b):
    k_width = w.shape[0]
    s = x.shape[1]
    xp = jnp.pad(x, ((0, 0), (k_width - 1, 0), (0, 0)))
    out = b + xp[:, 0:s] * w[0]
    for k in range(1, k_width):
        out = out + xp[:, k:k + s] * w[k]
    return out

def block_diag_linear(x, w, b):
    bsz, s, _ = x.shape
    h, dh, _ = w.shape
    xh = x.reshape(bsz, s, h, dh)
    return (jnp.einsum('bshi,hij->bshj', xh, w) + b).reshape(bsz, s, h * dh)

def rg_lru(x, w_a, b_a, w_x, b_x, lam):
    f32 = jnp.float32
    xf = x.astype(f32)
    gate_a = jax.nn.sigmoid(block_diag_linear(xf, w_a.astype(f32), b_a.astype(f32)))
    gate_x = jax.nn.sigmoid(block_diag_linear(xf, w_x.astype(f32), b_x.astype(f32)))
    log_a = -LRU_C * gate_a * jax.nn.softplus(-lam.astype(f32))
    a = jnp.exp(log_a)
    mult = jnp.sqrt(-jnp.expm1(2.0 * log_a))
    bx = xf * gate_x * mult

    def combine(left, right):
        a_l, b_l = left
        a_r, b_r = right
        return a_l * a_r, a_r * b_l + b_r

    _, h = lax.associative_scan(combine, (a, bx), axis=1)
    return h.astype(x.dtype)

def recurrent_mixer(x, w_in, conv_w, conv_b, gate_a_w, gate_a_b, gate_x_w, gate_x_b, lam, w_out):
    y, r = jnp.split(x @ w_in, 2, axis=-1)
    y = jax.nn.gelu(y)
    r = causal_depthwise_conv(r, conv_w, conv_b)
    h = rg_lru(r, gate_a_w, gate_a_b, gate_x_w, gate_x_b, lam)
    return (y * h) @ w_out

def spatial_gating_mixer(x, w_in, v_norm, w_s, b_s, w_out):
    bsz, s, _ = x.shape
    u, v = jnp.split(jax.nn.gelu(x @ w_in), 2, axis=-1)
    v = rms_norm_2(v, v_norm)
    h, p, _ = w_s.shape
    c = v.shape[-1] // h
    vc = v.reshape(bsz, s // p, p, h, c)
    causal = jnp.tril(jnp.ones((p, p), dtype=bool))
    ws = jnp.where(causal[None], w_s, jnp.zeros_like(w_s))
    sg = jnp.einsum('hpq,bnqhc->bnphc', ws, vc) + b_s.T[:, :, None]
    sg = sg.reshape(bsz, s, h * c)
    return (u * sg) @ w_out

def second_inputs(seed: int = 0) -> dict:
    key = jax.random.key(seed)
    ks = jax.random.split(key, 32)
    f32 = jnp.float32

    def nrm(k, shape, fan_in):
        return jax.random.normal(k, shape, f32) * (fan_in ** -0.5)

    def gain(k, shape):
        return 1.0 + 0.05 * jax.random.normal(k, shape, f32)

    def small(k, shape):
        return 0.01 * jax.random.normal(k, shape, f32)

    x = jax.random.normal(ks[0], (BATCH, SEQ, D_MODEL), f32)

    a0 = jax.random.uniform(ks[14], (N_A, LRU_WIDTH), f32, 0.9, 0.999)
    p0 = a0 ** (1.0 / LRU_C)
    rec_lambda = jnp.log(p0) - jnp.log1p(-p0)

    return {
        "x": x,
        "ffn1_norm": gain(ks[1], (DEPTH, D_MODEL)),
        "ffn1_w_in": nrm(ks[2], (DEPTH, D_MODEL, 2 * D_FF), D_MODEL),
        "ffn1_w_out": nrm(ks[3], (DEPTH, D_FF, D_MODEL), D_FF),
        "mix_norm": gain(ks[4], (DEPTH, D_MODEL)),
        "ffn2_norm": gain(ks[5], (DEPTH, D_MODEL)),
        "ffn2_w_in": nrm(ks[6], (DEPTH, D_MODEL, 2 * D_FF), D_MODEL),
        "ffn2_w_out": nrm(ks[7], (DEPTH, D_FF, D_MODEL), D_FF),
        "rec_w_in": nrm(ks[8], (N_A, D_MODEL, 2 * LRU_WIDTH), D_MODEL),
        "rec_conv_w": nrm(ks[9], (N_A, CONV_WIDTH, LRU_WIDTH), CONV_WIDTH),
        "rec_conv_b": small(ks[10], (N_A, LRU_WIDTH)),
        "rec_gate_a_w": nrm(ks[11], (N_A, LRU_HEADS, LRU_HEAD_DIM, LRU_HEAD_DIM), LRU_HEAD_DIM),
        "rec_gate_a_b": small(ks[12], (N_A, LRU_HEADS, LRU_HEAD_DIM)),
        "rec_gate_x_w": nrm(ks[13], (N_A, LRU_HEADS, LRU_HEAD_DIM, LRU_HEAD_DIM), LRU_HEAD_DIM),
        "rec_gate_x_b": small(ks[15], (N_A, LRU_HEADS, LRU_HEAD_DIM)),
        "rec_lambda": rec_lambda,
        "rec_w_out": nrm(ks[16], (N_A, LRU_WIDTH, D_MODEL), LRU_WIDTH),
        "sg_w_in": nrm(ks[17], (N_B, D_MODEL, 2 * SG_WIDTH), D_MODEL),
        "sg_v_norm": gain(ks[18], (N_B, SG_WIDTH)),
        "sg_w_s": nrm(ks[19], (N_B, SG_HEADS, CHUNK, CHUNK), CHUNK),
        "sg_b_s": 1.0 + 0.1 * jax.random.normal(ks[20], (N_B, SG_HEADS, CHUNK), f32),
        "sg_w_out": nrm(ks[21], (N_B, SG_WIDTH, D_MODEL), SG_WIDTH),
        "final_norm": gain(ks[22], (D_MODEL,)),
    }

def second_block(x, ffn1_norm, ffn1_w_in, ffn1_w_out, mix_norm, ffn2_norm, ffn2_w_in, ffn2_w_out,
              rec_w_in, rec_conv_w, rec_conv_b, rec_gate_a_w, rec_gate_a_b, rec_gate_x_w, rec_gate_x_b,
              rec_lambda, rec_w_out, sg_w_in, sg_v_norm, sg_w_s, sg_b_s, sg_w_out, final_norm):
    h = x
    for i in range(DEPTH):
        h = h + 0.5 * swiglu(rms_norm_2(h, ffn1_norm[i]), ffn1_w_in[i], ffn1_w_out[i])
        hn = rms_norm_2(h, mix_norm[i])
        j = i // N_MIXERS
        if i % N_MIXERS == 0:
            m = recurrent_mixer(hn, rec_w_in[j], rec_conv_w[j], rec_conv_b[j], rec_gate_a_w[j], rec_gate_a_b[j],
                                rec_gate_x_w[j], rec_gate_x_b[j], rec_lambda[j], rec_w_out[j])
        else:
            m = spatial_gating_mixer(hn, sg_w_in[j], sg_v_norm[j], sg_w_s[j], sg_b_s[j], sg_w_out[j])
        h = h + m
        h = h + 0.5 * swiglu(rms_norm_2(h, ffn2_norm[i]), ffn2_w_in[i], ffn2_w_out[i])
    return rms_norm_2(h, final_norm)


def setup_inputs(seed=0):
    out = dict(first_inputs(seed))
    for name, value in second_inputs(seed + 1).items():
        if name != "x":
            out[name + "_2"] = value
    return out


def reference(
    x, c, ctx, c_ctx, ada_w, ada_b, norm_w, w_in, ret_log_decay, ret_gn_w, na_rpb, q_norm_w,
    k_norm_w, w_ret_o, w_na_o, w_gqa_o, w_out, final_norm_w, ffn1_norm_2, ffn1_w_in_2,
    ffn1_w_out_2, mix_norm_2, ffn2_norm_2, ffn2_w_in_2, ffn2_w_out_2, rec_w_in_2, rec_conv_w_2,
    rec_conv_b_2, rec_gate_a_w_2, rec_gate_a_b_2, rec_gate_x_w_2, rec_gate_x_b_2, rec_lambda_2,
    rec_w_out_2, sg_w_in_2, sg_v_norm_2, sg_w_s_2, sg_b_s_2, sg_w_out_2, final_norm_2,
):
    x = first_block(
        x, c, ctx, c_ctx, ada_w, ada_b, norm_w, w_in, ret_log_decay, ret_gn_w, na_rpb, q_norm_w,
        k_norm_w, w_ret_o, w_na_o, w_gqa_o, w_out, final_norm_w,
    )
    return second_block(
        x, ffn1_norm_2, ffn1_w_in_2, ffn1_w_out_2, mix_norm_2, ffn2_norm_2, ffn2_w_in_2,
        ffn2_w_out_2, rec_w_in_2, rec_conv_w_2, rec_conv_b_2, rec_gate_a_w_2, rec_gate_a_b_2,
        rec_gate_x_w_2, rec_gate_x_b_2, rec_lambda_2, rec_w_out_2, sg_w_in_2, sg_v_norm_2,
        sg_w_s_2, sg_b_s_2, sg_w_out_2, final_norm_2,
    )


_drawn_inputs = setup_inputs


def setup_inputs(seed=0):
    import zlib

    import numpy as np

    out = dict(_drawn_inputs(seed))
    spreads = {}
    factors = {'norm_w': 2.894,
     'ret_gn_w': 5.487,
     'na_rpb': 8.0,
     'q_norm_w': 8.0,
     'k_norm_w': 8.0,
     'rec_gate_a_b_2': 60.81,
     'rec_gate_x_b_2': 32.919,
     'sg_v_norm_2': 3.601}
    for name, (base, spread) in spreads.items():
        noise = np.random.default_rng([zlib.crc32(name.encode()), seed]).standard_normal(out[name].shape)
        drawn = base * np.exp(spread * noise) if base else spread * noise
        out[name] = jnp.asarray(drawn.astype(out[name].dtype))
    for name, factor in factors.items():
        out[name] = (out[name] * factor).astype(out[name].dtype)
    return out
```

```python
from contextlib import ExitStack

import numpy as np

import concourse.bass as bass
from concourse import mybir

F32 = mybir.dt.float32
F32R = mybir.dt.float32r
ALU = mybir.AluOpType
ACT = mybir.ActivationFunctionType
AX_X = mybir.AxisListType.X

P = 128
D = 1024
KC = D // P
SEQ = 256
BOTH = 2 * SEQ
DEPTH = 2
GRID_W = 64
ROWS = SEQ // GRID_W
RET_HEADS = 4
NA_HEADS = 8
GQA_HEADS = 8
DH = 64
RPB_COLS = 31
D_FF = 2816
FC = D_FF // P
EPS = 1e-6

RAW = 6
SPLIT = 3
AHEAD = 2

IN_AT = dict(zip(
    "rq rk rv rg nq nk nv ng gq gk gv gg mg".split(),
    np.cumsum([0, 512, 512, 512, 512, 512, 512, 512, 512, 512, 128, 128, 512]).tolist(),
))
GQA_COLS = [np.r_[DH * c:DH * c + DH, DH * (c + 4):DH * (c + 4) + DH] for c in range(4)]


def tile_order():
    out = [("ada", 0, n) for n in range(16)]
    for layer in range(DEPTH):
        ada = [("ada", 0, n) for n in range(16, 24)] + [("ada", 1, n) for n in range(24)] if layer == 0 else []
        for c in range(4):
            for n, name in enumerate(("nk", "nv", "nq", "ng")):
                out.append((name, layer, c))
        for h in range(4):
            for n, name in enumerate(("rk", "rv", "rq", "rg")):
                out.append((name, layer, h))
                out += ada[:2]
                del ada[:2]
        for q in range(4):
            out += [("mg", layer, KC + 2 * q), ("mg", layer, KC + 2 * q + 1), ("w_na_o", layer, q)]
        out += [("gk", layer, 0), ("gv", layer, 0)]
        for c in range(4):
            out += [("gq", layer, c), ("gg", layer, c)]
            for q in {0: [], 1: [0], 2: [1], 3: [2, 3]}[c]:
                out += [("mg", layer, 2 * q), ("mg", layer, 2 * q + 1), ("w_ret_o", layer, q)]
        for q in range(4):
            out += [("mg", layer, 2 * KC + 2 * q), ("mg", layer, 2 * KC + 2 * q + 1), ("w_gqa_o", layer, q)]
        out += [("w_out", layer, n) for n in range(KC)]
    for layer in range(DEPTH):
        for f in (0, 1):
            ffn = [("ffn_g", layer, f, 0), ("ffn_u", layer, f, 0)]
            for i in range(FC - 1):
                ffn += [("ffn_g", layer, f, i + 1), ("ffn_u", layer, f, i + 1), ("ffn_o", layer, f, i)]
            out += ffn + [("ffn_o", layer, f, FC - 1)]
            if f == 0 and layer == 0:
                out += [("rec_r", 0, n) for n in range(KC)] + [("rec_y", 0, n) for n in range(KC)]
                out += [("rec_o", 0, n) for n in range(KC)]
            if f == 0 and layer == 1:
                out += [("sg_v", 0, n) for n in range(KC)] + [("sg_u", 0, n) for n in range(KC)]
                out += [("sg_o", 0, n) for n in range(KC)]
    return out


TILES = tile_order()
NT = len(TILES)


def column_tile(w, cols):
    return w[:, cols].reshape(KC, P, P).transpose(1, 0, 2).reshape(P, D)


def out_tile(w, q):
    return w[:, 2 * P * q:2 * P * (q + 1)].reshape(4, P, 2, P).transpose(1, 2, 0, 3).reshape(P, D)


def lay_out_weights(a):
    out = np.empty((NT, P, D), np.float32)
    gqa_rows = np.concatenate(GQA_COLS)
    for t, (kind, layer, *which) in enumerate(TILES):
        n = which[0]
        cols = slice(P * n, P * n + P)
        if kind == "ada":
            out[t] = column_tile(a["ada_w"][layer], cols)
        elif kind in ("gq", "gg"):
            out[t] = column_tile(a["w_in"][layer], IN_AT[kind] + GQA_COLS[n])
        elif kind in IN_AT:
            out[t] = column_tile(a["w_in"][layer], slice(IN_AT[kind] + P * n, IN_AT[kind] + P * n + P))
        elif kind == "w_gqa_o":
            out[t] = out_tile(a[kind][layer][gqa_rows], n)
        elif kind in ("w_na_o", "w_ret_o"):
            out[t] = out_tile(a[kind][layer], n)
        elif kind == "w_out":
            out[t] = column_tile(a[kind][layer], cols)
        elif kind in ("ffn_g", "ffn_u"):
            i = which[1] * P + (D_FF if kind == "ffn_u" else 0)
            out[t] = column_tile(a[f"ffn{n + 1}_w_in_2"][layer], slice(i, i + P))
        elif kind == "ffn_o":
            out[t] = a[f"ffn{n + 1}_w_out_2"][layer][P * which[1]:P * which[1] + P]
        elif kind == "rec_y":
            out[t] = column_tile(a["rec_w_in_2"][0], cols)
        elif kind == "rec_r":
            out[t] = column_tile(a["rec_w_in_2"][0], slice(D + P * n, D + P * n + P))
        elif kind == "rec_o":
            out[t] = column_tile(a["rec_w_out_2"][0], cols)
        elif kind == "sg_u":
            out[t] = column_tile(a["sg_w_in_2"][0], cols)
        elif kind == "sg_v":
            out[t] = column_tile(a["sg_w_in_2"][0], slice(D + P * n, D + P * n + P))
        elif kind == "sg_o":
            out[t] = column_tile(a["sg_w_out_2"][0], cols)
    return out


def by_partition(a):
    a = np.asarray(a)
    a = a.reshape(-1, a.shape[-1] // P, P)
    return a.transpose(2, 0, 1).reshape(P, -1)


PARAMS = [("c", 8), ("c_ctx", 8), ("ada_b", 48), ("norm_w", 16), ("ret_gn_w", 8), ("q_norm_w", 2), ("k_norm_w", 2),
          ("decay", 16), ("ffn1_norm", 16), ("mix_norm", 16), ("ffn2_norm", 16), ("final_norm_w", 8),
          ("final_norm", 8), ("rec_conv_w", 32), ("rec_conv_b", 8), ("rec_gate_a_b", 8), ("rec_gate_x_b", 8),
          ("rec_lambda", 8), ("sg_v_norm", 8)]
PARAM_AT = dict(zip([n for n, _ in PARAMS], np.cumsum([0] + [w for _, w in PARAMS]).tolist()))
NPARAM = sum(w for _, w in PARAMS)


def lay_out_params(a):
    rows = {
        "c": by_partition(a["c"]), "c_ctx": by_partition(a["c_ctx"]), "ada_b": by_partition(a["ada_b"]),
        "norm_w": by_partition(a["norm_w"]), "ret_gn_w": by_partition(a["ret_gn_w"]),
        "q_norm_w": np.tile(a["q_norm_w"], (1, 2)).T, "k_norm_w": np.tile(a["k_norm_w"], (1, 2)).T,
        "decay": np.broadcast_to(a["ret_log_decay"].reshape(1, -1), (P, 16)),
        "ffn1_norm": by_partition(a["ffn1_norm_2"]), "mix_norm": by_partition(a["mix_norm_2"]),
        "ffn2_norm": by_partition(a["ffn2_norm_2"]), "final_norm_w": by_partition(a["final_norm_w"]),
        "final_norm": by_partition(a["final_norm_2"]), "rec_conv_w": by_partition(a["rec_conv_w_2"][0]),
        "rec_conv_b": by_partition(a["rec_conv_b_2"]),
        "rec_gate_a_b": by_partition(a["rec_gate_a_b_2"].reshape(1, -1)),
        "rec_gate_x_b": by_partition(a["rec_gate_x_b_2"].reshape(1, -1)),
        "rec_lambda": by_partition(a["rec_lambda_2"]), "sg_v_norm": by_partition(a["sg_v_norm_2"]),
    }
    return np.ascontiguousarray(np.concatenate([rows[n] for n, _ in PARAMS], axis=1))


CONSTS = [("ident", P), ("mean_all", P), ("mean_head", P), ("swap", P), ("cos", SEQ), ("sin", SEQ),
          ("dif", 3 * P), ("window", GRID_W)]
CONST_AT = dict(zip([n for n, _ in CONSTS], np.cumsum([0] + [w for _, w in CONSTS]).tolist()))
NCONST = sum(w for _, w in CONSTS)


def shape_tables():
    p = np.arange(P)
    head = (p[:, None] // DH == p[None, :] // DH)
    partner = np.where(p % 32 < 16, p + 16, p - 16)
    t = np.arange(SEQ)
    freqs = (np.float32(10000.0) ** (-np.arange(16, dtype=np.float32) / 16)).astype(np.float32)
    pos = np.where(((p % DH) < 32)[:, None], (t // GRID_W)[None], (t % GRID_W)[None]).astype(np.float32)
    ang = (pos * freqs[p % 16][:, None]).astype(np.float32)
    sign = np.where(p % 32 < 16, -1.0, 1.0)[:, None]
    qc, kc = (p % GRID_W)[:, None], np.arange(GRID_W)[None]
    start = np.clip(qc - 8, 0, GRID_W - 16)
    rows = {
        "ident": np.eye(P), "mean_all": np.full((P, P), 1.0 / D), "mean_head": head / DH,
        "swap": (p[:, None] == partner[None, :]), "cos": np.cos(ang), "sin": np.sin(ang) * sign,
        "dif": np.arange(3 * P)[None] - P - p[:, None],
        "window": np.where((kc >= start) & (kc < start + 16), 0.0, -1e30),
    }
    return np.concatenate([rows[n].astype(np.float32) for n, _ in CONSTS], axis=1)


def lay_out_bias(rpb):
    pad = np.pad(rpb, ((0, 0), (0, 0), (0, 0), (GRID_W - 16, GRID_W - 16)))
    shifted = np.stack([pad[..., GRID_W - 1 - q:2 * GRID_W - 1 - q] for q in range(GRID_W)], axis=3)
    by_row = np.stack([shifted[:, :, 5 - r:11 - r] for r in range(2)], axis=2)
    by_row = by_row.reshape(DEPTH, NA_HEADS // 2, 2, 2, 6, GRID_W, GRID_W)
    return by_row.transpose(0, 1, 3, 5, 2, 4, 6).reshape(DEPTH, NA_HEADS // 2, P, 2, 6 * GRID_W)


class Step:

    def __init__(self, kind, n, add_n=None, at=None, b=None, base=None, before=None, bias=None, blocks=None,
                 bn_at=None, br=None, branch=None, c=None, cols=None, dc=None, evac=None, f=None,
                 first_half=None, g=None, gate=None, h=None, half_n=None, hp=None, j=None, job=None, k=None,
                 key_at=None, keys=None, layer=None, live=None, m=None, m_n=None, mixer=None, norm=None,
                 o_use=None, outs=None, part=None, s_use=None, slot=None, sq=None, src=None, t=None,
                 t_use=None, t_uses=None, tile=None, turn=None, u=None, up=None, what=None):
        self.kind, self.n = kind, n
        self.add_n, self.at, self.b, self.base = add_n, at, b, base
        self.before, self.bias, self.blocks, self.bn_at = before, bias, blocks, bn_at
        self.br, self.branch, self.c, self.cols = br, branch, c, cols
        self.dc, self.evac, self.f, self.first_half = dc, evac, f, first_half
        self.g, self.gate, self.h, self.half_n = g, gate, h, half_n
        self.hp, self.j, self.job, self.k = hp, j, job, k
        self.key_at, self.keys, self.layer, self.live = key_at, keys, layer, live
        self.m, self.m_n, self.mixer, self.norm = m, m_n, mixer, norm
        self.o_use, self.outs, self.part, self.s_use = o_use, outs, part, s_use
        self.slot, self.sq, self.src, self.t = slot, sq, src, t
        self.t_use, self.t_uses, self.tile, self.turn = t_use, t_uses, tile, turn
        self.u, self.up, self.what = u, up, what


class Schedule:

    def __init__(self):
        self.steps = []
        self.counts = {}
        self.uses = {}
        self.tile = 0
        self.half = 0
        self.background = []
        self.bn = 0

    def count(self, kind):
        n = self.counts.get(kind, 0)
        self.counts[kind] = n + 1
        return n

    def use(self, bank):
        n = self.uses.get(bank, 0)
        self.uses[bank] = n + 1
        return n

    def add(self, kind, **fields):
        step = Step(kind=kind, n=self.count(kind), **fields)
        self.steps.append(step)
        return step

    def split_ahead(self, t):
        if t + AHEAD < NT:
            self.add("split", t=t + AHEAD)

    def fill(self, slots=1):
        for _ in range(slots):
            if self.background:
                self.background.pop(0)()

    def drain(self):
        while self.background:
            self.fill()

    def product(self, what, src, n, blocks=KC, parts=(3, 3, 2), **fields):
        kind = TILES[self.tile][0]
        assert kind == what, (kind, what, self.tile)
        first_half = blocks < KC and self.half == 0
        job = Step(kind="job", n=self.use("G"), tile=self.tile, src=src, cols=n, blocks=blocks, what=what,
                   first_half=first_half, half_n=self.count("half") if first_half else None, **fields)
        base = 0 if blocks == KC else 4 * self.half
        if base == 0:
            self.split_ahead(self.tile)
        at = 0
        for part in (parts if blocks == KC else (2, 2)):
            self.add("product", job=job, at=at, part=part, base=base)
            at += part
            self.fill()
        if blocks == KC:
            self.tile += 1
        else:
            self.tile, self.half = self.tile + self.half, 1 - self.half
        return job


def schedule_layer(s, layer, h_norm):
    live = BOTH if layer == 0 else SEQ
    blocks = live // P
    groups = []
    first = {"h": h_norm}

    def src():
        return dict(src="h", norm=first.pop("h", None))

    def proj(what, n):
        return s.product(what, n=n, **src())

    def key(name, g):
        g.k_job = s_add_evac(proj(name, BOTH), "key", g)

    def value(name, g):
        job = proj(name, BOTH)
        g.v_evac = s.add("value_rows", job=job, g=g)
        g.v_turn = s.add("value_turn", evac=g.v_evac, g=g, m=s.use("M"))

    def query(name, g):
        g.q_job = s_add_evac(proj(name, live), "query", g)

    def s_add_evac(job, what, g):
        return s.add("evacuate", job=job, what=what, g=g)

    def gate(name, g):
        job = proj(name, live)
        g.gate = s.add("gate", job=job, g=g, cols=live)

    def new_group(branch, c):
        g = Step(kind="group", n=s.count("group"), branch=branch, c=c, layer=layer, live=live, blocks=blocks)
        g.slot = g.n % 2
        groups.append(g)
        return g

    def softmax_units(g):
        units = []
        for hp in range(2):
            for b in range(blocks):
                x = b < 2
                units.append(Step(kind="unit", n=s.count("unit"), g=g, hp=hp, b=b, keys=BOTH if x else SEQ,
                                  key_at=0 if x else SEQ, bias=x and g.branch == "na"))
        for u in units:
            u.bias_n = s.count("biased") if u.bias else None
            u.last = u is units[-1]
        g.units = units
        g.last_unit = units[-1]

        def slot(i):
            def run():
                if i < len(units):
                    u = units[i]
                    u.s_use = s.use("S")
                    s.add("scores", u=u)
                if 0 <= i - 1 < len(units):
                    u = units[i - 1]
                    u.t_use = s.use("T")
                    s.add("turn_probs", u=u)
                if 0 <= i - 2 < len(units):
                    u = units[i - 2]
                    u.o_use = s.use("O")
                    s.add("values", u=u)
            return run

        return [slot(i) for i in range(len(units) + 2)] + [lambda: turn_out(g)]

    def turn_out(g):
        g.out = s.add("turn_out", g=g, m=s.use("M"))

    def retention_units(g):
        def decay():
            g.decay = s.add("decay", g=g)

        def slot(j):
            def run():
                cols = live if j >= 2 else SEQ
                st = s.add("ret_scores", g=g, j=j, cols=cols, s_use=s.use("S"))
                g.last_scores = st
            return run

        def out():
            g.ret_out = s.add("ret_out", g=g, o_use=s.use("O"), bn_at=s.bn)
            s.bn += 2 * blocks + 1

        return [decay] + [slot(j) for j in range(4)] + [out, lambda: None, lambda: turn_out(g)]

    for c in range(4):
        g = new_group("na", c)
        g.bias = s.add("bias", g=g)
        key("nk", g)
        value("nv", g)
        query("nq", g)
        gate("ng", g)
        s.drain()
        s.background = softmax_units(g)

    ada = list(range(16, 24)) + [24 + n for n in range(24)] if layer == 0 else []

    def ada_jobs(k):
        for n in ada[:k]:
            job = s.product("ada", n=2, src="c", norm=None, parts=(8,))
            s.add("ada", job=job, at=n)
        del ada[:k]

    for h in range(4):
        g = new_group("ret", h)
        key("rk", g)
        ada_jobs(2)
        value("rv", g)
        ada_jobs(2)
        query("rq", g)
        ada_jobs(2)
        gate("rg", g)
        ada_jobs(2)
        s.drain()
        s.background = retention_units(g)

    merged = {"mg": [None, None]}

    def merge(branch, q, last_out):
        br = ("na", "ret", "gqa").index(branch)
        mg = []
        for dc in (2 * q, 2 * q + 1):
            job = proj("mg", live)
            mg.append(s.add("merge_gate", job=job, slot=dc % 2, before=merged["mg"][dc % 2], cols=live))
        if branch == "gqa":
            s.drain()
        for i, dc in enumerate((2 * q, 2 * q + 1)):
            job = s.product(f"w_{branch}_o", n=live, src=f"o_{branch}", blocks=4, norm=None, parts=None,
                            outs=last_out)
            st = s.add("merge", job=job, dc=dc, br=br, gate=mg[i], cols=live,
                       add_n=s.count("add") if br else None, m_n=s.count("m") if br == 2 else None)
            merged["mg"][dc % 2] = st

    na = [g for g in groups if g.branch == "na"]
    ret = [g for g in groups if g.branch == "ret"]
    for q in range(4):
        merge("na", q, na[-1])
    s.drain()
    kv = new_group("gqa_kv", 0)

    def norm_job(name, g, what, n):
        job = proj(name, n)
        st = s.add("head_norm", job=job, what=what, g=g, cols=n, m=s.use("M"))
        s.fill()
        rot = s.add("rotate", norm=st, g=g, what=what, m=s.use("M"))
        return rot

    kv.k_rot = norm_job("gk", kv, "key", BOTH)
    value("gv", kv)
    for c in range(4):
        g = new_group("gqa", c)
        g.kv = kv
        g.q_rot = norm_job("gq", g, "query", live)
        gate("gg", g)
        for q in {0: [], 1: [0], 2: [1], 3: [2]}[c]:
            merge("ret", q, ret[-1])
        s.drain()
        s.background = softmax_units(g)
        if c == 3:
            merge("ret", 3, ret[-1])
    gqa = [g for g in groups if g.branch == "gqa"]
    for q in range(4):
        merge("gqa", q, gqa[-1])
    s.drain()
    norm = new_norm(s, live if layer == 0 else SEQ)
    for dc in range(KC):
        job = s.product("w_out", n=live, src="m", norm=None)
        up = s.add("gated_residual", job=job, dc=dc, layer=layer, cols=live)
        s.add("square", norm=norm, k=dc, up=up, sq=s.count("sq"))
        if dc >= 1:
            s.add("square_sum", norm=norm, k=dc - 1)
    s.add("square_sum", norm=norm, k=KC - 1)
    if layer == 0:
        norm.cols = BOTH
    return norm


def new_norm(s, cols):
    norm = Step(kind="norm", n=s.count("norm"), cols=cols, m=s.use("M"))
    return norm


def finish_norm(s, norm, how, layer=None):
    norm.how, norm.layer = how, layer
    s.add("rms", norm=norm)
    split = how in ("ada", "h")
    norm.chunks = [s.add("normed", norm=norm, k=k, f=s.count("f") if split or how == "out" else None,
                         h=s.count("h") if split else None, t_use=s.use("T") if how == "out" else None)
                   for k in range(KC)]
    return norm


def squares(s, norm, ups):
    for k in range(KC):
        s.add("square", norm=norm, k=k, up=ups[k], sq=s.count("sq"))
        if k >= 1:
            s.add("square_sum", norm=norm, k=k - 1)
    s.add("square_sum", norm=norm, k=KC - 1)


def build_schedule():
    s = Schedule()
    for t in range(AHEAD):
        s.add("split", t=t)
    ups = [s.add("turn_in", k=k, t_use=s.use("T")) for k in range(KC)]
    norm = new_norm(s, BOTH)
    squares(s, norm, ups)
    for n in range(16):
        job = s.product("ada", n=2, src="c", norm=None, parts=(8,))
        s.add("ada", job=job, at=n)
    for layer in range(DEPTH):
        s.add("ada_scale", layer=layer)
        finish_norm(s, norm, "ada", layer)
        norm = schedule_layer(s, layer, norm)
    ups = finish_norm(s, norm, "residual", ("final_norm_w", 0)).chunks
    for layer in range(DEPTH):
        for f in (0, 1):
            norm = new_norm(s, SEQ)
            squares(s, norm, ups)
            finish_norm(s, norm, "h", (f"ffn{f + 1}_norm", layer))
            ffn = s.add("ffn", t=s.tile, norm=norm)
            s.tile += 3 * FC
            ups = [ffn] * KC
            if f == 0:
                norm = new_norm(s, SEQ)
                squares(s, norm, ups)
                finish_norm(s, norm, "h", ("mix_norm", layer))
                ups = (schedule_recurrent if layer == 0 else schedule_spatial)(s, norm)
    norm = new_norm(s, SEQ)
    squares(s, norm, ups)
    finish_norm(s, norm, "out", ("final_norm", 0))
    s.add("store")
    assert s.tile == NT
    return s


def schedule_recurrent(s, norm):
    for n in range(KC):
        job = s.product("rec_r", n=SEQ, src="h", norm=norm if n == 0 else None)
        s.add("conv", job=job, c=n)
        if n >= 1:
            s.add("rec_gates", c=n - 1, s_use=s.use("S"))
    s.add("rec_gates", c=KC - 1, s_use=s.use("S"))
    for n in range(KC):
        job = s.product("rec_y", n=SEQ, src="h", norm=None)
        s.add("rec_y", job=job, c=n)
        s.add("rec_decay", c=n)
    for n in range(KC):
        s.add("rec_root", c=n)
        s.add("rec_scan", c=n)
    for n in range(KC):
        s.add("rec_out", c=n)
    return mixer_out(s, "rec_o", 0)


def schedule_spatial(s, norm):
    def mix(c):
        turn = s.add("sg_turn", c=c, t_use=s.use("T"))
        s.add("sg_mix", c=c, turn=turn, s_use=s.use("S"))

    s.add("spatial_weights", t_uses=[s.use("T"), s.use("T")])
    vnorm = new_norm(s, SEQ)
    for n in range(KC):
        job = s.product("sg_v", n=SEQ, src="h", norm=norm if n == 0 else None)
        s.add("sg_v", job=job, c=n, norm=vnorm, sq=s.count("sq"))
        if n >= 1:
            s.add("square_sum", norm=vnorm, k=n - 1)
    s.add("square_sum", norm=vnorm, k=KC - 1)
    vnorm.how, vnorm.layer = "v", ("sg_v_norm", 0)
    s.add("rms", norm=vnorm)
    vnorm.chunks = []
    for n in range(KC):
        job = s.product("sg_u", n=SEQ, src="h", norm=None)
        s.add("sg_u", job=job, c=n)
        vnorm.chunks.append(s.add("normed", norm=vnorm, k=n, h=None))
        if n >= 1:
            mix(n - 1)
    mix(KC - 1)
    return mixer_out(s, "sg_o", 1)


def mixer_out(s, what, mixer):
    ups = []
    for n in range(KC):
        job = s.product(what, n=SEQ, src="mix", norm=None, mixer=mixer)
        ups.append(s.add("plain_residual", job=job, dc=n))
    return ups


def ffn_tile(which, i):
    if which == "o":
        return 3 * i + 4 if i < FC - 1 else 3 * FC - 1
    return (0 if i == 0 else 3 * i - 1) + (which == "u")


def block_kernel(nc, weights, params, consts, tokens, rpb, gate_a, gate_x, spatial, spatial_b, out):
    schedule = build_schedule()
    steps = schedule.steps
    ctx = ExitStack()
    with ctx:
        def sb(name, shape, dt=F32, stack=None):
            return (stack or ctx).enter_context(nc.sbuf_tensor(name, shape, dt))

        def sem(name):
            return ctx.enter_context(nc.semaphore(name))

        x = sb("x", [P, KC, BOTH])
        raw = sb("raw", [P, RAW, D])
        w_hi = sb("w_hi", [P, SPLIT, D], F32R)
        w_lo = sb("w_lo", [P, SPLIT, D], F32R)
        h_hi = sb("h_hi", [P, KC, BOTH], F32R)
        h_lo = sb("h_lo", [P, KC, BOTH], F32R)
        par = sb("par", [P, NPARAM])
        con = sb("con", [P, NCONST])
        c_silu = sb("c_silu", [P, KC, 2])
        c_hi = sb("c_hi", [P, KC, 2], F32R)
        c_lo = sb("c_lo", [P, KC, 2], F32R)
        ada = sb("ada", [P, DEPTH, 24, 2])
        ada_a = sb("ada_a", [P, KC, 2])
        eps = sb("eps", [P, 1])
        neg_half = sb("neg_half", [P, 1])
        log_g = sb("log_g", [P, 3, 16])
        gn_half = sb("gn_half", [P, 8])
        q_norm = sb("q_norm", [P, 2])
        lam = sb("lam", [P, 3, KC])
        square = sb("square", [P, 2, BOTH])
        rstd = sb("rstd", [P, BOTH])
        scaled = sb("scaled", [P, 2, BOTH])

        def P_(name, width=None):
            at = PARAM_AT[name]
            return par[:, at:at + (width or dict(PARAMS)[name])]

        def C_(name):
            at = CONST_AT[name]
            return con[:, at:at + dict(CONSTS)[name]]

        hybrid = ExitStack()

        def hb(name, shape, dt=F32, stack=None):
            return sb(name, shape, dt, stack or hybrid)

        o_hi = {"a": hb("oa_hi", [P, 4, BOTH], F32R)}
        o_lo = {"a": hb("oa_lo", [P, 4, BOTH], F32R)}
        m = hb("m", [P, KC, BOTH])
        tok = m[:, :, :].rearrange("p a b -> p (a b)").rearrange("p (t d) -> p t d", t=4)
        bias = hb("bias", [P, 2, 2, 6 * GRID_W])
        branch_gate = hb("branch_gate", [P, 2, BOTH])
        out_rows = hb("out_rows", [P, 4, P])
        gated = rstd
        attention = ExitStack()
        o_hi["b"] = hb("ob_hi", [P, 4, BOTH], F32R, attention)
        o_lo["b"] = hb("ob_lo", [P, 4, BOTH], F32R, attention)
        q_s = hb("q_s", [P, 2, BOTH], stack=attention)
        k_s = hb("k_s", [P, 2, BOTH], stack=attention)
        v_s = hb("v_s", [P, 2, 4, P], stack=attention)
        shared = hb("shared", [P, 4 * 3 * P], stack=attention)
        decay_s = shared[:, :].rearrange("p (k c) -> p k c", k=4)
        k_g, v_g = shared[:, 0:BOTH], shared[:, BOTH:2 * BOTH].rearrange("p (t d) -> p t d", t=4)
        stage = hb("stage", [P, BOTH], stack=attention)
        attention.close()
        m_hi = hb("m_hi", [P, KC, BOTH], F32R, attention)
        m_lo = hb("m_lo", [P, KC, BOTH], F32R, attention)
        attention.close()
        hb("reserved", [P, 8 * BOTH + 6 * BOTH + 12 * P + BOTH])
        half_tanh, head_sq = scaled[:, 0, :], scaled[:, 1, :]
        merge_tanh = hb("merge_tanh", [P, 2, BOTH])
        work = hb("work", [P, 4, BOTH])
        probs, probs_t = work[:, 0:2, :], work[:, 2:4, :]
        abs_dif = hb("abs_dif", [P, 3 * P])
        row_stat = hb("row_stat", [P, 3, 4])
        bn = hb("bn", [P, 4, 6])
        mean_var = hb("mean_var", [P, 4, 2])
        ret_rs = hb("ret_rs", [P, 4])
        hybrid.close()
        branch_sum = square

        silu_g = sb("silu_g", [P, 2, SEQ])
        hidden = sb("hidden", [P, 2, SEQ])
        hid_hi = sb("hid_hi", [P, 2, SEQ], F32R)
        hid_lo = sb("hid_lo", [P, 2, SEQ], F32R)
        mix_hi = sb("mix_hi", [P, KC, SEQ], F32R)
        mix_lo = sb("mix_lo", [P, KC, SEQ], F32R)
        mix_t = sb("mix_t", [P, 2, SEQ])
        rows_out = sb("rows_out", [P, 2, D])
        mixer = ExitStack()
        r_pad = sb("r_pad", [P, KC, SEQ + 3], stack=mixer)
        r_conv = sb("r_conv", [P, KC, SEQ], stack=mixer)
        g_a = sb("g_a", [P, KC, SEQ], stack=mixer)
        g_x = sb("g_x", [P, KC, SEQ], stack=mixer)
        y_act = sb("y_act", [P, KC, SEQ], stack=mixer)
        th = sb("th", [P, KC, SEQ], stack=mixer)
        gate_w = sb("gate_w", [P, 2, KC, P], stack=mixer)
        mixer.close()
        sg_v = sb("sg_v", [P, KC, SEQ], stack=mixer)
        sg_u = sb("sg_u", [P, KC, SEQ], stack=mixer)
        sg_vt = sb("sg_vt", [P, 2, SEQ], stack=mixer)
        ws = sb("ws", [P, KC, P], stack=mixer)
        ws_t = sb("ws_t", [P, KC, P], stack=mixer)
        ws_b = sb("ws_b", [P, KC, P], stack=mixer)
        mixer.close()

        bank = [ctx.enter_context(nc.psum_tensor(f"bank{i}", [P, 512], F32)) for i in range(8)]
        G, S, T, O, M = bank[0:2], bank[2:4], bank[4:6], bank[6], bank[7]

        raw_landed = [sem(f"raw_landed{i}") for i in range(RAW)]
        hi_ready = sem("hi_ready")
        lo_ready = sem("lo_ready")
        tile_used = sem("tile_used")
        half_used = sem("half_used")
        g_free = [sem("g_free0"), sem("g_free1")]
        s_full, s_free = sem("s_full"), [sem("s_free0"), sem("s_free1")]
        t_full, t_free = sem("t_full"), [sem("t_free0"), sem("t_free1")]
        o_full, o_free = sem("o_full"), sem("o_free")
        m_full, m_free = sem("m_full"), sem("m_free")
        par_landed, con_landed, tok_landed = sem("par_landed"), sem("con_landed"), sem("tok_landed")
        set_up_dve, set_up_act, set_up_pool = sem("set_up_dve"), sem("set_up_act"), sem("set_up_pool")
        squared, sq_used = sem("squared"), sem("sq_used")
        rstd_ready = sem("rstd_ready")
        f_ready, shifted, h_hi_ready, h_lo_ready = sem("f_ready"), sem("shifted"), sem("h_hi_ready"), sem("h_lo_ready")
        renormed, a_half, a_ready = sem("renormed"), sem("a_half"), sem("a_ready")
        bias_landed, bias_ready = [sem("bias_landed0"), sem("bias_landed1")], sem("bias_ready")
        biased, max_ready, sum_ready = sem("biased"), sem("max_ready"), sem("sum_ready")
        th_ready = sem("th_ready")
        decay_exp, decay_ready = sem("decay_exp"), sem("decay_ready")
        decay_cut = sem("decay_cut")
        bn_step, ret_pow = sem("bn_step"), sem("ret_pow")
        o_hi_ready, o_lo_ready = sem("o_hi_ready"), sem("o_lo_ready")
        head_rstd, qk_normed, cos_ready, rot_done = sem("head_rstd"), sem("qk_normed"), sem("cos_ready"), sem("rot_done")
        added = sem("added")
        m_hi_ready, m_lo_ready = sem("m_hi_ready"), sem("m_lo_ready")
        residual_half = sem("residual_half")
        silu_ready, hid_ready, hid_hi_ready, hid_lo_ready = (
            sem("silu_ready"), sem("hid_ready"), sem("hid_hi_ready"), sem("hid_lo_ready"))
        ffn_out = sem("ffn_out")
        ffn_added = sem("ffn_added")
        mix_zero, mix_landed = sem("mix_zero"), sem("mix_landed")
        conv_step, gates_ready, gated_ready = sem("conv_step"), sem("gates_ready"), sem("gated_ready")
        decays, root_in, root_step, root_out = sem("decays"), sem("root_in"), sem("root_step"), sem("root_out")
        bx_ready, scanned = sem("bx_ready"), sem("scanned")
        y_ready, mix_ready, mix_hi_ready, mix_lo_ready = sem("y_ready"), sem("mix_ready"), sem("mix_hi_ready"), sem("mix_lo_ready")
        v_ready, v_normed, ws_cut = sem("v_ready"), sem("v_normed"), sem("ws_cut")
        mix_step = sem("mix_step")
        rows_stored = sem("rows_stored")

        def evacuated(job):
            return g_free[job.n % 2], job.n // 2 + 1

        def complete(job):
            return (half_used, job.half_n + 1) if job.first_half else (tile_used, job.tile + 1)

        def s_out(use):
            return s_free[use % 2], use // 2 + 1

        def t_out(use):
            return t_free[use % 2], use // 2 + 1

        def residual_ready(up, k):
            if up.kind == "turn_in":
                return t_out(up.t_use)
            if up.kind in ("gated_residual", "plain_residual"):
                return evacuated(up.job)
            if up.kind == "normed":
                return renormed, k + 1
            return ffn_added, 4 * up.n + k // 2 + 1

        def g_buf(g, which):
            if which == "q":
                return q_s[:, g.slot, :]
            if g.branch in ("gqa", "gqa_kv"):
                return k_g[:, :] if which == "k" else v_g[:, :, :]
            return k_s[:, g.slot, :] if which == "k" else v_s[:, g.slot, :, :]

        def o_of(branch):
            return "b" if branch == "ret" else "a"

        def norm_weight(norm, k):
            name, row = norm.layer
            at = PARAM_AT[name] + KC * row + k
            return par[:, at:at + 1]

        def key_blocks(u):
            return range(u.key_at // P, u.key_at // P + u.keys // P)

        Q_SCALE = {"na": DH ** -0.5, "ret": 1.0}
        K_SCALE = {"na": 1.0, "ret": float(np.float32(P) ** np.float32(-0.5))}
        DECAY = 3 * P

        ffn_bank = [M, T[0], T[1], O]
        y_jobs = [st.job for st in steps if st.kind == "rec_y"]
        u_jobs = [st.job for st in steps if st.kind == "sg_u"]

        block = ctx.enter_context(nc.Block())

        @block.sync
        def _(sp):
            sp.dma_start(con[:, :], consts).then_inc(con_landed, 16)
            sp.dma_start(tok[:, 0:2, :], tokens.rearrange("(t p) d -> p t d", p=P)[:, 0:2, :]).then_inc(tok_landed, 16)
            sp.dma_start(tok[:, 2:4, :], tokens.rearrange("(t p) d -> p t d", p=P)[:, 2:4, :]).then_inc(tok_landed, 16)
            for t in range(RAW):
                sp.dma_start(raw[:, t, :], weights[t, :, :]).then_inc(raw_landed[t], 16)
            full = NT // RAW
            with sp.Fori(0, full - 1) as r:
                for i in range(RAW):
                    sp.wait_ge(lo_ready, r * RAW + (i + 1))
                    sp.dma_start(raw[:, i, :], weights[r * RAW + (RAW + i), :, :]).then_inc(raw_landed[i], 16)
            for t in range(full * RAW, NT):
                sp.wait_ge(lo_ready, t - RAW + 1)
                sp.dma_start(raw[:, t % RAW, :], weights[t, :, :]).then_inc(raw_landed[t % RAW], 16)
            t_uses = schedule.uses["T"]
            sp.wait_ge(t_free[0], (t_uses + 1) // 2)
            sp.wait_ge(t_free[1], t_uses // 2)
            sp.dma_start(out.rearrange("(t p) d -> p t d", p=P), rows_out[:, :, :]).then_inc(rows_stored, 16)
            sp.wait_ge(rows_stored, 16)

        @block.gpsimd
        def _(pool):
            pool.memset(eps[:, :], EPS).then_inc(set_up_pool, 1)
            pool.memset(neg_half[:, :], -0.5).then_inc(set_up_pool, 1)
            reader = [None, None]

            def bias_step(st):
                g = st.g
                slot = g.c % 2
                if reader[slot] is not None:
                    pool.wait_ge(biased, reader[slot] + 1)
                pool.dma_start(bias[:, slot, :, :], rpb[g.layer, g.c]).then_inc(bias_landed[slot], 16)
                pool.wait_ge(con_landed, 16)
                pool.wait_ge(bias_landed[slot], 16 * (st.n // 2 + 1))
                b = bias[:, slot, :, :].rearrange("p h (r c) -> p (h r) c", r=6)
                window = C_("window").unsqueeze(1).to_broadcast([P, 12, GRID_W])
                pool.tensor_tensor(b, b, window, ALU.add).then_inc(bias_ready, 1)

            def decay_step(st):
                n = st.n
                pool.wait_ge(decay_exp, 4 * n + 4)
                fwd, bwd, cross, cross_b = (decay_s[:, i, :] for i in range(4))
                pool.affine_select(out=fwd, in_=fwd, compare_op=ALU.is_ge, fill=0.0, base=-P,
                                   pattern=[[1, DECAY]], channel_multiplier=-1).then_inc(decay_cut, 1)
                pool.affine_select(out=bwd, in_=bwd, compare_op=ALU.is_ge, fill=0.0, base=P,
                                   pattern=[[-1, DECAY]], channel_multiplier=1).then_inc(decay_cut, 1)
                pool.tensor_tensor(cross, cross, cross_b, ALU.add).then_inc(decay_ready, 1)
                pool.wait_ge(decay_cut, 2 * n + 2)
                pool.tensor_tensor(fwd, fwd, bwd, ALU.add).then_inc(decay_ready, 1)

            def ret_out_step(st):
                nb = st.g.blocks
                pool.wait_ge(bn_step, st.bn_at + 2 * nb + 1)
                half = neg_half[:, 0:1].to_broadcast([P, nb])
                pool.tensor_tensor(ret_rs[:, 0:nb], ret_rs[:, 0:nb], half, ALU.pow).then_inc(ret_pow, 1)

            def rotate_step(st):
                pool.wait_ge(qk_normed, st.n + 1)
                dst = g_buf(st.g, "k" if st.what == "key" else "q")
                pool.tensor_tensor(stage[:, 0:SEQ], dst[:, 0:SEQ], C_("cos"), ALU.mult).then_inc(cos_ready, 1)

            def merge_step(st):
                if st.br == 0:
                    return
                pool.wait_ge(*evacuated(st.job))
                v = m[:, st.dc, 0:st.cols]
                pool.tensor_tensor(v, v, branch_sum[:, st.dc % 2, 0:st.cols], ALU.add).then_inc(added, 1)

            def spatial_weights_step(st):
                pool.wait_ge(mix_landed, 6 * 16)
                pool.affine_select(out=ws[:, :, :], in_=ws[:, :, :], compare_op=ALU.is_ge, fill=0.0, base=0,
                                   pattern=[[0, KC], [-1, P]], channel_multiplier=1).then_inc(ws_cut, 1)

            def ffn_step(st):
                if st.n % 2:
                    return
                pool.wait_ge(h_lo_ready, st.norm.chunks[KC - 1].h + 1)
                if st.n == 0:
                    pool.memset(gate_w[:, :, :, :], 0.0).then_inc(mix_zero, 1)
                    pool.wait_ge(mix_zero, 1)
                    for i, w in enumerate((gate_a, gate_x)):
                        halves = w.rearrange("(n two) i j -> two i n j", two=2)
                        for j in range(2):
                            at = slice(DH * j, DH * j + DH)
                            pool.dma_start(gate_w[at, i, :, at], halves[j]).then_inc(mix_landed, 16)
                else:
                    pool.dma_start(ws[:, :, :], spatial.rearrange("h p q -> p h q")).then_inc(mix_landed, 16)
                    rows = spatial_b.rearrange("h p -> (h p)").partition_broadcast(P)
                    pool.dma_start(ws_b[:, :, :].rearrange("p h q -> p (h q)"), rows).then_inc(mix_landed, 16)

            def rec_gates_step(st):
                pool.wait_ge(*s_out(st.s_use))
                v = g_x[:, st.c, :]
                pool.tensor_tensor(v, v, r_conv[:, st.c, :], ALU.mult).then_inc(gated_ready, 1)

            def rec_root_step(st):
                pool.wait_ge(root_out, st.n + 1)
                pool.wait_ge(gated_ready, st.n + 1)
                v = g_x[:, st.c, :]
                pool.tensor_tensor(v, v, th[:, st.c, :], ALU.mult).then_inc(bx_ready, 1)

            run = {"bias": bias_step, "decay": decay_step, "ret_out": ret_out_step, 
                   "rotate": rotate_step, "merge": merge_step, "spatial_weights": spatial_weights_step,
                   "ffn": ffn_step, "rec_gates": rec_gates_step, "rec_root": rec_root_step}
            for st in steps:
                if st.kind == "scores" and st.u.bias:
                    reader[st.u.g.c % 2] = st.u.bias_n
                if st.kind in run:
                    run[st.kind](st)

        @block.scalar
        def _(act):
            act.dma_start(par[:, :], params).then_inc(par_landed, 16)
            act.wait_ge(par_landed, 16)
            nc.scalar.activation(c_silu[:, :, 0], P_("c"), ACT.Silu).then_inc(set_up_act, 1)
            nc.scalar.activation(c_silu[:, :, 1], P_("c_ctx"), ACT.Silu).then_inc(set_up_act, 1)
            act.wait_ge(set_up_act, 2)
            nc.scalar.activation(c_hi[:, :, :], c_silu[:, :, :], ACT.Copy).then_inc(set_up_act, 1)
            nc.scalar.activation(log_g[:, 0, :], P_("decay"), ACT.Exp).then_inc(set_up_act, 1)
            nc.scalar.activation(lam[:, 0, :], P_("rec_lambda"), ACT.Abs).then_inc(set_up_act, 1)
            act.wait_ge(set_up_act, 5)
            nc.scalar.activation(lam[:, 1, :], lam[:, 0, :], ACT.Exp, scale=-1.0).then_inc(set_up_act, 1)
            act.wait_ge(set_up_act, 6)
            act.wait_ge(set_up_dve, 1)
            nc.scalar.activation(lam[:, 0, :], lam[:, 1, :], ACT.Ln, bias=lam[:, 2, 0:1]).then_inc(set_up_act, 1)
            act.wait_ge(con_landed, 16)
            nc.scalar.activation(abs_dif[:, :], C_("dif"), ACT.Abs).then_inc(set_up_act, 1)
            act.wait_ge(set_up_pool, 1)
            last = {"gate": None, "decay": None}

            def split_step(st):
                split(st.t, None)

            def split(t, r, t_static=None):
                base = 0 if r is None else r * RAW
                act.wait_ge(raw_landed[t % RAW], 16 * (t // RAW + 1) if r is None else r * 16 + 16 * (t // RAW + 1))
                if t >= SPLIT:
                    act.wait_ge(tile_used, base + (t - SPLIT + 1))
                nc.scalar.activation(w_hi[:, t % SPLIT, :], raw[:, t % RAW, :], ACT.Copy).then_inc(hi_ready, 1)

            def turn_in_step(st):
                if st.k % 2:
                    return
                act.wait_ge(t_full, st.t_use + 1)
                nc.scalar.activation(x[:, st.k, :], T[st.t_use % 2][:, :], ACT.Copy).then_inc(t_free[st.t_use % 2], 1)

            def square_step(st):
                act.wait_ge(*residual_ready(st.up, st.k))
                if st.k >= 2:
                    act.wait_ge(sq_used, (KC - 1) * st.norm.n + st.k - 1)
                c = st.norm.cols
                nc.scalar.activation(square[:, st.k % 2, 0:c], x[:, st.k, 0:c], ACT.Square).then_inc(squared, 1)

            def rms_step(st):
                c = st.norm.cols
                act.wait_ge(m_full, st.norm.m + 1)
                nc.scalar.activation(rstd[:, 0:c], M[:, 0:c], ACT.Sqrt, bias=eps[:, 0:1]).then_inc(m_free, 1)

            def normed_step(st):
                norm, k = st.norm, st.k
                if norm.how == "ada":
                    act.wait_ge(f_ready, st.f + 1)
                    for j in range(2):
                        v = scaled[:, k % 2, SEQ * j:SEQ * j + SEQ]
                        nc.scalar.activation(v, v, ACT.Identity, bias=ada[:, norm.layer, k, j:j + 1])\
                            .then_inc(shifted, 1)
                    act.wait_ge(shifted, 2 * (KC * norm.layer + k + 1))
                elif norm.how == "h":
                    act.wait_ge(f_ready, st.f + 1)
                else:
                    return
                nc.scalar.activation(h_hi[:, k, 0:norm.cols], scaled[:, k % 2, 0:norm.cols], ACT.Copy)\
                    .then_inc(h_hi_ready, 1)

            def evacuate_step(st):
                g, n = st.g, st.job.cols
                act.wait_ge(*complete(st.job))
                dst = g_buf(g, "q" if st.what == "query" else "k")
                scale = (Q_SCALE if st.what == "query" else K_SCALE)[g.branch]
                nc.scalar.activation(dst[:, 0:n], G[st.job.n % 2][:, 0:n], ACT.Copy, scale=scale)\
                    .then_inc(g_free[st.job.n % 2], 1)

            def value_rows_step(st):
                act.wait_ge(*complete(st.job))
                if last_rotate[0]:
                    act.wait_ge(rot_done, last_rotate[0])
                nc.scalar.activation(stage[:, :], G[st.job.n % 2][:, :], ACT.Copy).then_inc(g_free[st.job.n % 2], 1)

            last_rotate = [0]

            def gate_step(st):
                act.wait_ge(*complete(st.job))
                if last["gate"] is not None:
                    act.wait_ge(*evacuated(last["gate"].job))
                last["gate"] = st
                nc.scalar.activation(half_tanh[:, 0:st.cols], G[st.job.n % 2][:, 0:st.cols], ACT.Tanh, scale=0.5)\
                    .then_inc(th_ready, 1)

            def merge_gate_step(st):
                act.wait_ge(*complete(st.job))
                if st.before is not None:
                    act.wait_ge(*evacuated(st.before.job))
                nc.scalar.activation(merge_tanh[:, st.slot, 0:st.cols], G[st.job.n % 2][:, 0:st.cols], ACT.Tanh,
                                     scale=0.5).then_inc(g_free[st.job.n % 2], 1)

            def merge_step(st):
                if st.br < 2:
                    return
                act.wait_ge(added, st.add_n + 1)
                nc.scalar.activation(m_hi[:, st.dc, 0:st.cols], m[:, st.dc, 0:st.cols], ACT.Copy, scale=0.5)\
                    .then_inc(m_hi_ready, 1)

            def scores_step(st):
                u = st.u
                act.wait_ge(max_ready, u.n + 1)
                nc.scalar.activation(probs[:, u.n % 2, 0:u.keys], S[u.s_use % 2][:, 0:u.keys], ACT.Exp,
                                     bias=row_stat[:, 0, u.n % 4:u.n % 4 + 1],
                                     accum_out=row_stat[:, 1, u.n % 4:u.n % 4 + 1]).then_inc(s_free[u.s_use % 2], 1)

            def turn_probs_step(st):
                u = st.u
                act.wait_ge(t_full, u.t_use + 1)
                nc.scalar.activation(probs_t[:, u.n % 2, 0:u.keys], T[u.t_use % 2][:, 0:u.keys], ACT.Copy)\
                    .then_inc(t_free[u.t_use % 2], 1)

            def turn_out_step(st):
                g = st.g
                act.wait_ge(m_free, st.m + 1)
                nc.scalar.activation(o_hi[o_of(g.branch)][:, g.c, 0:g.live], gated[:, 0:g.live], ACT.Copy)\
                    .then_inc(o_hi_ready, 1)

            def decay_step(st):
                g = st.g
                if last["decay"] is not None:
                    act.wait_ge(*s_out(last["decay"].last_scores.s_use))
                last["decay"] = g
                f, b = g.layer * 8 + g.c, g.layer * 8 + 4 + g.c
                act.wait_ge(set_up_dve, 5)
                act.wait_ge(set_up_act, 8)
                lg = lambda kind, i: log_g[:, kind, i:i + 1]
                nc.scalar.activation(decay_s[:, 0, :], abs_dif[:, :], ACT.Exp, scale=lg(0, f)).then_inc(decay_exp, 1)
                nc.scalar.activation(decay_s[:, 1, :], abs_dif[:, :], ACT.Exp, scale=lg(0, b)).then_inc(decay_exp, 1)
                nc.scalar.activation(decay_s[:, 2, :], C_("dif"), ACT.Exp, scale=lg(0, f), bias=lg(2, f))\
                    .then_inc(decay_exp, 1)
                nc.scalar.activation(decay_s[:, 3, :], C_("dif"), ACT.Exp, scale=lg(1, b), bias=lg(2, b))\
                    .then_inc(decay_exp, 1)

            def head_norm_step(st):
                n = st.cols
                act.wait_ge(*complete(st.job))
                if last_rotate[0]:
                    act.wait_ge(rot_done, last_rotate[0])
                nc.scalar.activation(stage[:, 0:n], G[st.job.n % 2][:, 0:n], ACT.Copy).then_inc(th_ready, 1)
                nc.scalar.activation(head_sq[:, 0:n], G[st.job.n % 2][:, 0:n], ACT.Square)\
                    .then_inc(g_free[st.job.n % 2], 1)
                act.wait_ge(m_full, st.m + 1)
                nc.scalar.activation(head_sq[:, 0:n], M[:, 0:n], ACT.Sqrt, bias=eps[:, 0:1]).then_inc(m_free, 1)

            def rotate_step(st):
                last_rotate[0] = st.n + 1

            def ffn_step(st):
                f, t0 = st.n, st.t

                def silu(i, r=None):
                    up = 0 if r is None else r * 6
                    cnt = 0 if r is None else r * 2
                    act.wait_ge(tile_used, up + (t0 + ffn_tile("g", i) + 1))
                    if i >= 2:
                        act.wait_ge(hid_ready, cnt + (FC * f + i - 1))
                    nc.scalar.activation(silu_g[:, i % 2, :], G[i % 2][:, 0:SEQ], ACT.Silu).then_inc(silu_ready, 1)

                def hid(i, r=None):
                    cnt = 0 if r is None else r * 2
                    act.wait_ge(hid_ready, cnt + (FC * f + i + 1))
                    nc.scalar.activation(hid_hi[:, i % 2, :], hidden[:, i % 2, :], ACT.Copy).then_inc(hid_hi_ready, 1)

                def round_(i, r=None):
                    a = t0 + 2 + 3 * i
                    split(a + 2, r)
                    hid(i, r)
                    split(a + 3, r)
                    silu(i + 1, r)
                    if r is not None or a + 4 < NT:
                        split(a + 4, r)

                split(t0 + 2, None)
                split(t0 + 3, None)
                silu(0)
                round_(0)
                peeled = 2 if t0 + 3 * FC == NT else 0
                with act.Fori(0, (FC - 2 - peeled) // 2) as r:
                    round_(1, r)
                    round_(2, r)
                for i in range(FC - 1 - peeled, FC - 1):
                    round_(i)
                if t0 + 3 * FC - 1 + AHEAD < NT:
                    split(t0 + 3 * FC - 1 + AHEAD, None)
                hid(FC - 1)

            def rec_gates_step(st):
                act.wait_ge(s_full, st.s_use + 1)
                b = S[st.s_use % 2]
                at_a, at_x = PARAM_AT["rec_gate_a_b"] + st.c, PARAM_AT["rec_gate_x_b"] + st.c
                nc.scalar.activation(g_a[:, st.c, :], b[:, 0:SEQ], ACT.Sigmoid, bias=par[:, at_a:at_a + 1])\
                    .then_inc(gates_ready, 1)
                nc.scalar.activation(g_x[:, st.c, :], b[:, SEQ:BOTH], ACT.Sigmoid, bias=par[:, at_x:at_x + 1])\
                    .then_inc(s_free[st.s_use % 2], 1)

            def conv_step_act(st):
                act.wait_ge(*complete(st.job))
                nc.scalar.activation(r_pad[:, st.c, 3:], G[st.job.n % 2][:, 0:SEQ], ACT.Copy)\
                    .then_inc(g_free[st.job.n % 2], 1)

            def rec_y_step(st):
                act.wait_ge(*complete(st.job))
                nc.scalar.activation(y_act[:, st.c, :], G[st.job.n % 2][:, 0:SEQ], ACT.Copy)\
                    .then_inc(g_free[st.job.n % 2], 1)

            def rec_decay_step(st):
                act.wait_ge(gates_ready, st.c + 1)
                act.wait_ge(set_up_dve, 10)
                scale = lam[:, 0, st.c:st.c + 1]
                nc.scalar.activation(th[:, st.c, :], g_a[:, st.c, :], ACT.Tanh, scale=scale).then_inc(decays, 1)
                act.wait_ge(decays, 2 * st.c + 1)
                nc.scalar.activation(g_a[:, st.c, :], g_a[:, st.c, :], ACT.Exp, scale=scale).then_inc(decays, 1)

            def rec_root_step(st):
                act.wait_ge(root_in, st.n + 1)
                nc.scalar.activation(th[:, st.c, :], th[:, st.c, :], ACT.Sqrt).then_inc(root_out, 1)

            def rec_out_step(st):
                act.wait_ge(*evacuated(y_jobs[st.c]))
                nc.scalar.activation(y_act[:, st.c, :], y_act[:, st.c, :], ACT.Gelu_apprx_tanh).then_inc(y_ready, 1)
                mix_split(st.c, st.n)

            def mix_split(c, n):
                act.wait_ge(mix_ready, n + 1)
                nc.scalar.activation(mix_hi[:, c, :], mix_t[:, n % 2, :], ACT.Copy).then_inc(mix_hi_ready, 1)

            def sg_v_step(st):
                act.wait_ge(*complete(st.job))
                nc.scalar.activation(sg_v[:, st.c, :], G[st.job.n % 2][:, 0:SEQ], ACT.Gelu_apprx_tanh)\
                    .then_inc(g_free[st.job.n % 2], 1)
                act.wait_ge(*evacuated(st.job))
                if st.c >= 2:
                    act.wait_ge(sq_used, (KC - 1) * st.norm.n + st.c - 1)
                nc.scalar.activation(square[:, st.c % 2, 0:SEQ], sg_v[:, st.c, :], ACT.Square).then_inc(squared, 1)

            def sg_u_step(st):
                act.wait_ge(*complete(st.job))
                nc.scalar.activation(sg_u[:, st.c, :], G[st.job.n % 2][:, 0:SEQ], ACT.Gelu_apprx_tanh)\
                    .then_inc(g_free[st.job.n % 2], 1)

            def sg_turn_step(st):
                act.wait_ge(t_full, st.t_use + 1)
                nc.scalar.activation(sg_vt[:, st.c % 2, :], T[st.t_use % 2][:, 0:SEQ], ACT.Copy)\
                    .then_inc(t_free[st.t_use % 2], 1)

            def sg_mix_step(st):
                mix_split(st.c, KC + st.n)

            run = {"split": split_step, "turn_in": turn_in_step, "square": square_step, "rms": rms_step,
                   "normed": normed_step, "evacuate": evacuate_step, "value_rows": value_rows_step,
                   "gate": gate_step, "merge_gate": merge_gate_step, "merge": merge_step, "scores": scores_step,
                   "turn_probs": turn_probs_step, "turn_out": turn_out_step, "decay": decay_step,
                   "head_norm": head_norm_step, "rotate": rotate_step, "ffn": ffn_step, "rec_gates": rec_gates_step,
                   "conv": conv_step_act, "rec_y": rec_y_step, "rec_decay": rec_decay_step, "rec_root": rec_root_step,
                   "rec_out": rec_out_step, "sg_v": sg_v_step, "sg_u": sg_u_step, "sg_turn": sg_turn_step,
                   "sg_mix": sg_mix_step}
            for st in steps:
                if st.kind in run:
                    run[st.kind](st)

        @block.vector
        def _(dve):
            dve.memset(lam[:, 2, 0:1], 1.0).then_inc(set_up_dve, 1)
            dve.wait_ge(set_up_act, 4)
            dve.tensor_tensor(c_lo[:, :, :], c_silu[:, :, :], c_hi[:, :, :].bitcast(F32), ALU.subtract)\
                .then_inc(set_up_dve, 1)
            dve.tensor_scalar(log_g[:, 1, :], log_g[:, 0, :], 1.0, None, ALU.mult).then_inc(set_up_dve, 1)
            dve.tensor_scalar(log_g[:, 2, :], log_g[:, 0, :], -256.0, None, ALU.mult).then_inc(set_up_dve, 1)
            dve.wait_ge(set_up_dve, 4)
            dve.tensor_scalar(log_g[:, 0, :], log_g[:, 0, :], -1.0, None, ALU.mult).then_inc(set_up_dve, 1)
            dve.tensor_scalar(gn_half[:, :], P_("ret_gn_w"), 0.5, None, ALU.mult).then_inc(set_up_dve, 1)
            dve.tensor_scalar(q_norm[:, :], P_("q_norm_w"), DH ** -0.5, None, ALU.mult).then_inc(set_up_dve, 1)
            dve.wait_ge(set_up_act, 7)
            dve.tensor_scalar(lam[:, 1, :], P_("rec_lambda"), -1.0, 0.0, ALU.mult, ALU.max).then_inc(set_up_dve, 1)
            dve.wait_ge(set_up_dve, 8)
            dve.tensor_tensor(lam[:, 1, :], lam[:, 1, :], lam[:, 0, :], ALU.add).then_inc(set_up_dve, 1)
            dve.wait_ge(set_up_dve, 9)
            dve.tensor_scalar(lam[:, 0, :], lam[:, 1, :], -8.0, None, ALU.mult).then_inc(set_up_dve, 1)

            def split(t, r=None):
                base = 0 if r is None else r * RAW
                dve.wait_ge(hi_ready, base + (t + 1))
                dve.tensor_tensor(w_lo[:, t % SPLIT, :], raw[:, t % RAW, :], w_hi[:, t % SPLIT, :].bitcast(F32),
                                  ALU.subtract).then_inc(lo_ready, 1)

            def turn_in_step(st):
                if st.k % 2 == 0:
                    return
                dve.wait_ge(t_full, st.t_use + 1)
                dve.tensor_copy(x[:, st.k, :], T[st.t_use % 2][:, :]).then_inc(t_free[st.t_use % 2], 1)

            def ada_step(st):
                layer, idx = divmod(st.at, 24)
                at = PARAM_AT["ada_b"] + st.at
                dve.wait_ge(*complete(st.job))
                dve.wait_ge(par_landed, 16)
                dve.tensor_scalar(ada[:, layer, idx, :], G[st.job.n % 2][:, 0:2], par[:, at:at + 1], None, ALU.add)\
                    .then_inc(g_free[st.job.n % 2], 1)
                last_ada[layer] = st.job

            last_ada = [None, None]

            def ada_scale_step(st):
                at = PARAM_AT["norm_w"] + KC * st.layer
                dve.wait_ge(*evacuated(last_ada[st.layer]))
                for j in range(2):
                    dve.scalar_tensor_tensor(out=ada_a[:, :, j], in0=ada[:, st.layer, KC:2 * KC, j], scalar=1.0,
                                             in1=par[:, at:at + KC], op0=ALU.add, op1=ALU.mult).then_inc(a_ready, 1)

            def rms_step(st):
                c = st.norm.cols
                dve.wait_ge(m_free, st.norm.m + 1)
                dve.reciprocal(rstd[:, 0:c], rstd[:, 0:c]).then_inc(rstd_ready, 1)

            def normed_step(st):
                norm, k, c = st.norm, st.k, st.norm.cols
                if k == 0:
                    dve.wait_ge(rstd_ready, norm.n + 1)
                if st.h is not None and k >= 2:
                    dve.wait_ge(h_lo_ready, st.h - 1)
                if norm.how == "ada":
                    if k == 0:
                        dve.wait_ge(a_ready, 2 * norm.layer + 2)
                    for j in range(2):
                        at = slice(SEQ * j, SEQ * j + SEQ)
                        ins = dve.scalar_tensor_tensor(out=scaled[:, k % 2, at], in0=x[:, k, at],
                                                       scalar=ada_a[:, k, j:j + 1], in1=rstd[:, at],
                                                       op0=ALU.mult, op1=ALU.mult)
                    ins.then_inc(f_ready, 1)
                elif norm.how in ("h", "out"):
                    if norm.how == "out" and k >= 2:
                        dve.wait_ge(t_full, st.t_use - 1)
                    dve.scalar_tensor_tensor(out=scaled[:, k % 2, 0:c], in0=x[:, k, 0:c], scalar=norm_weight(norm, k),
                                             in1=rstd[:, 0:c], op0=ALU.mult, op1=ALU.mult).then_inc(f_ready, 1)
                    if norm.how == "out":
                        dve.wait_ge(t_full, st.t_use + 1)
                        dve.tensor_copy(rows_out[:, :, P * k:P * k + P],
                                        T[st.t_use % 2][:, 0:SEQ].rearrange("p (t d) -> p t d", t=2))\
                            .then_inc(t_free[st.t_use % 2], 1)
                        return
                elif norm.how == "residual":
                    dve.scalar_tensor_tensor(out=x[:, k, 0:SEQ], in0=x[:, k, 0:SEQ], scalar=norm_weight(norm, k),
                                             in1=rstd[:, 0:SEQ], op0=ALU.mult, op1=ALU.mult).then_inc(renormed, 1)
                    return
                else:
                    dve.scalar_tensor_tensor(out=sg_v[:, k, :], in0=sg_v[:, k, :], scalar=norm_weight(norm, k),
                                             in1=rstd[:, 0:SEQ], op0=ALU.mult, op1=ALU.mult).then_inc(v_normed, 1)
                    return

                if k >= 1:
                    h_low(norm.chunks[k - 1], c)
                if k == KC - 1:
                    h_low(st, c)

            def h_low(st, c):
                dve.wait_ge(h_hi_ready, st.h + 1)
                dve.tensor_tensor(h_lo[:, st.k, 0:c], scaled[:, st.k % 2, 0:c], h_hi[:, st.k, 0:c].bitcast(F32),
                                  ALU.subtract).then_inc(h_lo_ready, 1)

            def value_turn_step(st):
                dve.wait_ge(m_full, st.m + 1)
                dve.tensor_copy(g_buf(st.g, "v"), M[:, :].rearrange("p (t d) -> p t d", t=4)).then_inc(m_free, 1)

            def gate_step(st):
                th_count[0] += 1
                dve.wait_ge(th_ready, th_count[0])
                if turned[st.g.slot]:
                    dve.wait_ge(m_free, turned[st.g.slot])
                dve.scalar_tensor_tensor(out=branch_gate[:, st.g.slot, 0:st.cols], in0=half_tanh[:, 0:st.cols],
                                         scalar=1.0, in1=G[st.job.n % 2][:, 0:st.cols], op0=ALU.add, op1=ALU.mult)\
                    .then_inc(g_free[st.job.n % 2], 1)

            th_count = [0]
            turned = [0, 0]

            def merge_step(st):
                c = st.cols
                dve.wait_ge(*complete(st.job))
                dve.wait_ge(*evacuated(st.gate.job))
                if st.br and st.add_n >= 2:
                    dve.wait_ge(added, st.add_n - 1)
                dst = m[:, st.dc, 0:c] if st.br == 0 else branch_sum[:, st.dc % 2, 0:c]
                dve.scalar_tensor_tensor(out=dst, in0=merge_tanh[:, st.dc % 2, 0:c], scalar=1.0,
                                         in1=G[st.job.n % 2][:, 0:c], op0=ALU.add, op1=ALU.mult)\
                    .then_inc(g_free[st.job.n % 2], 1)
                if st.br == 2:
                    dve.wait_ge(m_hi_ready, st.m_n + 1)
                    dve.scalar_tensor_tensor(out=m_lo[:, st.dc, 0:c], in0=m[:, st.dc, 0:c], scalar=0.5,
                                             in1=m_hi[:, st.dc, 0:c].bitcast(F32), op0=ALU.mult,
                                             op1=ALU.subtract).then_inc(m_lo_ready, 1)

            def gated_residual_step(st):
                dve.wait_ge(*complete(st.job))
                halves = range(2 if st.cols == BOTH else 1)
                for j in halves:
                    at = slice(SEQ * j, SEQ * j + SEQ)
                    v = x[:, st.dc, at]
                    ins = dve.scalar_tensor_tensor(out=v, in0=G[st.job.n % 2][:, at],
                                                   scalar=ada[:, st.layer, 16 + st.dc, j:j + 1], in1=v,
                                                   op0=ALU.mult, op1=ALU.add)
                ins.then_inc(g_free[st.job.n % 2], 1)

            def plain_residual_step(st):
                dve.wait_ge(*complete(st.job))
                v = x[:, st.dc, 0:SEQ]
                dve.tensor_tensor(v, G[st.job.n % 2][:, 0:SEQ], v, ALU.add).then_inc(g_free[st.job.n % 2], 1)

            def scores_step(st):
                u = st.u
                s = S[u.s_use % 2]
                dve.wait_ge(s_full, u.s_use + 1)
                if u.bias:
                    dve.wait_ge(bias_ready, u.g.bias.n + 1)
                    row = (2 - 2 * u.b) * GRID_W
                    dve.tensor_tensor(s[:, 0:SEQ], s[:, 0:SEQ], bias[:, u.g.c % 2, u.hp, row:row + SEQ], ALU.add)\
                        .then_inc(biased, 1)
                    dve.wait_ge(biased, u.bias_n + 1)
                dve.tensor_reduce(row_stat[:, 0, u.n % 4:u.n % 4 + 1], s[:, 0:u.keys], AX_X, ALU.max, negate=True)\
                    .then_inc(max_ready, 1)

            def turn_probs_step(st):
                u = st.u
                dve.wait_ge(*s_out(u.s_use))
                dve.reciprocal(row_stat[:, 2, u.n % 4:u.n % 4 + 1], row_stat[:, 1, u.n % 4:u.n % 4 + 1])\
                    .then_inc(sum_ready, 1)

            def values_step(st):
                u = st.u
                dve.wait_ge(o_full, u.o_use + 1)
                dve.wait_ge(sum_ready, u.n + 1)
                dve.tensor_scalar(out_rows[:, u.b, DH * u.hp:DH * u.hp + DH], O[:, 0:DH],
                                  row_stat[:, 2, u.n % 4:u.n % 4 + 1], None, ALU.mult).then_inc(o_free, 1)

            def turn_out_step(st):
                g = st.g
                dve.wait_ge(m_full, st.m + 1)
                dve.wait_ge(*evacuated(g.gate.job))
                if st.n:
                    dve.wait_ge(o_lo_ready, st.n)
                turned[g.slot] = st.m + 1
                scale = gn_half[:, 4 * g.layer + g.c:4 * g.layer + g.c + 1] if g.branch == "ret" else 0.5
                dve.scalar_tensor_tensor(out=gated[:, 0:g.live], in0=M[:, 0:g.live], scalar=scale,
                                         in1=branch_gate[:, g.slot, 0:g.live], op0=ALU.mult, op1=ALU.mult)\
                    .then_inc(m_free, 1)
                o = o_of(g.branch)
                dve.wait_ge(o_hi_ready, st.n + 1)
                dve.tensor_tensor(o_lo[o][:, g.c, 0:g.live], gated[:, 0:g.live],
                                  o_hi[o][:, g.c, 0:g.live].bitcast(F32), ALU.subtract).then_inc(o_lo_ready, 1)

            def ret_scores_step(st):
                g, s = st.g, S[st.s_use % 2]
                dve.wait_ge(s_full, st.s_use + 1)
                dve.wait_ge(decay_ready, 2 * g.decay.n + 2)
                at = P * (1 - st.j % 2)
                own, cross = decay_s[:, 0, at:at + SEQ], decay_s[:, 2, at:at + SEQ]
                ins = dve.tensor_tensor(work[:, st.j, 0:SEQ], s[:, 0:SEQ], own if st.j < 2 else cross, ALU.mult)
                if st.cols == BOTH:
                    ins = dve.tensor_tensor(work[:, st.j, SEQ:BOTH], s[:, SEQ:BOTH], own, ALU.mult)
                ins.then_inc(s_free[st.s_use % 2], 1)

            def ret_out_step(st):
                nb = st.g.blocks
                dve.wait_ge(o_full, st.o_use + 1)
                for b in range(nb):
                    dve.bn_stats(bn[:, b, :], O[:, P * b:P * b + P]).then_inc(bn_step, 1)
                for b in range(nb):
                    dve.wait_ge(bn_step, st.bn_at + b + 1)
                    dve.bn_aggr(mean_var[:, b, :], bn[:, b, :]).then_inc(bn_step, 1)
                dve.wait_ge(bn_step, st.bn_at + 2 * nb)
                dve.tensor_scalar(ret_rs[:, 0:nb], mean_var[:, 0:nb, 1], EPS, None, ALU.add).then_inc(bn_step, 1)
                dve.wait_ge(ret_pow, st.n + 1)
                for b in range(nb):
                    ins = dve.tensor_scalar(out_rows[:, b, :], O[:, P * b:P * b + P],
                                            mean_var[:, b, 0:1], ret_rs[:, b:b + 1], ALU.subtract, ALU.mult)
                ins.then_inc(o_free, 1)

            def head_norm_step(st):
                th_count[0] += 1
                n = st.cols
                dve.wait_ge(m_free, st.m + 1)
                dve.reciprocal(head_sq[:, 0:n], head_sq[:, 0:n]).then_inc(head_rstd, 1)

            def rotate_step(st):
                n, norm = st.norm.cols, st.norm
                dst = g_buf(st.g, "k" if st.what == "key" else "q")
                at = PARAM_AT["k_norm_w"] + st.g.layer
                w = par[:, at:at + 1] if st.what == "key" else q_norm[:, st.g.layer:st.g.layer + 1]
                dve.wait_ge(head_rstd, norm.n + 1)
                dve.scalar_tensor_tensor(out=dst[:, 0:n], in0=stage[:, 0:n], scalar=w, in1=head_sq[:, 0:n],
                                         op0=ALU.mult, op1=ALU.mult).then_inc(qk_normed, 1)
                dve.wait_ge(m_full, st.m + 1)
                dve.tensor_tensor(head_sq[:, 0:SEQ], M[:, 0:SEQ], C_("sin"), ALU.mult).then_inc(m_free, 1)
                dve.wait_ge(cos_ready, st.n + 1)
                dve.wait_ge(m_free, st.m + 1)
                dve.tensor_tensor(dst[:, 0:SEQ], stage[:, 0:SEQ], head_sq[:, 0:SEQ], ALU.add).then_inc(rot_done, 1)

            def ffn_step(st):
                f, t0 = st.n, st.t

                def mult(i, r=None):
                    cnt, up = (0, 0) if r is None else (r * 2, r * 6)
                    dve.wait_ge(silu_ready, cnt + (FC * f + i + 1))
                    dve.wait_ge(tile_used, up + (t0 + ffn_tile("u", i) + 1))
                    if i >= 2:
                        dve.wait_ge(hid_lo_ready, cnt + (FC * f + i - 1))
                    dve.tensor_tensor(hidden[:, i % 2, :], silu_g[:, i % 2, :], S[i % 2][:, 0:SEQ], ALU.mult)\
                        .then_inc(hid_ready, 1)

                def low(i, r=None):
                    cnt = 0 if r is None else r * 2
                    dve.wait_ge(hid_hi_ready, cnt + (FC * f + i + 1))
                    dve.tensor_tensor(hid_lo[:, i % 2, :], hidden[:, i % 2, :], hid_hi[:, i % 2, :].bitcast(F32),
                                      ALU.subtract).then_inc(hid_lo_ready, 1)

                def round_(i, r=None):
                    a = t0 + 2 + 3 * i
                    split(a + 2, r)
                    low(i, r)
                    split(a + 3, r)
                    if r is not None or a + 4 < NT:
                        split(a + 4, r)
                    mult(i + 1, r)

                split(t0 + 2)
                split(t0 + 3)
                mult(0)
                round_(0)
                peeled = 2 if t0 + 3 * FC == NT else 0
                with dve.Fori(0, (FC - 2 - peeled) // 2) as r:
                    round_(1, r)
                    round_(2, r)
                for i in range(FC - 1 - peeled, FC - 1):
                    round_(i)
                low(FC - 1)
                if t0 + 3 * FC - 1 + AHEAD < NT:
                    split(t0 + 3 * FC - 1 + AHEAD)
                for q in range(4):
                    if q < 3:
                        dve.wait_ge(ffn_out, 3 * f + q + 1)
                    else:
                        dve.wait_ge(tile_used, t0 + 3 * FC)
                    v = x[:, 2 * q:2 * q + 2, 0:SEQ]
                    dve.scalar_tensor_tensor(out=v, in0=ffn_bank[q][:, :].rearrange("p (c t) -> p c t", c=2),
                                             scalar=0.5, in1=v, op0=ALU.mult, op1=ALU.add).then_inc(ffn_added, 1)

            def conv_step_dve(st):
                c = st.c
                at = PARAM_AT["rec_conv_w"] + c
                w = [par[:, at + KC * i:at + KC * i + 1] for i in range(4)]
                b = PARAM_AT["rec_conv_b"] + c
                if c == 0:
                    dve.memset(r_pad[:, :, 0:3], 0.0).then_inc(mix_step, 1)
                dve.wait_ge(*evacuated(st.job))
                dve.wait_ge(mix_step, 1)
                dst = r_conv[:, c, :]
                dve.tensor_scalar(dst, r_pad[:, c, 0:SEQ], w[0], par[:, b:b + 1], ALU.mult, ALU.add)\
                    .then_inc(conv_step, 1)
                for i in range(1, 4):
                    dve.wait_ge(conv_step, 4 * c + i)
                    dve.scalar_tensor_tensor(out=dst, in0=r_pad[:, c, i:i + SEQ], scalar=w[i], in1=dst,
                                             op0=ALU.mult, op1=ALU.add).then_inc(conv_step, 1)

            def rec_decay_step(st):
                c = st.c
                dve.wait_ge(decays, 2 * c + 1)
                if c >= 2:
                    dve.wait_ge(root_in, c - 1)
                q = mix_t[:, c % 2, :]
                dve.tensor_scalar(q, th[:, c, :], -1.0, 1.0, ALU.mult, ALU.add).then_inc(root_step, 1)
                dve.wait_ge(root_step, 2 * c + 1)
                dve.reciprocal(q, q).then_inc(root_step, 1)
                dve.wait_ge(root_step, 2 * c + 2)
                dve.scalar_tensor_tensor(out=th[:, c, :], in0=th[:, c, :], scalar=-2.0, in1=q, op0=ALU.mult,
                                         op1=ALU.mult).then_inc(root_in, 1)

            def rec_scan_step(st):
                c = st.c
                dve.wait_ge(bx_ready, c + 1)
                dve.wait_ge(decays, 2 * c + 2)
                dve.tensor_tensor_scan(r_conv[:, c, :], g_a[:, c, :], g_x[:, c, :], 0.0, ALU.mult, ALU.add)\
                    .then_inc(scanned, 1)

            def mix_low(c, n):
                dve.wait_ge(mix_hi_ready, n + 1)
                dve.tensor_tensor(mix_lo[:, c, :], mix_t[:, n % 2, :], mix_hi[:, c, :].bitcast(F32), ALU.subtract)\
                    .then_inc(mix_lo_ready, 1)

            def rec_out_step(st):
                c = st.c
                dve.wait_ge(y_ready, c + 1)
                dve.wait_ge(scanned, c + 1)
                if c >= 2:
                    dve.wait_ge(mix_lo_ready, st.n - 1)
                dve.tensor_tensor(mix_t[:, st.n % 2, :], y_act[:, c, :], r_conv[:, c, :], ALU.mult)\
                    .then_inc(mix_ready, 1)
                mix_low(c, st.n)

            def spatial_weights_step(st):
                for i in range(2):
                    dve.wait_ge(t_full, st.t_uses[i] + 1)
                    dve.tensor_copy(ws_t[:, 4 * i:4 * i + 4, :],
                                    T[st.t_uses[i] % 2][:, :].rearrange("p (h d) -> p h d", h=4))\
                        .then_inc(t_free[st.t_uses[i] % 2], 1)

            def sg_mix_step(st):
                c = st.c
                dve.wait_ge(s_full, st.s_use + 1)
                if c == 0:
                    dve.wait_ge(mix_landed, 6 * 16)
                if c >= 2:
                    dve.wait_ge(mix_lo_ready, KC + st.n - 1)
                q = mix_t[:, c % 2, :].rearrange("p (t d) -> p t d", t=2)
                s = S[st.s_use % 2][:, 0:SEQ].rearrange("p (t d) -> p t d", t=2)
                dve.tensor_tensor(q, s, ws_b[:, c, :].unsqueeze(1).to_broadcast([P, 2, P]), ALU.add)\
                    .then_inc(s_free[st.s_use % 2], 1)
                dve.wait_ge(*s_out(st.s_use))
                dve.wait_ge(*evacuated(u_jobs[c]))
                dve.tensor_tensor(mix_t[:, c % 2, :], mix_t[:, c % 2, :], sg_u[:, c, :], ALU.mult)\
                    .then_inc(mix_ready, 1)
                mix_low(c, KC + st.n)

            run = {"split": lambda st: split(st.t), "turn_in": turn_in_step, "ada": ada_step,
                   "ada_scale": ada_scale_step, "rms": rms_step, "normed": normed_step, "value_turn": value_turn_step,
                   "gate": gate_step, "merge": merge_step, "gated_residual": gated_residual_step,
                   "plain_residual": plain_residual_step, "scores": scores_step, "turn_probs": turn_probs_step,
                   "values": values_step, "turn_out": turn_out_step, "ret_scores": ret_scores_step,
                   "ret_out": ret_out_step, "head_norm": head_norm_step, "rotate": rotate_step, "ffn": ffn_step,
                   "conv": conv_step_dve, "rec_decay": rec_decay_step, "rec_scan": rec_scan_step,
                   "rec_out": rec_out_step, "spatial_weights": spatial_weights_step, "sg_mix": sg_mix_step}
            for st in steps:
                if st.kind in run:
                    run[st.kind](st)

        @block.tensor
        def _(pe):
            ident = C_("ident")

            def three(dst, w, hi, lo, start, stop, shared=False):
                slot, blk = w
                at = slice(P * blk, P * blk + P)
                nc.tensor.matmul(dst, w_hi[:, slot, at], hi, start=start, stop=False, skip_group_check=shared)
                nc.tensor.matmul(dst, w_hi[:, slot, at], lo, start=False, stop=False, skip_group_check=shared)
                return nc.tensor.matmul(dst, w_lo[:, slot, at], hi, start=False, stop=stop, skip_group_check=shared)

            def product_step(st):
                job = st.job
                n = job.cols
                dst = G[job.n % 2][:, 0:n]
                if st.at == 0:
                    pe.wait_ge(lo_ready, job.tile + 1)
                    if job.n >= 2:
                        pe.wait_ge(g_free[job.n % 2], job.n // 2)
                    if job.src == "c":
                        pe.wait_ge(set_up_dve, 2)
                    if job.src.startswith("o_"):
                        pe.wait_ge(o_lo_ready, job.outs.out.n + 1)
                for i in range(st.at, st.at + st.part):
                    if job.src == "h":
                        if job.norm:
                            pe.wait_ge(h_lo_ready, job.norm.chunks[i].h + 1)
                        hi, lo = h_hi[:, i, 0:n], h_lo[:, i, 0:n]
                    elif job.src == "c":
                        hi, lo = c_hi[:, i, :], c_lo[:, i, :]
                    elif job.src == "m":
                        if m_waited[0] < m_base(job) + i + 1:
                            m_waited[0] = m_base(job) + i + 1
                            pe.wait_ge(m_lo_ready, m_waited[0])
                        hi, lo = m_hi[:, i, 0:n], m_lo[:, i, 0:n]
                    elif job.src == "mix":
                        if mix_waited[0] < KC * job.mixer + i + 1:
                            mix_waited[0] = KC * job.mixer + i + 1
                            pe.wait_ge(mix_lo_ready, mix_waited[0])
                        hi, lo = mix_hi[:, i, :], mix_lo[:, i, :]
                    else:
                        o = o_of(job.src[2:])
                        hi, lo = o_hi[o][:, i, 0:n], o_lo[o][:, i, 0:n]
                    ins = three(dst, (job.tile % SPLIT, st.base + i), hi, lo, start=(i == 0), stop=(i == job.blocks - 1))
                if st.at + st.part == job.blocks:
                    ins.then_inc(half_used if job.first_half else tile_used, 1)

            m_waited, mix_waited = [0], [0]

            def m_base(job):
                return 0 if job.tile < TILES.index(("w_out", 1, 0)) else KC

            def turn_in_step(st):
                pe.wait_ge(con_landed, 16)
                pe.wait_ge(tok_landed, 32)
                if st.t_use >= 2:
                    pe.wait_ge(t_free[st.t_use % 2], st.t_use // 2)
                for b in range(4):
                    ins = nc.tensor.transpose(T[st.t_use % 2][:, P * b:P * b + P], tok[:, b, P * st.k:P * st.k + P], ident)
                ins.then_inc(t_full, 1)

            def square_sum_step(st):
                norm = st.norm
                c = norm.cols
                pe.wait_ge(squared, st.n + 1)
                if st.k == 0 and norm.m:
                    pe.wait_ge(m_free, norm.m)
                ins = nc.tensor.matmul(M[:, 0:c], C_("mean_all"), square[:, st.k % 2, 0:c], start=(st.k == 0),
                                       stop=(st.k == KC - 1))
                ins.then_inc(m_full if st.k == KC - 1 else sq_used, 1)

            def normed_step(st):
                if st.norm.how != "out":
                    return
                pe.wait_ge(f_ready, st.f + 1)
                pe.wait_ge(t_free[st.t_use % 2], st.t_use // 2)
                for b in range(2):
                    ins = nc.tensor.transpose(T[st.t_use % 2][:, P * b:P * b + P],
                                              scaled[:, st.k % 2, P * b:P * b + P], ident)
                ins.then_inc(t_full, 1)

            def value_turn_step(st):
                pe.wait_ge(*evacuated(st.evac.job))
                pe.wait_ge(m_free, st.m)
                for b in range(4):
                    ins = nc.tensor.transpose(M[:, P * b:P * b + P], stage[:, P * b:P * b + P], ident)
                ins.then_inc(m_full, 1)

            def scores_step(st):
                u = st.u
                g = u.g
                if g.branch == "na":
                    pe.wait_ge(*evacuated(g.k_job.job))
                    pe.wait_ge(*evacuated(g.q_job.job))
                else:
                    pe.wait_ge(rot_done, g.q_rot.n + 1)
                if u.s_use >= 2:
                    pe.wait_ge(s_free[u.s_use % 2], u.s_use // 2)
                at = slice(DH * u.hp, DH * u.hp + DH)
                nc.tensor.matmul(S[u.s_use % 2][:, 0:u.keys], g_buf(g, "q")[at, P * u.b:P * u.b + P],
                                 g_buf(g, "k")[at, u.key_at:u.key_at + u.keys], start=True, stop=True)\
                    .then_inc(s_full, 1)

            def turn_probs_step(st):
                u = st.u
                pe.wait_ge(*s_out(u.s_use))
                if u.t_use >= 2:
                    pe.wait_ge(t_free[u.t_use % 2], u.t_use // 2)
                for j in range(u.keys // P):
                    ins = nc.tensor.transpose(T[u.t_use % 2][:, P * j:P * j + P], probs[:, u.n % 2, P * j:P * j + P],
                                              ident)
                ins.then_inc(t_full, 1)

            def values_step(st):
                u = st.u
                g = u.g.kv if u.g.branch == "gqa" else u.g
                pe.wait_ge(*t_out(u.t_use))
                if u.o_use:
                    pe.wait_ge(o_free, u.o_use)
                pe.wait_ge(m_free, g.v_turn.m + 1)
                v = g_buf(g, "v")
                blocks = list(key_blocks(u))
                for i, j in enumerate(blocks):
                    ins = nc.tensor.matmul(O[:, 0:DH], probs_t[:, u.n % 2, P * i:P * i + P],
                                           v[:, j, DH * u.hp:DH * u.hp + DH], start=(i == 0),
                                           stop=(i == len(blocks) - 1))
                ins.then_inc(o_full, 1)

            def turn_out_step(st):
                g = st.g
                pe.wait_ge(o_free, (g.ret_out.o_use if g.branch == "ret" else g.last_unit.o_use) + 1)
                pe.wait_ge(m_free, st.m)
                for b in range(g.blocks):
                    ins = nc.tensor.transpose(M[:, P * b:P * b + P], out_rows[:, b, :], ident)
                ins.then_inc(m_full, 1)

            def ret_scores_step(st):
                g = st.g
                pe.wait_ge(*evacuated(g.k_job.job))
                pe.wait_ge(*evacuated(g.q_job.job))
                if st.s_use >= 2:
                    pe.wait_ge(s_free[st.s_use % 2], st.s_use // 2)
                nc.tensor.matmul(S[st.s_use % 2][:, 0:st.cols], g_buf(g, "k")[:, P * st.j:P * st.j + P],
                                 g_buf(g, "q")[:, 0:st.cols], start=True, stop=True).then_inc(s_full, 1)

            def ret_out_step(st):
                g = st.g
                pe.wait_ge(*s_out(g.last_scores.s_use))
                pe.wait_ge(m_free, g.v_turn.m + 1)
                if st.o_use:
                    pe.wait_ge(o_free, st.o_use)
                v = g_buf(g, "v")
                for b in range(g.blocks):
                    keys = range(4) if b < 2 else range(2, 4)
                    for j in keys:
                        ins = nc.tensor.matmul(O[:, P * b:P * b + P], work[:, j, P * b:P * b + P], v[:, j, :],
                                               start=(j == keys[0]), stop=(j == 3))
                ins.then_inc(o_full, 1)

            def head_norm_step(st):
                pe.wait_ge(*evacuated(st.job))
                pe.wait_ge(m_free, st.m)
                nc.tensor.matmul(M[:, 0:st.cols], C_("mean_head"), head_sq[:, 0:st.cols], start=True, stop=True)\
                    .then_inc(m_full, 1)

            def rotate_step(st):
                pe.wait_ge(qk_normed, st.n + 1)
                pe.wait_ge(m_free, st.m)
                dst = g_buf(st.g, "k" if st.what == "key" else "q")
                nc.tensor.matmul(M[:, 0:SEQ], C_("swap"), dst[:, 0:SEQ], start=True, stop=True).then_inc(m_full, 1)

            def ffn_step(st):
                f, t0, norm = st.n, st.t, st.norm

                def up(i, which, r=None, first=False):
                    t = t0 + ffn_tile(which, i)
                    base, cnt = (0, 0) if r is None else (r * 6, r * 2)
                    pe.wait_ge(lo_ready, base + (t + 1))
                    if i >= 2:
                        pe.wait_ge(silu_ready if which == "g" else hid_ready, cnt + (FC * f + i - 1))
                    dst = (G if which == "g" else S)[i % 2][:, 0:SEQ]
                    for k in range(KC):
                        if first:
                            pe.wait_ge(h_lo_ready, norm.chunks[k].h + 1)
                        ins = three(dst, (t % SPLIT, k), h_hi[:, k, 0:SEQ], h_lo[:, k, 0:SEQ], k == 0, k == KC - 1)
                    ins.then_inc(tile_used, 1)

                def down(i, r=None, last=False):
                    t = t0 + ffn_tile("o", i)
                    base, cnt = (0, 0) if r is None else (r * 6, r * 2)
                    pe.wait_ge(lo_ready, base + (t + 1))
                    pe.wait_ge(hid_lo_ready, cnt + (FC * f + i + 1))
                    for dc in range(KC):
                        dst = ffn_bank[dc // 2][:, SEQ * (dc % 2):SEQ * (dc % 2) + SEQ]
                        ins = three(dst, (t % SPLIT, dc), hid_hi[:, i % 2, :], hid_lo[:, i % 2, :],
                                    i == 0 and dc % 2 == 0, last, shared=True)
                        if last and dc % 2 and dc < KC - 1:
                            ins.then_inc(ffn_out, 1)
                    ins.then_inc(tile_used, 1)

                def round_(i, r=None):
                    up(i + 1, "g", r)
                    up(i + 1, "u", r)
                    down(i, r)

                up(0, "g", first=True)
                up(0, "u")
                round_(0)
                with pe.Fori(0, (FC - 2) // 2) as r:
                    round_(1, r)
                    round_(2, r)
                down(FC - 1, last=True)

            def rec_gates_step(st):
                if st.c == 0:
                    pe.wait_ge(mix_landed, 64)
                pe.wait_ge(conv_step, 4 * st.c + 4)
                pe.wait_ge(s_free[st.s_use % 2], st.s_use // 2)
                s = S[st.s_use % 2]
                nc.tensor.matmul(s[:, 0:SEQ], gate_w[:, 0, st.c, :], r_conv[:, st.c, :], start=True, stop=True)
                nc.tensor.matmul(s[:, SEQ:BOTH], gate_w[:, 1, st.c, :], r_conv[:, st.c, :], start=True, stop=True)\
                    .then_inc(s_full, 1)

            def spatial_weights_step(st):
                pe.wait_ge(ws_cut, 1)
                for i in range(2):
                    u = st.t_uses[i]
                    pe.wait_ge(t_free[u % 2], u // 2)
                    for h in range(4):
                        ins = nc.tensor.transpose(T[u % 2][:, P * h:P * h + P], ws[:, 4 * i + h, :], ident)
                    ins.then_inc(t_full, 1)

            def sg_turn_step(st):
                pe.wait_ge(v_normed, st.c + 1)
                pe.wait_ge(t_free[st.t_use % 2], st.t_use // 2)
                for b in range(2):
                    ins = nc.tensor.transpose(T[st.t_use % 2][:, P * b:P * b + P], sg_v[:, st.c, P * b:P * b + P],
                                              ident)
                ins.then_inc(t_full, 1)

            def sg_mix_step(st):
                pe.wait_ge(*t_out(st.turn.t_use))
                pe.wait_ge(s_free[st.s_use % 2], st.s_use // 2)
                for b in range(2):
                    ins = nc.tensor.matmul(S[st.s_use % 2][:, P * b:P * b + P], sg_vt[:, st.c % 2, P * b:P * b + P],
                                           ws_t[:, st.c, :], start=True, stop=True)
                ins.then_inc(s_full, 1)

            run = {"product": product_step, "turn_in": turn_in_step, "square_sum": square_sum_step,
                   "normed": normed_step, "value_turn": value_turn_step, "scores": scores_step,
                   "turn_probs": turn_probs_step, "values": values_step, "turn_out": turn_out_step,
                   "ret_scores": ret_scores_step, "ret_out": ret_out_step, "head_norm": head_norm_step,
                   "rotate": rotate_step, "ffn": ffn_step, "rec_gates": rec_gates_step,
                   "spatial_weights": spatial_weights_step, "sg_turn": sg_turn_step, "sg_mix": sg_mix_step}
            for st in steps:
                if st.kind in run:
                    run[st.kind](st)


def kernel(**inputs):
    from concourse import bacc
    from concourse.bass_utils import run_bass_kernel_spmd

    a = {name: np.ascontiguousarray(v) for name, v in inputs.items()}
    arrays = {
        "weights": lay_out_weights(a),
        "params": lay_out_params(a),
        "consts": shape_tables(),
        "tokens": np.concatenate([a["x"][0], a["ctx"][0]]),
        "rpb": lay_out_bias(a["na_rpb"]),
        "gate_a": a["rec_gate_a_w_2"][0],
        "gate_x": a["rec_gate_x_w_2"][0],
        "spatial": a["sg_w_s_2"][0],
        "spatial_b": a["sg_b_s_2"][0],
    }
    arrays = {name: np.ascontiguousarray(v) for name, v in arrays.items()}
    nc = bacc.Bacc("TRN2", target_bir_lowering=False, num_devices=1)
    args = [nc.dram_tensor(f"in_{n}", v.shape, F32, kind="ExternalInput").ap() for n, v in arrays.items()]
    args.append(nc.dram_tensor("out", (SEQ, D), F32, kind="ExternalOutput").ap())
    block_kernel(nc, *args)
    r = run_bass_kernel_spmd(nc, [{f"in_{n}": v for n, v in arrays.items()}], core_ids=[0])
    return r.results[0]["out"].reshape(1, SEQ, D)
```

```python
from contextlib import ExitStack

import numpy as np

import concourse.bass as bass
from concourse import mybir

F32 = mybir.dt.float32
F32R = mybir.dt.float32r
ALU = mybir.AluOpType
ACT = mybir.ActivationFunctionType
AX_X = mybir.AxisListType.X

P = 128
D = 1024
KC = D // P
SEQ = 256
BOTH = 2 * SEQ
DEPTH = 2
GRID_W = 64
ROWS = SEQ // GRID_W
RET_HEADS = 4
NA_HEADS = 8
GQA_HEADS = 8
DH = 64
RPB_COLS = 31
D_FF = 2816
FC = D_FF // P
EPS = 1e-6

RAW = 6
SPLIT = 3
AHEAD = 2

IN_AT = dict(zip(
    "rq rk rv rg nq nk nv ng gq gk gv gg mg".split(),
    np.cumsum([0, 512, 512, 512, 512, 512, 512, 512, 512, 512, 128, 128, 512]).tolist(),
))
GQA_COLS = [np.r_[DH * c:DH * c + DH, DH * (c + 4):DH * (c + 4) + DH] for c in range(4)]


ADA_FIRST = [(0, 0), (0, 1)]
ADA_BESIDE = [(0, 2), (1, 0), (1, 1), (1, 2)]
ADA_SLOTS = [0] * 4 + [3, 3, 2] * 4


def tile_order():
    out = [("ada", layer, section, k) for layer, section in ADA_FIRST for k in range(KC)]
    for layer in range(DEPTH):
        ada = [("ada", *section, k) for section in ADA_BESIDE for k in range(KC)] if layer == 0 else []
        slots = list(ADA_SLOTS)
        for c in range(4):
            for n, name in enumerate(("nk", "nv", "nq", "ng")):
                out.append((name, layer, c))
        for h in range(4):
            for n, name in enumerate(("rk", "rv", "rq", "rg")):
                out.append((name, layer, h))
                count = slots.pop(0)
                out += ada[:count]
                del ada[:count]
        for q in range(4):
            out += [("mg", layer, KC + 2 * q), ("mg", layer, KC + 2 * q + 1), ("w_na_o", layer, q)]
        out += [("gk", layer, 0), ("gv", layer, 0)]
        for c in range(4):
            out += [("gq", layer, c), ("gg", layer, c)]
            for q in {0: [], 1: [0], 2: [1], 3: [2, 3]}[c]:
                out += [("mg", layer, 2 * q), ("mg", layer, 2 * q + 1), ("w_ret_o", layer, q)]
        for q in range(4):
            out += [("mg", layer, 2 * KC + 2 * q), ("mg", layer, 2 * KC + 2 * q + 1), ("w_gqa_o", layer, q)]
        out += [("w_out", layer, n) for n in range(KC)]
    for layer in range(DEPTH):
        for f in (0, 1):
            ffn = [("ffn_g", layer, f, 0), ("ffn_u", layer, f, 0)]
            for i in range(FC - 1):
                ffn += [("ffn_g", layer, f, i + 1), ("ffn_u", layer, f, i + 1), ("ffn_o", layer, f, i)]
            out += ffn + [("ffn_o", layer, f, FC - 1)]
            if f == 0 and layer == 0:
                out += [("rec_r", 0, n) for n in range(KC)] + [("rec_y", 0, n) for n in range(KC)]
                out += [("rec_o", 0, n) for n in range(KC)]
            if f == 0 and layer == 1:
                out += [("sg_v", 0, n) for n in range(KC)] + [("sg_u", 0, n) for n in range(KC)]
                out += [("sg_o", 0, n) for n in range(KC)]
    return out


TILES = tile_order()
NT = len(TILES)


def column_tile(w, cols):
    return w[:, cols].reshape(KC, P, P).transpose(1, 0, 2).reshape(P, D)


def out_tile(w, q):
    return w[:, 2 * P * q:2 * P * (q + 1)].reshape(4, P, 2, P).transpose(1, 2, 0, 3).reshape(P, D)


def lay_out_weights(a):
    out = np.empty((NT, P, D), np.float32)
    gqa_rows = np.concatenate(GQA_COLS)
    for t, (kind, layer, *which) in enumerate(TILES):
        n = which[0]
        cols = slice(P * n, P * n + P)
        if kind == "ada":
            out[t] = a["ada_w"][layer][P * which[1]:P * which[1] + P, D * n:D * n + D]
        elif kind in ("gq", "gg"):
            out[t] = column_tile(a["w_in"][layer], IN_AT[kind] + GQA_COLS[n])
        elif kind in IN_AT:
            out[t] = column_tile(a["w_in"][layer], slice(IN_AT[kind] + P * n, IN_AT[kind] + P * n + P))
        elif kind == "w_gqa_o":
            out[t] = out_tile(a[kind][layer][gqa_rows], n)
        elif kind in ("w_na_o", "w_ret_o"):
            out[t] = out_tile(a[kind][layer], n)
        elif kind == "w_out":
            out[t] = column_tile(a[kind][layer], cols)
        elif kind in ("ffn_g", "ffn_u"):
            i = which[1] * P + (D_FF if kind == "ffn_u" else 0)
            out[t] = column_tile(a[f"ffn{n + 1}_w_in_2"][layer], slice(i, i + P))
        elif kind == "ffn_o":
            out[t] = a[f"ffn{n + 1}_w_out_2"][layer][P * which[1]:P * which[1] + P]
        elif kind == "rec_y":
            out[t] = column_tile(a["rec_w_in_2"][0], cols)
        elif kind == "rec_r":
            out[t] = column_tile(a["rec_w_in_2"][0], slice(D + P * n, D + P * n + P))
        elif kind == "rec_o":
            out[t] = column_tile(a["rec_w_out_2"][0], cols)
        elif kind == "sg_u":
            out[t] = column_tile(a["sg_w_in_2"][0], cols)
        elif kind == "sg_v":
            out[t] = column_tile(a["sg_w_in_2"][0], slice(D + P * n, D + P * n + P))
        elif kind == "sg_o":
            out[t] = column_tile(a["sg_w_out_2"][0], cols)
    return out


def by_partition(a):
    a = np.asarray(a)
    a = a.reshape(-1, a.shape[-1] // P, P)
    return a.transpose(2, 0, 1).reshape(P, -1)


PARAMS = [("c", 8), ("c_ctx", 8), ("ada_b", 48), ("norm_w", 16), ("ret_gn_w", 8), ("q_norm_w", 2), ("k_norm_w", 2),
          ("decay", 16), ("ffn1_norm", 16), ("mix_norm", 16), ("ffn2_norm", 16), ("final_norm_w", 8),
          ("final_norm", 8), ("rec_conv_w", 32), ("rec_conv_b", 8), ("rec_gate_a_b", 8), ("rec_gate_x_b", 8),
          ("rec_lambda", 8), ("sg_v_norm", 8)]
PARAM_AT = dict(zip([n for n, _ in PARAMS], np.cumsum([0] + [w for _, w in PARAMS]).tolist()))
NPARAM = sum(w for _, w in PARAMS)


def lay_out_params(a):
    rows = {
        "c": by_partition(a["c"]), "c_ctx": by_partition(a["c_ctx"]), "ada_b": by_partition(a["ada_b"]),
        "norm_w": by_partition(a["norm_w"]), "ret_gn_w": by_partition(a["ret_gn_w"]),
        "q_norm_w": np.tile(a["q_norm_w"], (1, 2)).T, "k_norm_w": np.tile(a["k_norm_w"], (1, 2)).T,
        "decay": np.broadcast_to(a["ret_log_decay"].reshape(1, -1), (P, 16)),
        "ffn1_norm": by_partition(a["ffn1_norm_2"]), "mix_norm": by_partition(a["mix_norm_2"]),
        "ffn2_norm": by_partition(a["ffn2_norm_2"]), "final_norm_w": by_partition(a["final_norm_w"]),
        "final_norm": by_partition(a["final_norm_2"]), "rec_conv_w": by_partition(a["rec_conv_w_2"][0]),
        "rec_conv_b": by_partition(a["rec_conv_b_2"]),
        "rec_gate_a_b": by_partition(a["rec_gate_a_b_2"].reshape(1, -1)),
        "rec_gate_x_b": by_partition(a["rec_gate_x_b_2"].reshape(1, -1)),
        "rec_lambda": by_partition(a["rec_lambda_2"]), "sg_v_norm": by_partition(a["sg_v_norm_2"]),
    }
    return np.ascontiguousarray(np.concatenate([rows[n] for n, _ in PARAMS], axis=1))


CONSTS = [("ident", P), ("mean_all", P), ("mean_head", P), ("swap", P), ("cos", SEQ), ("sin", SEQ),
          ("dif", 3 * P), ("window", GRID_W), ("parts", 2)]
CONST_AT = dict(zip([n for n, _ in CONSTS], np.cumsum([0] + [w for _, w in CONSTS]).tolist()))
NCONST = sum(w for _, w in CONSTS)


def shape_tables():
    p = np.arange(P)
    head = (p[:, None] // DH == p[None, :] // DH)
    partner = np.where(p % 32 < 16, p + 16, p - 16)
    t = np.arange(SEQ)
    freqs = (np.float32(10000.0) ** (-np.arange(16, dtype=np.float32) / 16)).astype(np.float32)
    pos = np.where(((p % DH) < 32)[:, None], (t // GRID_W)[None], (t % GRID_W)[None]).astype(np.float32)
    ang = (pos * freqs[p % 16][:, None]).astype(np.float32)
    sign = np.where(p % 32 < 16, -1.0, 1.0)[:, None]
    qc, kc = (p % GRID_W)[:, None], np.arange(GRID_W)[None]
    start = np.clip(qc - 8, 0, GRID_W - 16)
    rows = {
        "ident": np.eye(P), "mean_all": np.full((P, P), 1.0 / D), "mean_head": head / DH,
        "swap": (p[:, None] == partner[None, :]), "cos": np.cos(ang), "sin": np.sin(ang) * sign,
        "dif": np.arange(3 * P)[None] - P - p[:, None],
        "parts": (p[:, None] % 2 == np.arange(2)[None]),
        "window": np.where((kc >= start) & (kc < start + 16), 0.0, -1e30),
    }
    return np.concatenate([rows[n].astype(np.float32) for n, _ in CONSTS], axis=1)


def lay_out_bias(rpb):
    pad = np.pad(rpb, ((0, 0), (0, 0), (0, 0), (GRID_W - 16, GRID_W - 16)))
    shifted = np.stack([pad[..., GRID_W - 1 - q:2 * GRID_W - 1 - q] for q in range(GRID_W)], axis=3)
    by_row = np.stack([shifted[:, :, 5 - r:11 - r] for r in range(2)], axis=2)
    by_row = by_row.reshape(DEPTH, NA_HEADS // 2, 2, 2, 6, GRID_W, GRID_W)
    return by_row.transpose(0, 1, 3, 5, 2, 4, 6).reshape(DEPTH, NA_HEADS // 2, P, 2, 6 * GRID_W)


class Step:

    def __init__(self, kind, n, chunks=None, first=None, last=None, units=None, how=None, up_n=None, add_n=None, at=None, b=None, base=None, before=None, bias=None, blocks=None,
                 bn_at=None, br=None, branch=None, c=None, cols=None, dc=None, evac=None, f=None,
                 first_half=None, g=None, gate=None, h=None, half_n=None, hp=None, j=None, job=None, k=None,
                 key_at=None, keys=None, layer=None, live=None, m=None, m_n=None, mixer=None, norm=None,
                 o_use=None, outs=None, part=None, s_use=None, slot=None, sq=None, src=None, t=None,
                 t_use=None, t_uses=None, tile=None, turn=None, u=None, up=None, what=None):
        self.kind, self.n = kind, n
        self.chunks, self.first, self.last, self.units, self.how, self.up_n = chunks, first, last, units, how, up_n
        self.add_n, self.at, self.b, self.base = add_n, at, b, base
        self.before, self.bias, self.blocks, self.bn_at = before, bias, blocks, bn_at
        self.br, self.branch, self.c, self.cols = br, branch, c, cols
        self.dc, self.evac, self.f, self.first_half = dc, evac, f, first_half
        self.g, self.gate, self.h, self.half_n = g, gate, h, half_n
        self.hp, self.j, self.job, self.k = hp, j, job, k
        self.key_at, self.keys, self.layer, self.live = key_at, keys, layer, live
        self.m, self.m_n, self.mixer, self.norm = m, m_n, mixer, norm
        self.o_use, self.outs, self.part, self.s_use = o_use, outs, part, s_use
        self.slot, self.sq, self.src, self.t = slot, sq, src, t
        self.t_use, self.t_uses, self.tile, self.turn = t_use, t_uses, tile, turn
        self.u, self.up, self.what = u, up, what


class Schedule:

    def __init__(self):
        self.steps = []
        self.counts = {}
        self.uses = {}
        self.tile = 0
        self.half = 0
        self.background = []
        self.due = []
        self.section = None
        self.bn = 0

    def count(self, kind):
        n = self.counts.get(kind, 0)
        self.counts[kind] = n + 1
        return n

    def use(self, bank):
        n = self.uses.get(bank, 0)
        self.uses[bank] = n + 1
        return n

    def add(self, kind, **fields):
        step = Step(kind=kind, n=self.count(kind), **fields)
        self.steps.append(step)
        return step

    def split_ahead(self, t):
        if t + AHEAD < NT:
            self.add("split", t=t + AHEAD)

    def fill(self, slots=1):
        for _ in range(slots):
            if self.background:
                self.background.pop(0)()

    def drain(self):
        while self.background:
            self.fill()

    def later(self, parts, add_step):
        self.due.append([parts, add_step])

    def turn_due(self):
        while self.due:
            self.due.pop(0)[1]()

    def part_done(self):
        for entry in self.due:
            entry[0] -= 1
        while self.due and self.due[0][0] <= 0:
            self.due.pop(0)[1]()

    def product(self, what, src, n, blocks=KC, parts=(3, 3, 2), **fields):
        kind = TILES[self.tile][0]
        assert kind == what, (kind, what, self.tile)
        first_half = blocks < KC and self.half == 0
        job = Step(kind="job", n=self.use("G"), tile=self.tile, src=src, cols=n, blocks=blocks, what=what,
                   first_half=first_half, half_n=self.count("half") if first_half else None, **fields)
        base = 0 if blocks == KC else 4 * self.half
        if base == 0:
            self.split_ahead(self.tile)
        at = 0
        for part in (parts if blocks == KC else (2, 2)):
            self.add("product", job=job, at=at, part=part, base=base)
            at += part
            self.part_done()
            self.fill()
        if blocks == KC:
            self.tile += 1
        else:
            self.tile, self.half = self.tile + self.half, 1 - self.half
        return job


def schedule_layer(s, layer, h_norm):
    live = BOTH if layer == 0 else SEQ
    blocks = live // P
    groups = []
    first = {"h": h_norm}

    def src():
        return dict(src="h", norm=first.pop("h", None))

    def proj(what, n):
        return s.product(what, n=n, **src())

    def key(name, g):
        g.k_job = s_add_evac(proj(name, BOTH), "key", g)

    def value(name, g):
        job = proj(name, BOTH)
        g.v_evac = s.add("value_rows", job=job, g=g)

        def turn():
            g.v_turn = s.add("value_turn", evac=g.v_evac, g=g, m=s.use("M"))

        s.later(1, turn)

    def query(name, g):
        g.q_job = s_add_evac(proj(name, live), "query", g)

    def s_add_evac(job, what, g):
        return s.add("evacuate", job=job, what=what, g=g)

    def gate(name, g):
        job = proj(name, live)
        g.gate = s.add("gate", job=job, g=g, cols=live)

    def new_group(branch, c):
        g = Step(kind="group", n=s.count("group"), branch=branch, c=c, layer=layer, live=live, blocks=blocks)
        g.slot = g.n % 2
        groups.append(g)
        return g

    def softmax_units(g):
        units = []
        for hp in range(2):
            for b in range(blocks):
                x = b < 2
                units.append(Step(kind="unit", n=s.count("unit"), g=g, hp=hp, b=b, keys=BOTH if x else SEQ,
                                  key_at=0 if x else SEQ, bias=x and g.branch == "na"))
        for u in units:
            u.bias_n = s.count("biased") if u.bias else None
            u.last = u is units[-1]
        g.units = units
        g.last_unit = units[-1]

        def slot(i):
            def run():
                if i < len(units):
                    u = units[i]
                    u.s_use = s.use("S")
                    s.add("scores", u=u)
                if 0 <= i - 1 < len(units):
                    u = units[i - 1]
                    u.t_use = s.use("T")
                    s.add("turn_probs", u=u)
                if 0 <= i - 2 < len(units):
                    u = units[i - 2]
                    u.o_use = s.use("O")
                    s.add("values", u=u)
            return run

        return [slot(i) for i in range(len(units) + 2)] + [lambda: turn_out(g)]

    def turn_out(g):
        g.out = s.add("turn_out", g=g, m=s.use("M"))

    def retention_units(g):
        def decay():
            g.decay = s.add("decay", g=g)

        def slot(j):
            def run():
                cols = live if j >= 2 else SEQ
                st = s.add("ret_scores", g=g, j=j, cols=cols, s_use=s.use("S"))
                g.last_scores = st
            return run

        def out():
            g.ret_out = s.add("ret_out", g=g, o_use=s.use("O"), bn_at=s.bn)
            s.bn += 2 * blocks + 1

        return [decay] + [slot(j) for j in range(4)] + [out, lambda: None, lambda: turn_out(g)]

    for c in range(4):
        g = new_group("na", c)
        g.bias = s.add("bias", g=g)
        key("nk", g)
        value("nv", g)
        query("nq", g)
        gate("ng", g)
        s.drain()
        s.background = softmax_units(g)

    ada = [(section, k) for section in ADA_BESIDE for k in range(KC)] if layer == 0 else []
    slots = list(ADA_SLOTS)

    def ada_tiles():
        count = slots.pop(0)
        for section, k in ada[:count]:
            ada_tile(s, section, k)
        del ada[:count]

    for h in range(4):
        g = new_group("ret", h)
        key("rk", g)
        ada_tiles()
        value("rv", g)
        ada_tiles()
        query("rq", g)
        ada_tiles()
        gate("rg", g)
        ada_tiles()
        s.drain()
        s.background = retention_units(g)

    merged = {"mg": [None, None]}

    def merge(branch, q, last_out):
        br = ("na", "ret", "gqa").index(branch)
        mg = []
        for dc in (2 * q, 2 * q + 1):
            job = proj("mg", live)
            mg.append(s.add("merge_gate", job=job, slot=dc % 2, before=merged["mg"][dc % 2], cols=live))
        if branch == "gqa":
            s.drain()
        for i, dc in enumerate((2 * q, 2 * q + 1)):
            job = s.product(f"w_{branch}_o", n=live, src=f"o_{branch}", blocks=4, norm=None, parts=None,
                            outs=last_out)
            st = s.add("merge", job=job, dc=dc, br=br, gate=mg[i], cols=live,
                       add_n=s.count("add") if br else None, m_n=s.count("m") if br == 2 else None)
            merged["mg"][dc % 2] = st

    na = [g for g in groups if g.branch == "na"]
    ret = [g for g in groups if g.branch == "ret"]
    for q in range(4):
        merge("na", q, na[-1])
    s.drain()
    kv = new_group("gqa_kv", 0)

    def norm_job(name, g, what, n):
        job = proj(name, n)
        evac = s.add("head_evacuate", job=job, what=what, g=g, cols=n)

        def norm():
            st = s.add("head_norm", job=job, what=what, g=g, cols=n, m=s.use("M"), evac=evac)
            s.later(2, lambda: rotate(st))

        def rotate(st):
            rot = s.add("rotate", norm=st, g=g, what=what, m=s.use("M"))
            if what == "key":
                g.k_rot = rot
            else:
                g.q_rot = rot

        s.later(1, norm)

    norm_job("gk", kv, "key", BOTH)
    value("gv", kv)
    for c in range(4):
        g = new_group("gqa", c)
        g.kv = kv
        norm_job("gq", g, "query", live)
        gate("gg", g)
        for q in {0: [], 1: [0], 2: [1], 3: [2]}[c]:
            merge("ret", q, ret[-1])
        s.drain()
        s.background = softmax_units(g)
        if c == 3:
            merge("ret", 3, ret[-1])
    gqa = [g for g in groups if g.branch == "gqa"]
    for q in range(4):
        merge("gqa", q, gqa[-1])
    s.drain()
    norm = new_norm(s, live if layer == 0 else SEQ)
    for dc in range(KC):
        job = s.product("w_out", n=live, src="m", norm=None)
        up = s.add("gated_residual", job=job, dc=dc, layer=layer, cols=live)
        square(s, norm, dc, 1, up)
    if layer == 0:
        norm.cols = BOTH
    return norm


def ada_tile(s, section, k):
    if k == 0:
        s.section = Step("section", s.count("section"), layer=section[0], c=section[1],
                         t_uses=[s.use("T"), s.use("T")])
    s.split_ahead(s.tile)
    s.add("ada_tile", tile=s.tile, u=s.section, k=k)
    s.tile += 1
    if k == KC - 1:
        done = s.section
        done.tile = s.tile - 1
        s.add("ada_rows", u=done)

        def turn():
            done.m = s.use("M")
            s.add("ada_turn", u=done)

        s.later(2, turn)


def new_norm(s, cols, how=None, weight=None):
    return Step("norm", s.count("norm"), cols=cols, m=s.use("M"), how=how, layer=weight, units=[], chunks=[])


def square(s, norm, k, chunks, up):
    st = s.add("square", norm=norm, k=k, blocks=chunks, up=up, first=not norm.units,
               add_n=s.count("sq_add") if norm.units else None)
    norm.units.append(st)


def follow(s, norm, q, ups):
    if norm.how == "h":
        for k in (2 * q, 2 * q + 1):
            norm.chunks.append(s.add("split_x", norm=norm, k=k, up=ups[k], h=s.count("h")))
    square(s, norm, 2 * q, 2, ups[2 * q + 1])


def normed(s, norm, k):
    split = norm.how == "ada"
    st = s.add("normed", norm=norm, k=k, f=s.count("f") if split or norm.how == "out" else None,
               h=s.count("h") if split else None, t_use=s.use("T") if norm.how == "out" else None)
    norm.chunks.append(st)
    return st


def build_schedule():
    s = Schedule()
    for t in range(AHEAD):
        s.add("split", t=t)
    norm = new_norm(s, BOTH)
    for k in range(KC):
        square(s, norm, k, 1, s.add("turn_in", k=k, t_use=s.use("T")))
    s.add("rms", norm=norm)
    for section in ADA_FIRST:
        for k in range(KC):
            ada_tile(s, section, k)
            if k == 0:
                s.turn_due()
    s.turn_due()
    for layer in range(DEPTH):
        if layer:
            s.add("rms", norm=norm)
        norm.how, norm.layer = "ada", layer
        s.add("ada_scale", layer=layer)
        for k in range(KC):
            normed(s, norm, k)
        norm = schedule_layer(s, layer, norm)
    norm.how, norm.layer = "residual", ("final_norm_w", 0)
    s.add("rms", norm=norm)
    before, norm = norm, new_norm(s, SEQ, "h", ("ffn1_norm", 0))
    for q in range(KC // 2):
        ups = [normed(s, before, k) for k in (2 * q, 2 * q + 1)]
        follow(s, norm, q, [None] * (2 * q) + ups)
    for layer in range(DEPTH):
        norm = schedule_ffn(s, norm, "h", ("mix_norm", layer))
        mixer = schedule_recurrent if layer == 0 else schedule_spatial
        norm = mixer(s, norm, ("ffn2_norm", layer))
        norm = schedule_ffn(s, norm, *((("h", ("ffn1_norm", 1))) if layer == 0 else ("out", ("final_norm", 0))))
    s.add("rms", norm=norm)
    for k in range(KC):
        normed(s, norm, k)
    s.add("store")
    assert s.tile == NT
    return s


def schedule_ffn(s, norm, how, weight):
    ffn = s.add("ffn", t=s.tile, norm=norm, job=s.uses["G"], s_use=s.uses["S"])
    s.tile += 3 * FC
    after = new_norm(s, SEQ, how, weight)
    for q in range(KC // 2):
        up = s.add("ffn_residual", u=ffn, k=q)
        follow(s, after, q, [up] * KC)
    return after


def schedule_recurrent(s, norm, weight):
    for n in range(KC):
        job = s.product("rec_r", n=SEQ, src="h", norm=norm if n == 0 else None)
        if n == 0:
            s.add("rms", norm=norm)
        s.add("conv", job=job, c=n, norm=norm)
        if n >= 1:
            s.add("rec_gates", c=n - 1, s_use=s.use("S"))
    s.add("rec_gates", c=KC - 1, s_use=s.use("S"))
    for n in range(KC):
        job = s.product("rec_y", n=SEQ, src="h", norm=None)
        s.add("rec_y", job=job, c=n)
        if n < 4:
            s.add("rec_decay", c=2 * n)
            s.add("rec_decay", c=2 * n + 1)
        if n == 4:
            for c in range(KC):
                s.add("rec_root", c=c)
        if n >= 4:
            for c in (2 * n - 8, 2 * n - 7):
                s.add("rec_scan", c=c)
        if n >= 5:
            for c in (2 * n - 10, 2 * n - 9):
                s.add("rec_out", c=c)
    for c in (6, 7):
        s.add("rec_out", c=c)
    return mixer_out(s, "rec_o", 0, weight)


def schedule_spatial(s, norm, weight):
    turns = []

    def turn(c):
        turns.append(s.add("sg_turn", c=c, t_use=s.use("T")))

    def mix(c):
        s.add("sg_mix", c=c, turn=turns[c], s_use=s.use("S"))

    vnorm = new_norm(s, SEQ, "v", ("sg_v_norm", 0))
    for n in range(KC):
        job = s.product("sg_v", n=SEQ, src="h", norm=norm if n == 0 else None)
        if n == 0:
            s.add("rms", norm=norm)
        square(s, vnorm, n, 1, s.add("sg_v", job=job, c=n, norm=norm))
        if n == 1:
            s.add("spatial_weights", t_uses=[s.use("T"), s.use("T")])
    for n in range(KC):
        job = s.product("sg_u", n=SEQ, src="h", norm=None)
        if n == 0:
            s.add("rms", norm=vnorm)
        s.add("sg_u", job=job, c=n)
        normed(s, vnorm, n)
        if n >= 1:
            turn(n - 1)
        if n >= 2:
            mix(n - 2)
    turn(KC - 1)
    mix(KC - 2)
    mix(KC - 1)
    return mixer_out(s, "sg_o", 1, weight)


def mixer_out(s, what, mixer, weight):
    norm = new_norm(s, SEQ, "h", weight)
    ups = []
    for n in range(KC):
        job = s.product(what, n=SEQ, src="mix", norm=None, mixer=mixer)
        ups.append(s.add("plain_residual", job=job, dc=n))
        if n % 2:
            follow(s, norm, n // 2, ups)
    return norm


def ffn_tile(which, i):
    if which == "o":
        return 3 * i + 4 if i < FC - 1 else 3 * FC - 1
    return (0 if i == 0 else 3 * i - 1) + (which == "u")


def block_kernel(nc, weights, params, consts, tokens, rpb, gate_a, gate_x, spatial, spatial_b, out):
    schedule = build_schedule()
    steps = schedule.steps
    ctx = ExitStack()
    with ctx:
        def sb(name, shape, dt=F32, stack=None):
            return (stack or ctx).enter_context(nc.sbuf_tensor(name, shape, dt))

        def sem(name):
            return ctx.enter_context(nc.semaphore(name))

        x = sb("x", [P, KC, BOTH])
        raw = sb("raw", [P, RAW, D])
        w_hi = sb("w_hi", [P, SPLIT, D], F32R)
        w_lo = sb("w_lo", [P, SPLIT, D], F32R)
        h_hi = sb("h_hi", [P, KC, BOTH], F32R)
        h_lo = sb("h_lo", [P, KC, BOTH], F32R)
        par = sb("par", [P, NPARAM])
        con = sb("con", [P, NCONST])
        c_silu = sb("c_silu", [P, KC, 2])
        c_split = sb("c_split", [P, KC, 4], F32R)
        ada = sb("ada", [P, DEPTH, 24, 2])
        ada_a = sb("ada_a", [P, KC, 2])
        eps = sb("eps", [P, 1])
        neg_half = sb("neg_half", [P, 1])
        log_g = sb("log_g", [P, 3, 16])
        gn_half = sb("gn_half", [P, 8])
        q_norm = sb("q_norm", [P, 2])
        lam = sb("lam", [P, 3, KC])
        square = sb("square", [P, 2, BOTH])
        rstd = sb("rstd", [P, BOTH])
        scaled = sb("scaled", [P, 2, BOTH])

        def P_(name, width=None):
            at = PARAM_AT[name]
            return par[:, at:at + (width or dict(PARAMS)[name])]

        def C_(name):
            at = CONST_AT[name]
            return con[:, at:at + dict(CONSTS)[name]]

        hybrid = ExitStack()

        def hb(name, shape, dt=F32, stack=None):
            return sb(name, shape, dt, stack or hybrid)

        o_hi = {"a": hb("oa_hi", [P, 4, BOTH], F32R)}
        o_lo = {"a": hb("oa_lo", [P, 4, BOTH], F32R)}
        m = hb("m", [P, KC, BOTH])
        tok = m[:, :, :].rearrange("p a b -> p (a b)").rearrange("p (t d) -> p t d", t=4)
        bias = hb("bias", [P, 2, 2, 6 * GRID_W])
        branch_gate = hb("branch_gate", [P, 2, BOTH])
        out_rows = hb("out_rows", [P, 4, P])
        gated = rstd
        attention = ExitStack()
        o_hi["b"] = hb("ob_hi", [P, 4, BOTH], F32R, attention)
        o_lo["b"] = hb("ob_lo", [P, 4, BOTH], F32R, attention)
        q_s = hb("q_s", [P, 2, BOTH], stack=attention)
        k_s = hb("k_s", [P, 2, BOTH], stack=attention)
        v_s = hb("v_s", [P, 2, 4, P], stack=attention)
        shared = hb("shared", [P, 4 * 3 * P], stack=attention)
        decay_s = shared[:, :].rearrange("p (k c) -> p k c", k=4)
        k_g, v_g = shared[:, 0:BOTH], shared[:, BOTH:2 * BOTH].rearrange("p (t d) -> p t d", t=4)
        stage = hb("stage", [P, BOTH], stack=attention)
        head_rows = k_s
        attention.close()
        m_hi = hb("m_hi", [P, KC, BOTH], F32R, attention)
        m_lo = hb("m_lo", [P, KC, BOTH], F32R, attention)
        attention.close()
        hb("reserved", [P, 8 * BOTH + 6 * BOTH + 12 * P + BOTH])
        half_tanh, head_sq = scaled[:, 0, :], scaled[:, 1, :]
        merge_tanh = hb("merge_tanh", [P, 2, BOTH])
        ada_rows = merge_tanh[0:4, :, :].rearrange("p a b -> p (a b)")
        work = hb("work", [P, 4, BOTH])
        probs, probs_t = work[:, 0:2, :], work[:, 2:4, :]
        abs_dif = hb("abs_dif", [P, 3 * P])
        row_stat = hb("row_stat", [P, 3, 4])
        bn = hb("bn", [P, 4, 6])
        mean_var = hb("mean_var", [P, 4, 2])
        ret_rs = hb("ret_rs", [P, 4])
        hybrid.close()
        branch_sum = square
        sum_sq = scaled[:, 0, :]

        silu_g = sb("silu_g", [P, 2, SEQ])
        hidden = sb("hidden", [P, 2, SEQ])
        hid_hi = sb("hid_hi", [P, 2, SEQ], F32R)
        hid_lo = sb("hid_lo", [P, 2, SEQ], F32R)
        mix_hi = sb("mix_hi", [P, KC, SEQ], F32R)
        mix_lo = sb("mix_lo", [P, KC, SEQ], F32R)
        mix_t = sb("mix_t", [P, 2, SEQ])
        rows_out = sb("rows_out", [P, 2, D])
        mixer = ExitStack()
        r_pad = sb("r_pad", [P, KC, SEQ + 3], stack=mixer)
        r_conv = sb("r_conv", [P, KC, SEQ], stack=mixer)
        g_a = sb("g_a", [P, KC, SEQ], stack=mixer)
        g_x = sb("g_x", [P, KC, SEQ], stack=mixer)
        y_act = sb("y_act", [P, KC, SEQ], stack=mixer)
        th = sb("th", [P, KC, SEQ], stack=mixer)
        gate_w = sb("gate_w", [P, 2, KC, P], stack=mixer)
        mixer.close()
        sg_v = sb("sg_v", [P, KC, SEQ], stack=mixer)
        sg_u = sb("sg_u", [P, KC, SEQ], stack=mixer)
        sg_vt = sb("sg_vt", [P, 2, SEQ], stack=mixer)
        ws = sb("ws", [P, KC, P], stack=mixer)
        ws_t = sb("ws_t", [P, KC, P], stack=mixer)
        ws_b = sb("ws_b", [P, KC, P], stack=mixer)
        mixer.close()

        bank = [ctx.enter_context(nc.psum_tensor(f"bank{i}", [P, 512], F32)) for i in range(8)]
        G, S, T, O, M = bank[0:2], bank[2:4], bank[4:6], bank[6], bank[7]

        raw_landed = [sem(f"raw_landed{i}") for i in range(RAW)]
        hi_ready = sem("hi_ready")
        lo_ready = sem("lo_ready")
        tile_used = sem("tile_used")
        half_used = sem("half_used")
        g_free = [sem("g_free0"), sem("g_free1")]
        s_full, s_free = sem("s_full"), [sem("s_free0"), sem("s_free1")]
        t_full, t_free = sem("t_full"), [sem("t_free0"), sem("t_free1")]
        o_full, o_free = sem("o_full"), sem("o_free")
        m_full, m_free = sem("m_full"), sem("m_free")
        par_landed, con_landed, tok_landed = sem("par_landed"), sem("con_landed"), sem("tok_landed")
        set_up_dve, set_up_act, set_up_pool = sem("set_up_dve"), sem("set_up_act"), sem("set_up_pool")
        squared, sq_added = sem("squared"), sem("sq_added")
        rstd_ready = sem("rstd_ready")
        f_ready, shifted, h_hi_ready, h_lo_ready = sem("f_ready"), sem("shifted"), sem("h_hi_ready"), sem("h_lo_ready")
        renormed, a_ready = sem("renormed"), sem("a_ready")
        bias_landed, bias_ready = [sem("bias_landed0"), sem("bias_landed1")], sem("bias_ready")
        biased, max_ready, sum_ready = sem("biased"), sem("max_ready"), sem("sum_ready")
        th_ready = sem("th_ready")
        head_copied = sem("head_copied")
        decay_exp, decay_ready = sem("decay_exp"), sem("decay_ready")
        decay_cut = sem("decay_cut")
        bn_step, ret_pow = sem("bn_step"), sem("ret_pow")
        o_hi_ready, o_lo_ready = sem("o_hi_ready"), sem("o_lo_ready")
        head_rstd, qk_normed, cos_ready, rot_done = sem("head_rstd"), sem("qk_normed"), sem("cos_ready"), sem("rot_done")
        added = sem("added")
        m_hi_ready, m_lo_ready = sem("m_hi_ready"), sem("m_lo_ready")
        residual_half = sem("residual_half")
        gate_scaled, silu_scaled = sem("gate_scaled"), sem("silu_scaled")
        v_rows, u_ready = sem("v_rows"), sem("u_ready")
        silu_ready, hid_ready, hid_hi_ready, hid_lo_ready = (
            sem("silu_ready"), sem("hid_ready"), sem("hid_hi_ready"), sem("hid_lo_ready"))
        ffn_out = sem("ffn_out")
        ffn_added = sem("ffn_added")
        mix_zero, mix_landed = sem("mix_zero"), sem("mix_landed")
        conv_step, gates_ready, gated_ready = sem("conv_step"), sem("gates_ready"), sem("gated_ready")
        decays, a_squared, root_in, root_out = sem("decays"), sem("a_squared"), sem("root_in"), sem("root_out")
        bx_ready, scanned = sem("bx_ready"), sem("scanned")
        y_ready, mix_ready, mix_hi_ready, mix_lo_ready = sem("y_ready"), sem("mix_ready"), sem("mix_hi_ready"), sem("mix_lo_ready")
        v_ready, v_normed, ws_cut = sem("v_ready"), sem("v_normed"), sem("ws_cut")
        mix_step = sem("mix_step")
        rows_stored = sem("rows_stored")

        def evacuated(job):
            return g_free[job.n % 2], job.n // 2 + 1

        def complete(job):
            return (half_used, job.half_n + 1) if job.first_half else (tile_used, job.tile + 1)

        def s_out(use):
            return s_free[use % 2], use // 2 + 1

        def t_out(use):
            return t_free[use % 2], use // 2 + 1

        def residual_ready(up, k):
            if up.kind == "turn_in":
                return t_out(up.t_use)
            if up.kind in ("gated_residual", "plain_residual"):
                return evacuated(up.job)
            if up.kind == "normed":
                return renormed, k + 1
            if up.kind == "sg_v":
                return v_rows, up.c + 1
            return ffn_added, up.n + 1

        def square_of(st):
            n = st.blocks * st.norm.cols
            return sum_sq[:, 0:n] if st.first else square[:, st.add_n % 2, 0:n]

        def rstd_of(norm):
            return scaled[:, 1, 0:SEQ] if norm.how == "v" else rstd[:, 0:norm.cols]

        def g_buf(g, which):
            if which == "q":
                return q_s[:, g.slot, :]
            if g.branch in ("gqa", "gqa_kv"):
                return k_g[:, :] if which == "k" else v_g[:, :, :]
            return k_s[:, g.slot, :] if which == "k" else v_s[:, g.slot, :, :]

        def o_of(branch):
            return "b" if branch == "ret" else "a"

        def norm_weight(norm, k):
            name, row = norm.layer
            at = PARAM_AT[name] + KC * row + k
            return par[:, at:at + 1]

        def key_blocks(u):
            return range(u.key_at // P, u.key_at // P + u.keys // P)

        Q_SCALE = {"na": DH ** -0.5, "ret": 1.0}
        K_SCALE = {"na": 1.0, "ret": float(np.float32(P) ** np.float32(-0.5))}
        DECAY = 3 * P

        ffn_bank = [M, T[0], T[1], O]
        y_jobs = [st.job for st in steps if st.kind == "rec_y"]
        u_jobs = [st.job for st in steps if st.kind == "sg_u"]

        block = ctx.enter_context(nc.Block())

        @block.sync
        def _(sp):
            sp.dma_start(con[:, :], consts).then_inc(con_landed, 16)
            sp.dma_start(tok[:, 0:2, :], tokens.rearrange("(t p) d -> p t d", p=P)[:, 0:2, :]).then_inc(tok_landed, 16)
            sp.dma_start(tok[:, 2:4, :], tokens.rearrange("(t p) d -> p t d", p=P)[:, 2:4, :]).then_inc(tok_landed, 16)
            for t in range(RAW):
                sp.dma_start(raw[:, t, :], weights[t, :, :]).then_inc(raw_landed[t], 16)
            full = NT // RAW
            with sp.Fori(0, full - 1) as r:
                for i in range(RAW):
                    sp.wait_ge(lo_ready, r * RAW + (i + 1))
                    sp.dma_start(raw[:, i, :], weights[r * RAW + (RAW + i), :, :]).then_inc(raw_landed[i], 16)
            for t in range(full * RAW, NT):
                sp.wait_ge(lo_ready, t - RAW + 1)
                sp.dma_start(raw[:, t % RAW, :], weights[t, :, :]).then_inc(raw_landed[t % RAW], 16)
            t_uses = schedule.uses["T"]
            sp.wait_ge(t_free[0], (t_uses + 1) // 2)
            sp.wait_ge(t_free[1], t_uses // 2)
            sp.dma_start(out.rearrange("(t p) d -> p t d", p=P), rows_out[:, :, :]).then_inc(rows_stored, 16)
            sp.wait_ge(rows_stored, 16)

        @block.gpsimd
        def _(pool):
            pool.memset(eps[:, :], EPS).then_inc(set_up_pool, 1)
            pool.memset(neg_half[:, :], -0.5).then_inc(set_up_pool, 1)
            reader = [None, None]

            def bias_step(st):
                g = st.g
                slot = g.c % 2
                if reader[slot] is not None:
                    pool.wait_ge(biased, reader[slot] + 1)
                pool.dma_start(bias[:, slot, :, :], rpb[g.layer, g.c]).then_inc(bias_landed[slot], 16)
                pool.wait_ge(con_landed, 16)
                pool.wait_ge(bias_landed[slot], 16 * (st.n // 2 + 1))
                b = bias[:, slot, :, :].rearrange("p h (r c) -> p (h r) c", r=6)
                window = C_("window").unsqueeze(1).to_broadcast([P, 12, GRID_W])
                pool.tensor_tensor(b, b, window, ALU.add).then_inc(bias_ready, 1)

            def decay_step(st):
                n = st.n
                pool.wait_ge(decay_exp, 4 * n + 4)
                fwd, bwd, cross, cross_b = (decay_s[:, i, :] for i in range(4))
                pool.affine_select(out=fwd, in_=fwd, compare_op=ALU.is_ge, fill=0.0, base=-P,
                                   pattern=[[1, DECAY]], channel_multiplier=-1).then_inc(decay_cut, 1)
                pool.affine_select(out=bwd, in_=bwd, compare_op=ALU.is_ge, fill=0.0, base=P,
                                   pattern=[[-1, DECAY]], channel_multiplier=1).then_inc(decay_cut, 1)
                pool.tensor_tensor(cross, cross, cross_b, ALU.add).then_inc(decay_ready, 1)
                pool.wait_ge(decay_cut, 2 * n + 2)
                pool.tensor_tensor(fwd, fwd, bwd, ALU.add).then_inc(decay_ready, 1)

            def ret_out_step(st):
                nb = st.g.blocks
                pool.wait_ge(bn_step, st.bn_at + 2 * nb + 1)
                half = neg_half[:, 0:1].to_broadcast([P, nb])
                pool.tensor_tensor(ret_rs[:, 0:nb], ret_rs[:, 0:nb], half, ALU.pow).then_inc(ret_pow, 1)

            def rotate_step(st):
                pool.wait_ge(qk_normed, st.n + 1)
                dst = g_buf(st.g, "k" if st.what == "key" else "q")
                pool.tensor_tensor(head_rows[:, st.n % 2, 0:SEQ], dst[:, 0:SEQ], C_("cos"), ALU.mult).then_inc(cos_ready, 1)

            def merge_step(st):
                if st.br == 0:
                    return
                pool.wait_ge(*evacuated(st.job))
                v = m[:, st.dc, 0:st.cols]
                pool.tensor_tensor(v, v, branch_sum[:, st.dc % 2, 0:st.cols], ALU.add).then_inc(added, 1)

            def spatial_weights_step(st):
                pool.wait_ge(mix_landed, 6 * 16)
                pool.affine_select(out=ws[:, :, :], in_=ws[:, :, :], compare_op=ALU.is_ge, fill=0.0, base=0,
                                   pattern=[[0, KC], [-1, P]], channel_multiplier=1).then_inc(ws_cut, 1)

            def square_step(st):
                if st.first:
                    return
                pool.wait_ge(squared, st.n + 1)
                n = st.blocks * st.norm.cols
                if st.add_n:
                    pool.wait_ge(sq_added, st.add_n)
                pool.tensor_tensor(sum_sq[:, 0:n], sum_sq[:, 0:n], square_of(st), ALU.add).then_inc(sq_added, 1)

            def ffn_step(st):
                mixer_parameters(st)
                f = st.n
                pool.wait_ge(rstd_ready, st.norm.n + 1)

                def scale_silu(i, r=None):
                    cnt = 0 if r is None else r * 2
                    pool.wait_ge(silu_ready, cnt + (FC * f + i + 1))
                    v = silu_g[:, i % 2, :]
                    pool.tensor_tensor(v, v, rstd[:, 0:SEQ], ALU.mult).then_inc(silu_scaled, 1)

                scale_silu(0)
                scale_silu(1)
                with pool.Fori(0, (FC - 2) // 2) as r:
                    scale_silu(2, r)
                    scale_silu(3, r)

            def mixer_parameters(st):
                if st.n % 2:
                    return
                pool.wait_ge(h_lo_ready, st.norm.chunks[KC - 1].h + 1)
                if st.n == 0:
                    pool.memset(gate_w[:, :, :, :], 0.0).then_inc(mix_zero, 1)
                    pool.wait_ge(mix_zero, 1)
                    for i, w in enumerate((gate_a, gate_x)):
                        halves = w.rearrange("(n two) i j -> two i n j", two=2)
                        for j in range(2):
                            at = slice(DH * j, DH * j + DH)
                            pool.dma_start(gate_w[at, i, :, at], halves[j]).then_inc(mix_landed, 16)
                else:
                    pool.dma_start(ws[:, :, :], spatial.rearrange("h p q -> p h q")).then_inc(mix_landed, 16)
                    rows = spatial_b.rearrange("h p -> (h p)").partition_broadcast(P)
                    pool.dma_start(ws_b[:, :, :].rearrange("p h q -> p (h q)"), rows).then_inc(mix_landed, 16)

            def rec_gates_step(st):
                pool.wait_ge(*s_out(st.s_use))
                v = g_x[:, st.c, :]
                pool.tensor_tensor(v, v, r_conv[:, st.c, :], ALU.mult).then_inc(gated_ready, 1)

            def rec_root_step(st):
                pool.wait_ge(root_out, st.n + 1)
                pool.wait_ge(gated_ready, st.n + 1)
                v = g_x[:, st.c, :]
                pool.tensor_tensor(v, v, th[:, st.c, :], ALU.mult).then_inc(bx_ready, 1)

            run = {"square": square_step, "bias": bias_step, "decay": decay_step, "ret_out": ret_out_step, 
                   "rotate": rotate_step, "merge": merge_step, "spatial_weights": spatial_weights_step,
                   "ffn": ffn_step, "rec_gates": rec_gates_step, "rec_root": rec_root_step}
            for st in steps:
                if st.kind == "scores" and st.u.bias:
                    reader[st.u.g.c % 2] = st.u.bias_n
                if st.kind in run:
                    run[st.kind](st)

        @block.scalar
        def _(act):
            act.dma_start(par[:, :], params).then_inc(par_landed, 16)
            act.wait_ge(par_landed, 16)
            nc.scalar.activation(c_silu[:, :, 0], P_("c"), ACT.Silu).then_inc(set_up_act, 1)
            nc.scalar.activation(c_silu[:, :, 1], P_("c_ctx"), ACT.Silu).then_inc(set_up_act, 1)
            act.wait_ge(set_up_act, 2)
            nc.scalar.activation(c_split[:, :, 0:2], c_silu[:, :, :], ACT.Copy).then_inc(set_up_act, 1)
            nc.scalar.activation(log_g[:, 0, :], P_("decay"), ACT.Exp).then_inc(set_up_act, 1)
            nc.scalar.activation(lam[:, 0, :], P_("rec_lambda"), ACT.Abs).then_inc(set_up_act, 1)
            act.wait_ge(set_up_act, 5)
            nc.scalar.activation(lam[:, 1, :], lam[:, 0, :], ACT.Exp, scale=-1.0).then_inc(set_up_act, 1)
            act.wait_ge(set_up_act, 6)
            act.wait_ge(set_up_dve, 1)
            nc.scalar.activation(lam[:, 0, :], lam[:, 1, :], ACT.Ln, bias=lam[:, 2, 0:1]).then_inc(set_up_act, 1)
            act.wait_ge(con_landed, 16)
            nc.scalar.activation(abs_dif[:, :], C_("dif"), ACT.Abs).then_inc(set_up_act, 1)
            act.wait_ge(set_up_pool, 1)
            last = {"gate": None, "decay": None}

            def split_step(st):
                split(st.t, None)

            def ada_rows_step(st):
                u = st.u
                if u.n:
                    act.wait_ge(m_full, last["section"].m + 1)
                last["section"] = u
                for j, use in enumerate(u.t_uses):
                    if j == 0:
                        act.wait_ge(t_full, use + 1)
                    else:
                        act.wait_ge(tile_used, u.tile + 1)
                    nc.scalar.activation(ada_rows[:, 512 * j:512 * j + 512], T[use % 2][0:4, :], ACT.Copy)\
                        .then_inc(t_free[use % 2], 1)

            def split(t, r, t_static=None):
                base = 0 if r is None else r * RAW
                act.wait_ge(raw_landed[t % RAW], 16 * (t // RAW + 1) if r is None else r * 16 + 16 * (t // RAW + 1))
                if t >= SPLIT:
                    act.wait_ge(tile_used, base + (t - SPLIT + 1))
                nc.scalar.activation(w_hi[:, t % SPLIT, :], raw[:, t % RAW, :], ACT.Copy).then_inc(hi_ready, 1)

            def turn_in_step(st):
                if st.k % 2:
                    return
                act.wait_ge(t_full, st.t_use + 1)
                nc.scalar.activation(x[:, st.k, :], T[st.t_use % 2][:, :], ACT.Copy).then_inc(t_free[st.t_use % 2], 1)

            def square_step(st):
                act.wait_ge(*residual_ready(st.up, st.k))
                if st.add_n is not None and st.add_n >= 2:
                    act.wait_ge(sq_added, st.add_n - 1)
                c, n = st.norm.cols, st.blocks
                src = sg_v[:, st.k:st.k + n, :] if st.norm.how == "v" else x[:, st.k:st.k + n, 0:c]
                nc.scalar.activation(square_of(st).rearrange("p (a b) -> p a b", a=n), src, ACT.Square)\
                    .then_inc(squared, 1)

            def rms_step(st):
                norm = st.norm
                act.wait_ge(m_full, norm.m + 1)
                nc.scalar.activation(rstd_of(norm), M[:, 0:norm.cols], ACT.Sqrt, bias=eps[:, 0:1]).then_inc(m_free, 1)

            def split_x_step(st):
                act.wait_ge(*residual_ready(st.up, st.k))
                nc.scalar.activation(h_hi[:, st.k, 0:SEQ], x[:, st.k, 0:SEQ], ACT.Copy, scale=norm_weight(st.norm, st.k))\
                    .then_inc(h_hi_ready, 1)

            def normed_step(st):
                norm, k = st.norm, st.k
                if norm.how != "ada":
                    return
                act.wait_ge(f_ready, st.f + 1)
                for j in range(2):
                    v = scaled[:, k % 2, SEQ * j:SEQ * j + SEQ]
                    nc.scalar.activation(v, v, ACT.Identity, bias=ada[:, norm.layer, k, j:j + 1]).then_inc(shifted, 1)
                act.wait_ge(shifted, 2 * (KC * norm.layer + k + 1))
                nc.scalar.activation(h_hi[:, k, 0:norm.cols], scaled[:, k % 2, 0:norm.cols], ACT.Copy)\
                    .then_inc(h_hi_ready, 1)

            def evacuate_step(st):
                g, n = st.g, st.job.cols
                act.wait_ge(*complete(st.job))
                dst = g_buf(g, "q" if st.what == "query" else "k")
                scale = (Q_SCALE if st.what == "query" else K_SCALE)[g.branch]
                nc.scalar.activation(dst[:, 0:n], G[st.job.n % 2][:, 0:n], ACT.Copy, scale=scale)\
                    .then_inc(g_free[st.job.n % 2], 1)

            def value_rows_step(st):
                act.wait_ge(*complete(st.job))
                nc.scalar.activation(stage[:, :], G[st.job.n % 2][:, :], ACT.Copy).then_inc(g_free[st.job.n % 2], 1)

            def gate_step(st):
                act.wait_ge(*complete(st.job))
                if last["gate"] is not None:
                    act.wait_ge(*evacuated(last["gate"].job))
                last["gate"] = st
                nc.scalar.activation(half_tanh[:, 0:st.cols], G[st.job.n % 2][:, 0:st.cols], ACT.Tanh, scale=0.5)\
                    .then_inc(th_ready, 1)

            def merge_gate_step(st):
                act.wait_ge(*complete(st.job))
                if st.before is not None:
                    act.wait_ge(*evacuated(st.before.job))
                nc.scalar.activation(merge_tanh[:, st.slot, 0:st.cols], G[st.job.n % 2][:, 0:st.cols], ACT.Tanh,
                                     scale=0.5).then_inc(g_free[st.job.n % 2], 1)

            def merge_step(st):
                if st.br < 2:
                    return
                act.wait_ge(added, st.add_n + 1)
                nc.scalar.activation(m_hi[:, st.dc, 0:st.cols], m[:, st.dc, 0:st.cols], ACT.Copy, scale=0.5)\
                    .then_inc(m_hi_ready, 1)

            def scores_step(st):
                u = st.u
                act.wait_ge(max_ready, u.n + 1)
                nc.scalar.activation(probs[:, u.n % 2, 0:u.keys], S[u.s_use % 2][:, 0:u.keys], ACT.Exp,
                                     bias=row_stat[:, 0, u.n % 4:u.n % 4 + 1],
                                     accum_out=row_stat[:, 1, u.n % 4:u.n % 4 + 1]).then_inc(s_free[u.s_use % 2], 1)

            def turn_probs_step(st):
                u = st.u
                act.wait_ge(t_full, u.t_use + 1)
                nc.scalar.activation(probs_t[:, u.n % 2, 0:u.keys], T[u.t_use % 2][:, 0:u.keys], ACT.Copy)\
                    .then_inc(t_free[u.t_use % 2], 1)

            def turn_out_step(st):
                g = st.g
                act.wait_ge(m_free, st.m + 1)
                nc.scalar.activation(o_hi[o_of(g.branch)][:, g.c, 0:g.live], gated[:, 0:g.live], ACT.Copy)\
                    .then_inc(o_hi_ready, 1)

            def decay_step(st):
                g = st.g
                if last["decay"] is not None:
                    act.wait_ge(*s_out(last["decay"].last_scores.s_use))
                last["decay"] = g
                f, b = g.layer * 8 + g.c, g.layer * 8 + 4 + g.c
                act.wait_ge(set_up_dve, 5)
                act.wait_ge(set_up_act, 8)
                lg = lambda kind, i: log_g[:, kind, i:i + 1]
                nc.scalar.activation(decay_s[:, 0, :], abs_dif[:, :], ACT.Exp, scale=lg(0, f)).then_inc(decay_exp, 1)
                nc.scalar.activation(decay_s[:, 1, :], abs_dif[:, :], ACT.Exp, scale=lg(0, b)).then_inc(decay_exp, 1)
                nc.scalar.activation(decay_s[:, 2, :], C_("dif"), ACT.Exp, scale=lg(0, f), bias=lg(2, f))\
                    .then_inc(decay_exp, 1)
                nc.scalar.activation(decay_s[:, 3, :], C_("dif"), ACT.Exp, scale=lg(1, b), bias=lg(2, b))\
                    .then_inc(decay_exp, 1)

            def head_evacuate_step(st):
                n = st.cols
                act.wait_ge(*complete(st.job))
                if st.n >= 1:
                    act.wait_ge(rot_done, st.n)
                nc.scalar.activation(head_rows[:, st.n % 2, 0:n], G[st.job.n % 2][:, 0:n], ACT.Copy)\
                    .then_inc(head_copied, 1)
                nc.scalar.activation(head_sq[:, 0:n], G[st.job.n % 2][:, 0:n], ACT.Square)\
                    .then_inc(g_free[st.job.n % 2], 1)

            def head_norm_step(st):
                n = st.cols
                act.wait_ge(m_full, st.m + 1)
                nc.scalar.activation(head_sq[:, 0:n], M[:, 0:n], ACT.Sqrt, bias=eps[:, 0:1]).then_inc(m_free, 1)

            def ffn_step(st):
                f, t0 = st.n, st.t

                def silu(i, r=None):
                    cnt = 0 if r is None else r * 2
                    act.wait_ge(gate_scaled, cnt + (FC * f + i + 1))
                    nc.scalar.activation(silu_g[:, i % 2, :], silu_g[:, i % 2, :], ACT.Silu).then_inc(silu_ready, 1)

                def hid(i, r=None):
                    cnt = 0 if r is None else r * 2
                    act.wait_ge(hid_ready, cnt + (FC * f + i + 1))
                    nc.scalar.activation(hid_hi[:, i % 2, :], hidden[:, i % 2, :], ACT.Copy).then_inc(hid_hi_ready, 1)

                def round_(i, r=None):
                    a = t0 + 2 + 3 * i
                    split(a + 2, r)
                    hid(i, r)
                    split(a + 3, r)
                    silu(i + 1, r)
                    if r is not None or a + 4 < NT:
                        split(a + 4, r)

                split(t0 + 2, None)
                rms_step(st)
                split(t0 + 3, None)
                silu(0)
                round_(0)
                peeled = 2 if t0 + 3 * FC == NT else 0
                with act.Fori(0, (FC - 2 - peeled) // 2) as r:
                    round_(1, r)
                    round_(2, r)
                for i in range(FC - 1 - peeled, FC - 1):
                    round_(i)
                if t0 + 3 * FC - 1 + AHEAD < NT:
                    split(t0 + 3 * FC - 1 + AHEAD, None)
                hid(FC - 1)

            def rec_gates_step(st):
                act.wait_ge(s_full, st.s_use + 1)
                b = S[st.s_use % 2]
                at_a, at_x = PARAM_AT["rec_gate_a_b"] + st.c, PARAM_AT["rec_gate_x_b"] + st.c
                nc.scalar.activation(g_a[:, st.c, :], b[:, 0:SEQ], ACT.Sigmoid, bias=par[:, at_a:at_a + 1])\
                    .then_inc(gates_ready, 1)
                nc.scalar.activation(g_x[:, st.c, :], b[:, SEQ:BOTH], ACT.Sigmoid, bias=par[:, at_x:at_x + 1])\
                    .then_inc(s_free[st.s_use % 2], 1)

            def rec_decay_step(st):
                act.wait_ge(gates_ready, st.c + 1)
                act.wait_ge(set_up_dve, 10)
                scale = lam[:, 0, st.c:st.c + 1]
                nc.scalar.activation(th[:, st.c, :], g_a[:, st.c, :], ACT.Tanh, scale=scale).then_inc(decays, 1)
                act.wait_ge(decays, 2 * st.c + 1)
                nc.scalar.activation(g_a[:, st.c, :], g_a[:, st.c, :], ACT.Exp, scale=scale).then_inc(decays, 1)
                act.wait_ge(decays, 2 * st.c + 2)
                if st.c >= 2:
                    act.wait_ge(root_in, st.c - 1)
                nc.scalar.activation(mix_t[:, st.c % 2, :], g_a[:, st.c, :], ACT.Square).then_inc(a_squared, 1)

            def rec_root_step(st):
                act.wait_ge(root_in, st.n + 1)
                nc.scalar.activation(th[:, st.c, :], th[:, st.c, :], ACT.Sqrt, scale=-1.0).then_inc(root_out, 1)

            def rec_out_step(st):
                act.wait_ge(*evacuated(y_jobs[st.c]))
                nc.scalar.activation(y_act[:, st.c, :], y_act[:, st.c, :], ACT.Gelu_apprx_tanh).then_inc(y_ready, 1)
                mix_split(st.c, st.n)

            def mix_split(c, n):
                act.wait_ge(mix_ready, n + 1)
                nc.scalar.activation(mix_hi[:, c, :], mix_t[:, n % 2, :], ACT.Copy).then_inc(mix_hi_ready, 1)

            def sg_v_step(st):
                act.wait_ge(*evacuated(st.job))
                v = sg_v[:, st.c, :]
                nc.scalar.activation(v, v, ACT.Gelu_apprx_tanh).then_inc(v_rows, 1)

            def sg_u_step(st):
                act.wait_ge(*evacuated(st.job))
                v = sg_u[:, st.c, :]
                nc.scalar.activation(v, v, ACT.Gelu_apprx_tanh).then_inc(u_ready, 1)

            def sg_turn_step(st):
                act.wait_ge(t_full, st.t_use + 1)
                nc.scalar.activation(sg_vt[:, st.c % 2, :], T[st.t_use % 2][:, 0:SEQ], ACT.Copy)\
                    .then_inc(t_free[st.t_use % 2], 1)

            def sg_mix_step(st):
                mix_split(st.c, KC + st.n)

            run = {"split": split_step, "ada_rows": ada_rows_step, "turn_in": turn_in_step, "square": square_step, "rms": rms_step,
                   "normed": normed_step, "evacuate": evacuate_step, "value_rows": value_rows_step,
                   "gate": gate_step, "merge_gate": merge_gate_step, "merge": merge_step, "scores": scores_step,
                   "turn_probs": turn_probs_step, "turn_out": turn_out_step, "decay": decay_step,
                   "head_evacuate": head_evacuate_step, "head_norm": head_norm_step, "ffn": ffn_step,
                   "rec_gates": rec_gates_step, "split_x": split_x_step, "rec_decay": rec_decay_step, "rec_root": rec_root_step,
                   "rec_out": rec_out_step, "sg_v": sg_v_step, "sg_u": sg_u_step, "sg_turn": sg_turn_step,
                   "sg_mix": sg_mix_step}
            for st in steps:
                if st.kind in run:
                    run[st.kind](st)

        @block.vector
        def _(dve):
            dve.memset(lam[:, 2, 0:1], 1.0).then_inc(set_up_dve, 1)
            dve.wait_ge(set_up_act, 4)
            dve.tensor_tensor(c_split[:, :, 2:4], c_silu[:, :, :], c_split[:, :, 0:2].bitcast(F32), ALU.subtract)\
                .then_inc(set_up_dve, 1)
            dve.tensor_scalar(log_g[:, 1, :], log_g[:, 0, :], 1.0, None, ALU.mult).then_inc(set_up_dve, 1)
            dve.tensor_scalar(log_g[:, 2, :], log_g[:, 0, :], -256.0, None, ALU.mult).then_inc(set_up_dve, 1)
            dve.wait_ge(set_up_dve, 4)
            dve.tensor_scalar(log_g[:, 0, :], log_g[:, 0, :], -1.0, None, ALU.mult).then_inc(set_up_dve, 1)
            dve.tensor_scalar(gn_half[:, :], P_("ret_gn_w"), 0.5, None, ALU.mult).then_inc(set_up_dve, 1)
            dve.tensor_scalar(q_norm[:, :], P_("q_norm_w"), DH ** -0.5, None, ALU.mult).then_inc(set_up_dve, 1)
            dve.wait_ge(set_up_act, 7)
            dve.tensor_scalar(lam[:, 1, :], P_("rec_lambda"), -1.0, 0.0, ALU.mult, ALU.max).then_inc(set_up_dve, 1)
            dve.wait_ge(set_up_dve, 8)
            dve.tensor_tensor(lam[:, 1, :], lam[:, 1, :], lam[:, 0, :], ALU.add).then_inc(set_up_dve, 1)
            dve.wait_ge(set_up_dve, 9)
            dve.tensor_scalar(lam[:, 0, :], lam[:, 1, :], -8.0, None, ALU.mult).then_inc(set_up_dve, 1)

            def split(t, r=None):
                base = 0 if r is None else r * RAW
                dve.wait_ge(hi_ready, base + (t + 1))
                dve.tensor_tensor(w_lo[:, t % SPLIT, :], raw[:, t % RAW, :], w_hi[:, t % SPLIT, :].bitcast(F32),
                                  ALU.subtract).then_inc(lo_ready, 1)

            def turn_in_step(st):
                if st.k % 2 == 0:
                    return
                dve.wait_ge(t_full, st.t_use + 1)
                dve.tensor_copy(x[:, st.k, :], T[st.t_use % 2][:, :]).then_inc(t_free[st.t_use % 2], 1)

            def ada_turn_step(st):
                u = st.u
                at = PARAM_AT["ada_b"] + 24 * u.layer + KC * u.c
                dve.wait_ge(m_full, u.m + 1)
                dve.wait_ge(par_landed, 16)
                b = par[:, at:at + KC].unsqueeze(2).to_broadcast([P, KC, 2])
                dve.tensor_tensor(ada[:, u.layer, KC * u.c:KC * u.c + KC, :],
                                  M[:, 0:2 * KC].rearrange("p (k j) -> p k j", j=2), b, ALU.add).then_inc(m_free, 1)
                if u.c == 1:
                    ada_m[u.layer] = u.m + 1

            ada_m = [0, 0]

            def ada_scale_step(st):
                at = PARAM_AT["norm_w"] + KC * st.layer
                dve.wait_ge(m_free, ada_m[st.layer])
                for j in range(2):
                    dve.scalar_tensor_tensor(out=ada_a[:, :, j], in0=ada[:, st.layer, KC:2 * KC, j], scalar=1.0,
                                             in1=par[:, at:at + KC], op0=ALU.add, op1=ALU.mult).then_inc(a_ready, 1)

            def rms_step(st):
                norm = st.norm
                dve.wait_ge(m_free, norm.m + 1)
                dve.reciprocal(rstd_of(norm), rstd_of(norm)).then_inc(rstd_ready, 1)

            def split_x_step(st):
                k = st.k
                dve.wait_ge(*residual_ready(st.up, k))
                dve.wait_ge(h_hi_ready, st.h + 1)
                dve.scalar_tensor_tensor(out=h_lo[:, k, 0:SEQ], in0=x[:, k, 0:SEQ], scalar=norm_weight(st.norm, k),
                                         in1=h_hi[:, k, 0:SEQ].bitcast(F32), op0=ALU.mult, op1=ALU.subtract)\
                    .then_inc(h_lo_ready, 1)

            def scaled_product(st, dst, norm=None):
                if norm is not None:
                    dve.wait_ge(rstd_ready, norm.n + 1)
                dve.wait_ge(*complete(st.job))
                dve.tensor_tensor(dst, G[st.job.n % 2][:, 0:SEQ], rstd[:, 0:SEQ], ALU.mult)\
                    .then_inc(g_free[st.job.n % 2], 1)

            def rec_y_step(st):
                scaled_product(st, y_act[:, st.c, :])

            def sg_v_step(st):
                scaled_product(st, sg_v[:, st.c, :], st.norm)

            def sg_u_step(st):
                scaled_product(st, sg_u[:, st.c, :])

            def normed_step(st):
                norm, k, c = st.norm, st.k, st.norm.cols
                if k == 0:
                    dve.wait_ge(rstd_ready, norm.n + 1)
                if st.h is not None and k >= 2:
                    dve.wait_ge(h_lo_ready, st.h - 1)
                if norm.how == "ada":
                    if k == 0:
                        dve.wait_ge(a_ready, 2 * norm.layer + 2)
                    for j in range(2):
                        at = slice(SEQ * j, SEQ * j + SEQ)
                        ins = dve.scalar_tensor_tensor(out=scaled[:, k % 2, at], in0=x[:, k, at],
                                                       scalar=ada_a[:, k, j:j + 1], in1=rstd[:, at],
                                                       op0=ALU.mult, op1=ALU.mult)
                    ins.then_inc(f_ready, 1)
                elif norm.how == "out":
                    if k >= 2:
                        dve.wait_ge(t_full, st.t_use - 1)
                    dve.scalar_tensor_tensor(out=scaled[:, k % 2, 0:c], in0=x[:, k, 0:c], scalar=norm_weight(norm, k),
                                             in1=rstd[:, 0:c], op0=ALU.mult, op1=ALU.mult).then_inc(f_ready, 1)
                    dve.wait_ge(t_full, st.t_use + 1)
                    dve.tensor_copy(rows_out[:, :, P * k:P * k + P],
                                    T[st.t_use % 2][:, 0:SEQ].rearrange("p (t d) -> p t d", t=2))\
                        .then_inc(t_free[st.t_use % 2], 1)
                    return
                elif norm.how == "residual":
                    dve.scalar_tensor_tensor(out=x[:, k, 0:SEQ], in0=x[:, k, 0:SEQ], scalar=norm_weight(norm, k),
                                             in1=rstd[:, 0:SEQ], op0=ALU.mult, op1=ALU.mult).then_inc(renormed, 1)
                    return
                else:
                    dve.scalar_tensor_tensor(out=sg_v[:, k, :], in0=sg_v[:, k, :], scalar=norm_weight(norm, k),
                                             in1=rstd_of(norm), op0=ALU.mult, op1=ALU.mult).then_inc(v_normed, 1)
                    return

                if k >= 1:
                    h_low(norm.chunks[k - 1], c)
                if k == KC - 1:
                    h_low(st, c)

            def h_low(st, c):
                dve.wait_ge(h_hi_ready, st.h + 1)
                dve.tensor_tensor(h_lo[:, st.k, 0:c], scaled[:, st.k % 2, 0:c], h_hi[:, st.k, 0:c].bitcast(F32),
                                  ALU.subtract).then_inc(h_lo_ready, 1)

            def value_turn_step(st):
                dve.wait_ge(m_full, st.m + 1)
                dve.tensor_copy(g_buf(st.g, "v"), M[:, :].rearrange("p (t d) -> p t d", t=4)).then_inc(m_free, 1)

            def gate_step(st):
                th_count[0] += 1
                dve.wait_ge(th_ready, th_count[0])
                if turned[st.g.slot]:
                    dve.wait_ge(m_free, turned[st.g.slot])
                dve.scalar_tensor_tensor(out=branch_gate[:, st.g.slot, 0:st.cols], in0=half_tanh[:, 0:st.cols],
                                         scalar=1.0, in1=G[st.job.n % 2][:, 0:st.cols], op0=ALU.add, op1=ALU.mult)\
                    .then_inc(g_free[st.job.n % 2], 1)

            th_count = [0]
            turned = [0, 0]

            def merge_step(st):
                c = st.cols
                dve.wait_ge(*complete(st.job))
                dve.wait_ge(*evacuated(st.gate.job))
                if st.br and st.add_n >= 2:
                    dve.wait_ge(added, st.add_n - 1)
                dst = m[:, st.dc, 0:c] if st.br == 0 else branch_sum[:, st.dc % 2, 0:c]
                dve.scalar_tensor_tensor(out=dst, in0=merge_tanh[:, st.dc % 2, 0:c], scalar=1.0,
                                         in1=G[st.job.n % 2][:, 0:c], op0=ALU.add, op1=ALU.mult)\
                    .then_inc(g_free[st.job.n % 2], 1)
                if st.br == 2:
                    dve.wait_ge(m_hi_ready, st.m_n + 1)
                    dve.scalar_tensor_tensor(out=m_lo[:, st.dc, 0:c], in0=m[:, st.dc, 0:c], scalar=0.5,
                                             in1=m_hi[:, st.dc, 0:c].bitcast(F32), op0=ALU.mult,
                                             op1=ALU.subtract).then_inc(m_lo_ready, 1)

            def gated_residual_step(st):
                dve.wait_ge(*complete(st.job))
                halves = range(2 if st.cols == BOTH else 1)
                for j in halves:
                    at = slice(SEQ * j, SEQ * j + SEQ)
                    v = x[:, st.dc, at]
                    ins = dve.scalar_tensor_tensor(out=v, in0=G[st.job.n % 2][:, at],
                                                   scalar=ada[:, st.layer, 16 + st.dc, j:j + 1], in1=v,
                                                   op0=ALU.mult, op1=ALU.add)
                ins.then_inc(g_free[st.job.n % 2], 1)

            def plain_residual_step(st):
                dve.wait_ge(*complete(st.job))
                v = x[:, st.dc, 0:SEQ]
                dve.tensor_tensor(v, G[st.job.n % 2][:, 0:SEQ], v, ALU.add).then_inc(g_free[st.job.n % 2], 1)

            def scores_step(st):
                u = st.u
                s = S[u.s_use % 2]
                dve.wait_ge(s_full, u.s_use + 1)
                if u.bias:
                    dve.wait_ge(bias_ready, u.g.bias.n + 1)
                    row = (2 - 2 * u.b) * GRID_W
                    dve.tensor_tensor(s[:, 0:SEQ], s[:, 0:SEQ], bias[:, u.g.c % 2, u.hp, row:row + SEQ], ALU.add)\
                        .then_inc(biased, 1)
                    dve.wait_ge(biased, u.bias_n + 1)
                dve.tensor_reduce(row_stat[:, 0, u.n % 4:u.n % 4 + 1], s[:, 0:u.keys], AX_X, ALU.max, negate=True)\
                    .then_inc(max_ready, 1)

            def turn_probs_step(st):
                u = st.u
                dve.wait_ge(*s_out(u.s_use))
                dve.reciprocal(row_stat[:, 2, u.n % 4:u.n % 4 + 1], row_stat[:, 1, u.n % 4:u.n % 4 + 1])\
                    .then_inc(sum_ready, 1)

            def values_step(st):
                u = st.u
                dve.wait_ge(o_full, u.o_use + 1)
                dve.wait_ge(sum_ready, u.n + 1)
                dve.tensor_scalar(out_rows[:, u.b, DH * u.hp:DH * u.hp + DH], O[:, 0:DH],
                                  row_stat[:, 2, u.n % 4:u.n % 4 + 1], None, ALU.mult).then_inc(o_free, 1)

            def turn_out_step(st):
                g = st.g
                dve.wait_ge(m_full, st.m + 1)
                dve.wait_ge(*evacuated(g.gate.job))
                if st.n:
                    dve.wait_ge(o_lo_ready, st.n)
                turned[g.slot] = st.m + 1
                scale = gn_half[:, 4 * g.layer + g.c:4 * g.layer + g.c + 1] if g.branch == "ret" else 0.5
                dve.scalar_tensor_tensor(out=gated[:, 0:g.live], in0=M[:, 0:g.live], scalar=scale,
                                         in1=branch_gate[:, g.slot, 0:g.live], op0=ALU.mult, op1=ALU.mult)\
                    .then_inc(m_free, 1)
                o = o_of(g.branch)
                dve.wait_ge(o_hi_ready, st.n + 1)
                dve.tensor_tensor(o_lo[o][:, g.c, 0:g.live], gated[:, 0:g.live],
                                  o_hi[o][:, g.c, 0:g.live].bitcast(F32), ALU.subtract).then_inc(o_lo_ready, 1)

            def ret_scores_step(st):
                g, s = st.g, S[st.s_use % 2]
                dve.wait_ge(s_full, st.s_use + 1)
                dve.wait_ge(decay_ready, 2 * g.decay.n + 2)
                at = P * (1 - st.j % 2)
                own, cross = decay_s[:, 0, at:at + SEQ], decay_s[:, 2, at:at + SEQ]
                ins = dve.tensor_tensor(work[:, st.j, 0:SEQ], s[:, 0:SEQ], own if st.j < 2 else cross, ALU.mult)
                if st.cols == BOTH:
                    ins = dve.tensor_tensor(work[:, st.j, SEQ:BOTH], s[:, SEQ:BOTH], own, ALU.mult)
                ins.then_inc(s_free[st.s_use % 2], 1)

            def ret_out_step(st):
                nb = st.g.blocks
                dve.wait_ge(o_full, st.o_use + 1)
                for b in range(nb):
                    dve.bn_stats(bn[:, b, :], O[:, P * b:P * b + P]).then_inc(bn_step, 1)
                for b in range(nb):
                    dve.wait_ge(bn_step, st.bn_at + b + 1)
                    dve.bn_aggr(mean_var[:, b, :], bn[:, b, :]).then_inc(bn_step, 1)
                dve.wait_ge(bn_step, st.bn_at + 2 * nb)
                dve.tensor_scalar(ret_rs[:, 0:nb], mean_var[:, 0:nb, 1], EPS, None, ALU.add).then_inc(bn_step, 1)
                dve.wait_ge(ret_pow, st.n + 1)
                for b in range(nb):
                    ins = dve.tensor_scalar(out_rows[:, b, :], O[:, P * b:P * b + P],
                                            mean_var[:, b, 0:1], ret_rs[:, b:b + 1], ALU.subtract, ALU.mult)
                ins.then_inc(o_free, 1)

            def head_norm_step(st):
                n = st.cols
                dve.wait_ge(m_free, st.m + 1)
                dve.reciprocal(head_sq[:, 0:n], head_sq[:, 0:n]).then_inc(head_rstd, 1)

            def rotate_step(st):
                n, norm = st.norm.cols, st.norm
                dst = g_buf(st.g, "k" if st.what == "key" else "q")
                at = PARAM_AT["k_norm_w"] + st.g.layer
                w = par[:, at:at + 1] if st.what == "key" else q_norm[:, st.g.layer:st.g.layer + 1]
                dve.wait_ge(head_rstd, norm.n + 1)
                dve.wait_ge(head_copied, norm.n + 1)
                dve.scalar_tensor_tensor(out=dst[:, 0:n], in0=head_rows[:, norm.n % 2, 0:n], scalar=w, in1=head_sq[:, 0:n],
                                         op0=ALU.mult, op1=ALU.mult).then_inc(qk_normed, 1)
                dve.wait_ge(m_full, st.m + 1)
                dve.tensor_tensor(head_sq[:, 0:SEQ], M[:, 0:SEQ], C_("sin"), ALU.mult).then_inc(m_free, 1)
                dve.wait_ge(cos_ready, st.n + 1)
                dve.wait_ge(m_free, st.m + 1)
                dve.tensor_tensor(dst[:, 0:SEQ], head_rows[:, st.n % 2, 0:SEQ], head_sq[:, 0:SEQ], ALU.add).then_inc(rot_done, 1)

            def ffn_step(st):
                f, t0 = st.n, st.t

                def gate(i, r=None):
                    cnt, up = (0, 0) if r is None else (r * 2, r * 6)
                    dve.wait_ge(tile_used, up + (t0 + ffn_tile("g", i) + 1))
                    if i >= 2:
                        dve.wait_ge(hid_ready, cnt + (FC * f + i - 1))
                    dve.tensor_tensor(silu_g[:, i % 2, :], G[i % 2][:, 0:SEQ], rstd[:, 0:SEQ], ALU.mult)\
                        .then_inc(gate_scaled, 1)

                def mult(i, r=None):
                    cnt, up = (0, 0) if r is None else (r * 2, r * 6)
                    dve.wait_ge(silu_scaled, cnt + (FC * f + i + 1))
                    dve.wait_ge(tile_used, up + (t0 + ffn_tile("u", i) + 1))
                    if i >= 2:
                        dve.wait_ge(hid_lo_ready, cnt + (FC * f + i - 1))
                    dve.tensor_tensor(hidden[:, i % 2, :], silu_g[:, i % 2, :], S[i % 2][:, 0:SEQ], ALU.mult)\
                        .then_inc(hid_ready, 1)

                def low(i, r=None):
                    cnt = 0 if r is None else r * 2
                    dve.wait_ge(hid_hi_ready, cnt + (FC * f + i + 1))
                    dve.tensor_tensor(hid_lo[:, i % 2, :], hidden[:, i % 2, :], hid_hi[:, i % 2, :].bitcast(F32),
                                      ALU.subtract).then_inc(hid_lo_ready, 1)

                def round_(i, r=None):
                    a = t0 + 2 + 3 * i
                    split(a + 2, r)
                    low(i, r)
                    split(a + 3, r)
                    gate(i + 1, r)
                    if r is not None or a + 4 < NT:
                        split(a + 4, r)
                    mult(i + 1, r)

                split(t0 + 2)
                rms_step(st)
                split(t0 + 3)
                dve.wait_ge(rstd_ready, st.norm.n + 1)
                gate(0)
                mult(0)
                round_(0)
                peeled = 2 if t0 + 3 * FC == NT else 0
                with dve.Fori(0, (FC - 2 - peeled) // 2) as r:
                    round_(1, r)
                    round_(2, r)
                for i in range(FC - 1 - peeled, FC - 1):
                    round_(i)
                low(FC - 1)
                if t0 + 3 * FC - 1 + AHEAD < NT:
                    split(t0 + 3 * FC - 1 + AHEAD)

            def ffn_residual_step(st):
                q, ffn = st.k, st.u
                if q < 3:
                    dve.wait_ge(ffn_out, 3 * ffn.n + q + 1)
                else:
                    dve.wait_ge(tile_used, ffn.t + 3 * FC)
                v = x[:, 2 * q:2 * q + 2, 0:SEQ]
                dve.scalar_tensor_tensor(out=v, in0=ffn_bank[q][:, :].rearrange("p (c t) -> p c t", c=2),
                                         scalar=0.5, in1=v, op0=ALU.mult, op1=ALU.add).then_inc(ffn_added, 1)

            def conv_step_dve(st):
                c = st.c
                at = PARAM_AT["rec_conv_w"] + c
                w = [par[:, at + KC * i:at + KC * i + 1] for i in range(4)]
                b = PARAM_AT["rec_conv_b"] + c
                if c == 0:
                    dve.memset(r_pad[:, :, 0:3], 0.0).then_inc(mix_step, 1)
                scaled_product(st, r_pad[:, c, 3:], st.norm)
                dve.wait_ge(*evacuated(st.job))
                dve.wait_ge(mix_step, 1)
                dst = r_conv[:, c, :]
                dve.tensor_scalar(dst, r_pad[:, c, 0:SEQ], w[0], par[:, b:b + 1], ALU.mult, ALU.add)\
                    .then_inc(conv_step, 1)
                for i in range(1, 4):
                    dve.wait_ge(conv_step, 4 * c + i)
                    dve.scalar_tensor_tensor(out=dst, in0=r_pad[:, c, i:i + SEQ], scalar=w[i], in1=dst,
                                             op0=ALU.mult, op1=ALU.add).then_inc(conv_step, 1)

            def rec_decay_step(st):
                c = st.c
                dve.wait_ge(a_squared, c + 1)
                dve.scalar_tensor_tensor(out=th[:, c, :], in0=mix_t[:, c % 2, :], scalar=1.0, in1=th[:, c, :],
                                         op0=ALU.add, op1=ALU.mult).then_inc(root_in, 1)

            def rec_scan_step(st):
                c = st.c
                dve.wait_ge(bx_ready, c + 1)
                dve.wait_ge(decays, 2 * c + 2)
                dve.tensor_tensor_scan(r_conv[:, c, :], g_a[:, c, :], g_x[:, c, :], 0.0, ALU.mult, ALU.add)\
                    .then_inc(scanned, 1)

            def mix_low(c, n):
                dve.wait_ge(mix_hi_ready, n + 1)
                dve.tensor_tensor(mix_lo[:, c, :], mix_t[:, n % 2, :], mix_hi[:, c, :].bitcast(F32), ALU.subtract)\
                    .then_inc(mix_lo_ready, 1)

            def rec_out_step(st):
                c = st.c
                dve.wait_ge(y_ready, c + 1)
                dve.wait_ge(scanned, c + 1)
                if c >= 2:
                    dve.wait_ge(mix_lo_ready, st.n - 1)
                dve.tensor_tensor(mix_t[:, st.n % 2, :], y_act[:, c, :], r_conv[:, c, :], ALU.mult)\
                    .then_inc(mix_ready, 1)
                mix_low(c, st.n)

            def spatial_weights_step(st):
                for i in range(2):
                    dve.wait_ge(t_full, st.t_uses[i] + 1)
                    dve.tensor_copy(ws_t[:, 4 * i:4 * i + 4, :],
                                    T[st.t_uses[i] % 2][:, :].rearrange("p (h d) -> p h d", h=4))\
                        .then_inc(t_free[st.t_uses[i] % 2], 1)

            def sg_mix_step(st):
                c = st.c
                dve.wait_ge(s_full, st.s_use + 1)
                if c == 0:
                    dve.wait_ge(mix_landed, 6 * 16)
                if c >= 2:
                    dve.wait_ge(mix_lo_ready, KC + st.n - 1)
                q = mix_t[:, c % 2, :].rearrange("p (t d) -> p t d", t=2)
                s = S[st.s_use % 2][:, 0:SEQ].rearrange("p (t d) -> p t d", t=2)
                dve.tensor_tensor(q, s, ws_b[:, c, :].unsqueeze(1).to_broadcast([P, 2, P]), ALU.add)\
                    .then_inc(s_free[st.s_use % 2], 1)
                dve.wait_ge(*s_out(st.s_use))
                dve.wait_ge(u_ready, c + 1)
                dve.tensor_tensor(mix_t[:, c % 2, :], mix_t[:, c % 2, :], sg_u[:, c, :], ALU.mult)\
                    .then_inc(mix_ready, 1)
                mix_low(c, KC + st.n)

            run = {"split": lambda st: split(st.t), "turn_in": turn_in_step, "ada_turn": ada_turn_step,
                   "ada_scale": ada_scale_step, "rms": rms_step, "normed": normed_step, "value_turn": value_turn_step,
                   "split_x": split_x_step, "rec_y": rec_y_step, "sg_v": sg_v_step, "sg_u": sg_u_step,
                   "ffn_residual": ffn_residual_step, "gate": gate_step, "merge": merge_step, "gated_residual": gated_residual_step,
                   "plain_residual": plain_residual_step, "scores": scores_step, "turn_probs": turn_probs_step,
                   "values": values_step, "turn_out": turn_out_step, "ret_scores": ret_scores_step,
                   "ret_out": ret_out_step, "head_norm": head_norm_step, "rotate": rotate_step, "ffn": ffn_step,
                   "conv": conv_step_dve, "rec_decay": rec_decay_step, "rec_scan": rec_scan_step,
                   "rec_out": rec_out_step, "spatial_weights": spatial_weights_step, "sg_mix": sg_mix_step}
            for st in steps:
                if st.kind in run:
                    run[st.kind](st)

        @block.tensor
        def _(pe):
            ident = C_("ident")

            def three(dst, w, hi, lo, start, stop, shared=False):
                slot, blk = w
                at = slice(P * blk, P * blk + P)
                nc.tensor.matmul(dst, w_hi[:, slot, at], hi, start=start, stop=False, skip_group_check=shared)
                nc.tensor.matmul(dst, w_hi[:, slot, at], lo, start=False, stop=False, skip_group_check=shared)
                return nc.tensor.matmul(dst, w_lo[:, slot, at], hi, start=False, stop=stop, skip_group_check=shared)

            def product_step(st):
                job = st.job
                n = job.cols
                dst = G[job.n % 2][:, 0:n]
                if st.at == 0:
                    pe.wait_ge(lo_ready, job.tile + 1)
                    if job.n >= 2:
                        pe.wait_ge(g_free[job.n % 2], job.n // 2)
                    if job.src.startswith("o_"):
                        pe.wait_ge(o_lo_ready, job.outs.out.n + 1)
                for i in range(st.at, st.at + st.part):
                    if job.src == "h":
                        if job.norm:
                            pe.wait_ge(h_lo_ready, job.norm.chunks[i].h + 1)
                        hi, lo = h_hi[:, i, 0:n], h_lo[:, i, 0:n]
                    elif job.src == "m":
                        if m_waited[0] < m_base(job) + i + 1:
                            m_waited[0] = m_base(job) + i + 1
                            pe.wait_ge(m_lo_ready, m_waited[0])
                        hi, lo = m_hi[:, i, 0:n], m_lo[:, i, 0:n]
                    elif job.src == "mix":
                        if mix_waited[0] < KC * job.mixer + i + 1:
                            mix_waited[0] = KC * job.mixer + i + 1
                            pe.wait_ge(mix_lo_ready, mix_waited[0])
                        hi, lo = mix_hi[:, i, :], mix_lo[:, i, :]
                    else:
                        o = o_of(job.src[2:])
                        hi, lo = o_hi[o][:, i, 0:n], o_lo[o][:, i, 0:n]
                    ins = three(dst, (job.tile % SPLIT, st.base + i), hi, lo, start=(i == 0), stop=(i == job.blocks - 1))
                if st.at + st.part == job.blocks:
                    ins.then_inc(half_used if job.first_half else tile_used, 1)

            def ada_tile_step(st):
                u, k, slot = st.u, st.k, st.tile % SPLIT
                pe.wait_ge(lo_ready, st.tile + 1)
                if k == 0:
                    pe.wait_ge(set_up_dve, 2)
                    for use in u.t_uses:
                        pe.wait_ge(t_free[use % 2], use // 2)
                for j, use in enumerate(u.t_uses):
                    dst, at = T[use % 2][0:4, :], slice(512 * j, 512 * j + 512)
                    nc.tensor.matmul(dst, c_split[:, k, :], w_hi[:, slot, at], start=(k == 0), stop=False)
                    ins = nc.tensor.matmul(dst, c_split[:, k, :], w_lo[:, slot, at], start=False, stop=(k == KC - 1))
                    if j == 0 and k == KC - 1:
                        ins.then_inc(t_full, 2)
                ins.then_inc(tile_used, 1)

            def ada_turn_step(st):
                u = st.u
                for use in u.t_uses:
                    pe.wait_ge(*t_out(use))
                pe.wait_ge(m_free, u.m)
                for k in range(KC):
                    ins = nc.tensor.matmul(M[:, 2 * k:2 * k + 2], ada_rows[:, P * k:P * k + P], C_("parts")[0:4, :],
                                           start=True, stop=True)
                ins.then_inc(m_full, 1)

            m_waited, mix_waited = [0], [0]

            def m_base(job):
                return 0 if job.tile < TILES.index(("w_out", 1, 0)) else KC

            def turn_in_step(st):
                pe.wait_ge(con_landed, 16)
                pe.wait_ge(tok_landed, 32)
                if st.t_use >= 2:
                    pe.wait_ge(t_free[st.t_use % 2], st.t_use // 2)
                for b in range(4):
                    ins = nc.tensor.transpose(T[st.t_use % 2][:, P * b:P * b + P], tok[:, b, P * st.k:P * st.k + P], ident)
                ins.then_inc(t_full, 1)

            def rms_step(st):
                norm = st.norm
                c, units = norm.cols, norm.units
                pe.wait_ge(sq_added, units[-1].add_n + 1)
                if norm.m:
                    pe.wait_ge(m_free, norm.m)
                for j in range(units[0].blocks):
                    ins = nc.tensor.matmul(M[:, 0:c], C_("mean_all"), sum_sq[:, c * j:c * j + c], start=(j == 0),
                                           stop=(j == units[0].blocks - 1))
                ins.then_inc(m_full, 1)

            def normed_step(st):
                if st.norm.how != "out":
                    return
                pe.wait_ge(f_ready, st.f + 1)
                pe.wait_ge(t_free[st.t_use % 2], st.t_use // 2)
                for b in range(2):
                    ins = nc.tensor.transpose(T[st.t_use % 2][:, P * b:P * b + P],
                                              scaled[:, st.k % 2, P * b:P * b + P], ident)
                ins.then_inc(t_full, 1)

            def value_turn_step(st):
                pe.wait_ge(*evacuated(st.evac.job))
                pe.wait_ge(m_free, st.m)
                for b in range(4):
                    ins = nc.tensor.transpose(M[:, P * b:P * b + P], stage[:, P * b:P * b + P], ident)
                ins.then_inc(m_full, 1)

            def scores_step(st):
                u = st.u
                g = u.g
                if g.branch == "na":
                    pe.wait_ge(*evacuated(g.k_job.job))
                    pe.wait_ge(*evacuated(g.q_job.job))
                else:
                    pe.wait_ge(rot_done, g.q_rot.n + 1)
                if u.s_use >= 2:
                    pe.wait_ge(s_free[u.s_use % 2], u.s_use // 2)
                at = slice(DH * u.hp, DH * u.hp + DH)
                nc.tensor.matmul(S[u.s_use % 2][:, 0:u.keys], g_buf(g, "q")[at, P * u.b:P * u.b + P],
                                 g_buf(g, "k")[at, u.key_at:u.key_at + u.keys], start=True, stop=True)\
                    .then_inc(s_full, 1)

            def turn_probs_step(st):
                u = st.u
                pe.wait_ge(*s_out(u.s_use))
                if u.t_use >= 2:
                    pe.wait_ge(t_free[u.t_use % 2], u.t_use // 2)
                for j in range(u.keys // P):
                    ins = nc.tensor.transpose(T[u.t_use % 2][:, P * j:P * j + P], probs[:, u.n % 2, P * j:P * j + P],
                                              ident)
                ins.then_inc(t_full, 1)

            def values_step(st):
                u = st.u
                g = u.g.kv if u.g.branch == "gqa" else u.g
                pe.wait_ge(*t_out(u.t_use))
                if u.o_use:
                    pe.wait_ge(o_free, u.o_use)
                pe.wait_ge(m_free, g.v_turn.m + 1)
                v = g_buf(g, "v")
                blocks = list(key_blocks(u))
                for i, j in enumerate(blocks):
                    ins = nc.tensor.matmul(O[:, 0:DH], probs_t[:, u.n % 2, P * i:P * i + P],
                                           v[:, j, DH * u.hp:DH * u.hp + DH], start=(i == 0),
                                           stop=(i == len(blocks) - 1))
                ins.then_inc(o_full, 1)

            def turn_out_step(st):
                g = st.g
                pe.wait_ge(o_free, (g.ret_out.o_use if g.branch == "ret" else g.last_unit.o_use) + 1)
                pe.wait_ge(m_free, st.m)
                for b in range(g.blocks):
                    ins = nc.tensor.transpose(M[:, P * b:P * b + P], out_rows[:, b, :], ident)
                ins.then_inc(m_full, 1)

            def ret_scores_step(st):
                g = st.g
                pe.wait_ge(*evacuated(g.k_job.job))
                pe.wait_ge(*evacuated(g.q_job.job))
                if st.s_use >= 2:
                    pe.wait_ge(s_free[st.s_use % 2], st.s_use // 2)
                nc.tensor.matmul(S[st.s_use % 2][:, 0:st.cols], g_buf(g, "k")[:, P * st.j:P * st.j + P],
                                 g_buf(g, "q")[:, 0:st.cols], start=True, stop=True).then_inc(s_full, 1)

            def ret_out_step(st):
                g = st.g
                pe.wait_ge(*s_out(g.last_scores.s_use))
                pe.wait_ge(m_free, g.v_turn.m + 1)
                if st.o_use:
                    pe.wait_ge(o_free, st.o_use)
                v = g_buf(g, "v")
                for b in range(g.blocks):
                    keys = range(4) if b < 2 else range(2, 4)
                    for j in keys:
                        ins = nc.tensor.matmul(O[:, P * b:P * b + P], work[:, j, P * b:P * b + P], v[:, j, :],
                                               start=(j == keys[0]), stop=(j == 3))
                ins.then_inc(o_full, 1)

            def head_norm_step(st):
                pe.wait_ge(*evacuated(st.job))
                pe.wait_ge(m_free, st.m)
                nc.tensor.matmul(M[:, 0:st.cols], C_("mean_head"), head_sq[:, 0:st.cols], start=True, stop=True)\
                    .then_inc(m_full, 1)

            def rotate_step(st):
                pe.wait_ge(qk_normed, st.n + 1)
                pe.wait_ge(m_free, st.m)
                dst = g_buf(st.g, "k" if st.what == "key" else "q")
                nc.tensor.matmul(M[:, 0:SEQ], C_("swap"), dst[:, 0:SEQ], start=True, stop=True).then_inc(m_full, 1)

            def ffn_step(st):
                f, t0, norm = st.n, st.t, st.norm

                def up(i, which, r=None, first=False):
                    t = t0 + ffn_tile(which, i)
                    base, cnt = (0, 0) if r is None else (r * 6, r * 2)
                    pe.wait_ge(lo_ready, base + (t + 1))
                    if i < 2:
                        bank_free, uses = (g_free, st.job) if which == "g" else (s_free, st.s_use)
                        pe.wait_ge(bank_free[i], (uses + 1 - i) // 2)
                    else:
                        pe.wait_ge(gate_scaled if which == "g" else hid_ready, cnt + (FC * f + i - 1))
                    dst = (G if which == "g" else S)[i % 2][:, 0:SEQ]
                    for k in range(KC):
                        if first:
                            pe.wait_ge(h_lo_ready, norm.chunks[k].h + 1)
                        ins = three(dst, (t % SPLIT, k), h_hi[:, k, 0:SEQ], h_lo[:, k, 0:SEQ], k == 0, k == KC - 1)
                    ins.then_inc(tile_used, 1)

                def down(i, r=None, last=False):
                    t = t0 + ffn_tile("o", i)
                    base, cnt = (0, 0) if r is None else (r * 6, r * 2)
                    pe.wait_ge(lo_ready, base + (t + 1))
                    pe.wait_ge(hid_lo_ready, cnt + (FC * f + i + 1))
                    for dc in range(KC):
                        dst = ffn_bank[dc // 2][:, SEQ * (dc % 2):SEQ * (dc % 2) + SEQ]
                        ins = three(dst, (t % SPLIT, dc), hid_hi[:, i % 2, :], hid_lo[:, i % 2, :],
                                    i == 0 and dc % 2 == 0, last, shared=True)
                        if last and dc % 2 and dc < KC - 1:
                            ins.then_inc(ffn_out, 1)
                    ins.then_inc(tile_used, 1)

                def round_(i, r=None):
                    up(i + 1, "g", r)
                    up(i + 1, "u", r)
                    down(i, r)

                up(0, "g", first=True)
                rms_step(st)
                up(0, "u")
                round_(0)
                with pe.Fori(0, (FC - 2) // 2) as r:
                    round_(1, r)
                    round_(2, r)
                down(FC - 1, last=True)

            def rec_gates_step(st):
                if st.c == 0:
                    pe.wait_ge(mix_landed, 64)
                pe.wait_ge(conv_step, 4 * st.c + 4)
                pe.wait_ge(s_free[st.s_use % 2], st.s_use // 2)
                s = S[st.s_use % 2]
                nc.tensor.matmul(s[:, 0:SEQ], gate_w[:, 0, st.c, :], r_conv[:, st.c, :], start=True, stop=True)
                nc.tensor.matmul(s[:, SEQ:BOTH], gate_w[:, 1, st.c, :], r_conv[:, st.c, :], start=True, stop=True)\
                    .then_inc(s_full, 1)

            def spatial_weights_step(st):
                pe.wait_ge(ws_cut, 1)
                pe.wait_ge(ffn_added, 4 * 3)
                for i in range(2):
                    u = st.t_uses[i]
                    pe.wait_ge(t_free[u % 2], u // 2)
                    for h in range(4):
                        ins = nc.tensor.transpose(T[u % 2][:, P * h:P * h + P], ws[:, 4 * i + h, :], ident)
                    ins.then_inc(t_full, 1)

            def sg_turn_step(st):
                pe.wait_ge(v_normed, st.c + 1)
                pe.wait_ge(t_free[st.t_use % 2], st.t_use // 2)
                for b in range(2):
                    ins = nc.tensor.transpose(T[st.t_use % 2][:, P * b:P * b + P], sg_v[:, st.c, P * b:P * b + P],
                                              ident)
                ins.then_inc(t_full, 1)

            def sg_mix_step(st):
                pe.wait_ge(*t_out(st.turn.t_use))
                pe.wait_ge(s_free[st.s_use % 2], st.s_use // 2)
                for b in range(2):
                    ins = nc.tensor.matmul(S[st.s_use % 2][:, P * b:P * b + P], sg_vt[:, st.c % 2, P * b:P * b + P],
                                           ws_t[:, st.c, :], start=True, stop=True)
                ins.then_inc(s_full, 1)

            run = {"product": product_step, "ada_tile": ada_tile_step, "ada_turn": ada_turn_step, "turn_in": turn_in_step, "rms": rms_step,
                   "normed": normed_step, "value_turn": value_turn_step, "scores": scores_step,
                   "turn_probs": turn_probs_step, "values": values_step, "turn_out": turn_out_step,
                   "ret_scores": ret_scores_step, "ret_out": ret_out_step, "head_norm": head_norm_step,
                   "rotate": rotate_step, "ffn": ffn_step, "rec_gates": rec_gates_step,
                   "spatial_weights": spatial_weights_step, "sg_turn": sg_turn_step, "sg_mix": sg_mix_step}
            for st in steps:
                if st.kind in run:
                    run[st.kind](st)


def kernel(**inputs):
    from concourse import bacc
    from concourse.bass_utils import run_bass_kernel_spmd

    a = {name: np.ascontiguousarray(v) for name, v in inputs.items()}
    arrays = {
        "weights": lay_out_weights(a),
        "params": lay_out_params(a),
        "consts": shape_tables(),
        "tokens": np.concatenate([a["x"][0], a["ctx"][0]]),
        "rpb": lay_out_bias(a["na_rpb"]),
        "gate_a": a["rec_gate_a_w_2"][0],
        "gate_x": a["rec_gate_x_w_2"][0],
        "spatial": a["sg_w_s_2"][0],
        "spatial_b": a["sg_b_s_2"][0],
    }
    arrays = {name: np.ascontiguousarray(v) for name, v in arrays.items()}
    nc = bacc.Bacc("TRN2", target_bir_lowering=False, num_devices=1)
    args = [nc.dram_tensor(f"in_{n}", v.shape, F32, kind="ExternalInput").ap() for n, v in arrays.items()]
    args.append(nc.dram_tensor("out", (SEQ, D), F32, kind="ExternalOutput").ap())
    block_kernel(nc, *args)
    r = run_bass_kernel_spmd(nc, [{f"in_{n}": v for n, v in arrays.items()}], core_ids=[0])
    return r.results[0]["out"].reshape(1, SEQ, D)
```

```python
from contextlib import ExitStack

import numpy as np

import concourse.bass as bass
from concourse import mybir

F32 = mybir.dt.float32
F32R = mybir.dt.float32r
ALU = mybir.AluOpType
ACT = mybir.ActivationFunctionType
AX_X = mybir.AxisListType.X

P = 128
D = 1024
KC = D // P
SEQ = 256
BOTH = 2 * SEQ
DEPTH = 2
GRID_W = 64
NA_HEADS = 8
DH = 64
D_FF = 2816
FC = D_FF // P
EPS = 1e-6

RAW = 4
SPLIT = 4
ROUND = 4
AHEAD = 3

IN_AT = dict(zip(
    "rq rk rv rg nq nk nv ng gq gk gv gg mg".split(),
    np.cumsum([0, 512, 512, 512, 512, 512, 512, 512, 512, 512, 128, 128, 512]).tolist(),
))
GQA_COLS = [np.r_[DH * c:DH * c + DH, DH * (c + 4):DH * (c + 4) + DH] for c in range(4)]


ADA_FIRST = [(0, 0), (0, 1)]
ADA_BESIDE = [(0, 2), (1, 0), (1, 1), (1, 2)]
ADA_SLOTS = [0] * 4 + [1] * 12 + [2] * 10


def tile_order():
    out = [("ada", layer, section, k) for layer, section in ADA_FIRST for k in range(KC)]
    for layer in range(DEPTH):
        ada = [("ada", *section, k) for section in ADA_BESIDE for k in range(KC)] if layer == 0 else []
        slots = list(ADA_SLOTS) if layer == 0 else [0] * len(ADA_SLOTS)

        def beside(tile):
            count = slots.pop(0)
            found = [tile] + ada[:count]
            del ada[:count]
            return found

        for c in range(4):
            for n, name in enumerate(("nk", "nv", "nq", "ng")):
                out.append((name, layer, c))
        for h in range(4):
            for n, name in enumerate(("rk", "rv", "rq", "rg")):
                out += beside((name, layer, h))
        for q in range(4):
            out += beside(("mg", layer, KC + 2 * q)) + beside(("mg", layer, KC + 2 * q + 1))
            out.append(("w_na_o", layer, q))
        out += beside(("gk", layer, 0)) + beside(("gv", layer, 0))
        for c in range(4):
            out += [("gq", layer, c), ("gg", layer, c)]
            for q in {0: [], 1: [0], 2: [1], 3: [2, 3]}[c]:
                out += [("mg", layer, 2 * q), ("mg", layer, 2 * q + 1), ("w_ret_o", layer, q)]
        for q in range(4):
            out += [("mg", layer, 2 * KC + 2 * q), ("mg", layer, 2 * KC + 2 * q + 1), ("w_gqa_o", layer, q)]
        out += [("w_out", layer, n) for n in range(KC)]
    for layer in range(DEPTH):
        for f in (0, 1):
            ffn = [("ffn_g", layer, f, 0), ("ffn_u", layer, f, 0)]
            for i in range(FC - 1):
                ffn += [("ffn_g", layer, f, i + 1), ("ffn_u", layer, f, i + 1), ("ffn_o", layer, f, i)]
            out += ffn + [("ffn_o", layer, f, FC - 1)]
            if f == 0 and layer == 0:
                out += [("rec_r", 0, n) for n in range(KC)] + [("rec_y", 0, n) for n in range(KC)]
                out += [("rec_o", 0, n) for n in range(KC)]
            if f == 0 and layer == 1:
                out += [("sg_v", 0, n) for n in range(KC)] + [("sg_u", 0, n) for n in range(KC)]
                out += [("sg_o", 0, n) for n in range(KC)]
    return out


TILES = tile_order()
NT = len(TILES)


def column_tile(w, cols):
    return w[:, cols].reshape(KC, P, P).transpose(1, 0, 2).reshape(P, D)


def out_tile(w, q):
    return w[:, 2 * P * q:2 * P * (q + 1)].reshape(4, P, 2, P).transpose(1, 2, 0, 3).reshape(P, D)


def lay_out_weights(a):
    out = np.empty((NT, P, D), np.float32)
    gqa_rows = np.concatenate(GQA_COLS)
    for t, (kind, layer, *which) in enumerate(TILES):
        n = which[0]
        cols = slice(P * n, P * n + P)
        if kind == "ada":
            out[t] = a["ada_w"][layer][P * which[1]:P * which[1] + P, D * n:D * n + D]
        elif kind in ("gq", "gg"):
            out[t] = column_tile(a["w_in"][layer], IN_AT[kind] + GQA_COLS[n])
        elif kind in IN_AT:
            out[t] = column_tile(a["w_in"][layer], slice(IN_AT[kind] + P * n, IN_AT[kind] + P * n + P))
        elif kind == "w_gqa_o":
            out[t] = out_tile(a[kind][layer][gqa_rows], n)
        elif kind in ("w_na_o", "w_ret_o"):
            out[t] = out_tile(a[kind][layer], n)
        elif kind == "w_out":
            out[t] = column_tile(a[kind][layer], cols)
        elif kind in ("ffn_g", "ffn_u"):
            i = which[1] * P + (D_FF if kind == "ffn_u" else 0)
            out[t] = column_tile(a[f"ffn{n + 1}_w_in_2"][layer], slice(i, i + P))
        elif kind == "ffn_o":
            out[t] = a[f"ffn{n + 1}_w_out_2"][layer][P * which[1]:P * which[1] + P]
        elif kind == "rec_y":
            out[t] = column_tile(a["rec_w_in_2"][0], cols)
        elif kind == "rec_r":
            out[t] = column_tile(a["rec_w_in_2"][0], slice(D + P * n, D + P * n + P))
        elif kind == "rec_o":
            out[t] = column_tile(a["rec_w_out_2"][0], cols)
        elif kind == "sg_u":
            out[t] = column_tile(a["sg_w_in_2"][0], cols)
        elif kind == "sg_v":
            out[t] = column_tile(a["sg_w_in_2"][0], slice(D + P * n, D + P * n + P))
        elif kind == "sg_o":
            out[t] = column_tile(a["sg_w_out_2"][0], cols)
    return out


def by_partition(a):
    a = np.asarray(a)
    a = a.reshape(-1, a.shape[-1] // P, P)
    return a.transpose(2, 0, 1).reshape(P, -1)


PARAMS = [("c", 8), ("c_ctx", 8), ("ada_b", 48), ("norm_w", 16), ("ret_gn_w", 8), ("q_norm_w", 2), ("k_norm_w", 2),
          ("decay", 16), ("ffn1_norm", 16), ("mix_norm", 16), ("ffn2_norm", 16), ("final_norm_w", 8),
          ("final_norm", 8), ("rec_conv_w", 32), ("rec_conv_b", 8), ("rec_gate_a_b", 8), ("rec_gate_x_b", 8),
          ("rec_lambda", 8), ("sg_v_norm", 8)]
PARAM_AT = dict(zip([n for n, _ in PARAMS], np.cumsum([0] + [w for _, w in PARAMS]).tolist()))
NPARAM = sum(w for _, w in PARAMS)


def lay_out_params(a):
    rows = {
        "c": by_partition(a["c"]), "c_ctx": by_partition(a["c_ctx"]), "ada_b": by_partition(a["ada_b"]),
        "norm_w": by_partition(a["norm_w"]), "ret_gn_w": by_partition(a["ret_gn_w"]),
        "q_norm_w": np.tile(a["q_norm_w"], (1, 2)).T, "k_norm_w": np.tile(a["k_norm_w"], (1, 2)).T,
        "decay": np.broadcast_to(a["ret_log_decay"].reshape(1, -1), (P, 16)),
        "ffn1_norm": by_partition(a["ffn1_norm_2"]), "mix_norm": by_partition(a["mix_norm_2"]),
        "ffn2_norm": by_partition(a["ffn2_norm_2"]), "final_norm_w": by_partition(a["final_norm_w"]),
        "final_norm": by_partition(a["final_norm_2"]), "rec_conv_w": by_partition(a["rec_conv_w_2"][0]),
        "rec_conv_b": by_partition(a["rec_conv_b_2"]),
        "rec_gate_a_b": by_partition(a["rec_gate_a_b_2"].reshape(1, -1)),
        "rec_gate_x_b": by_partition(a["rec_gate_x_b_2"].reshape(1, -1)),
        "rec_lambda": by_partition(a["rec_lambda_2"]), "sg_v_norm": by_partition(a["sg_v_norm_2"]),
    }
    return np.ascontiguousarray(np.concatenate([rows[n] for n, _ in PARAMS], axis=1))


CONSTS = [("ident", P), ("swap", P), ("cos", SEQ), ("sin", SEQ),
          ("dif", 3 * P), ("window", GRID_W), ("parts", 2), ("ones", 1),
          ("heads", 2)]
CONST_AT = dict(zip([n for n, _ in CONSTS], np.cumsum([0] + [w for _, w in CONSTS]).tolist()))
NCONST = sum(w for _, w in CONSTS)


def shape_tables():
    p = np.arange(P)
    partner = np.where(p % 32 < 16, p + 16, p - 16)
    t = np.arange(SEQ)
    freqs = (np.float32(10000.0) ** (-np.arange(16, dtype=np.float32) / 16)).astype(np.float32)
    pos = np.where(((p % DH) < 32)[:, None], (t // GRID_W)[None], (t % GRID_W)[None]).astype(np.float32)
    ang = (pos * freqs[p % 16][:, None]).astype(np.float32)
    sign = np.where(p % 32 < 16, -1.0, 1.0)[:, None]
    qc, kc = (p % GRID_W)[:, None], np.arange(GRID_W)[None]
    start = np.clip(qc - 8, 0, GRID_W - 16)
    rows = {
        "ident": np.eye(P), "swap": (p[:, None] == partner[None, :]), "cos": np.cos(ang), "sin": np.sin(ang) * sign,
        "dif": np.arange(3 * P)[None] - P - p[:, None],
        "ones": np.full((P, 1), 1.0 / D), "heads": (p[:, None] // DH == np.arange(2)[None]) / DH,
        "parts": (p[:, None] % 2 == np.arange(2)[None]),
        "window": np.where((kc >= start) & (kc < start + 16), 0.0, -1e30),
    }
    return np.concatenate([rows[n].astype(np.float32) for n, _ in CONSTS], axis=1)


def lay_out_bias(rpb):
    pad = np.pad(rpb, ((0, 0), (0, 0), (0, 0), (GRID_W - 16, GRID_W - 16)))
    shifted = np.stack([pad[..., GRID_W - 1 - q:2 * GRID_W - 1 - q] for q in range(GRID_W)], axis=3)
    by_row = np.stack([shifted[:, :, 5 - r:11 - r] for r in range(2)], axis=2)
    by_row = by_row.reshape(DEPTH, NA_HEADS // 2, 2, 2, 6, GRID_W, GRID_W)
    return by_row.transpose(0, 1, 3, 5, 2, 4, 6).reshape(DEPTH, NA_HEADS // 2, P, 2, 6 * GRID_W)


class Step:

    def __init__(self, kind, n, rows=None, m_spread=None, spread=None, chunks=None, first=None, last=None,
                 units=None, how=None, add_n=None, at=None, b=None, base=None, before=None, bias=None, blocks=None,
                 bn_at=None, br=None, branch=None, c=None, cols=None, dc=None, evac=None, f=None,
                 first_half=None, g=None, gate=None, h=None, half_n=None, hp=None, j=None, job=None, k=None,
                 key_at=None, keys=None, layer=None, live=None, m=None, m_n=None, mixer=None, norm=None,
                 o_use=None, outs=None, part=None, s_use=None, slot=None, src=None, t=None,
                 t_use=None, t_uses=None, tile=None, turn=None, u=None, up=None, what=None):
        self.kind, self.n = kind, n
        self.rows, self.m_spread, self.spread = rows, m_spread, spread
        self.chunks, self.first, self.last, self.units, self.how = chunks, first, last, units, how
        self.add_n, self.at, self.b, self.base = add_n, at, b, base
        self.before, self.bias, self.blocks, self.bn_at = before, bias, blocks, bn_at
        self.br, self.branch, self.c, self.cols = br, branch, c, cols
        self.dc, self.evac, self.f, self.first_half = dc, evac, f, first_half
        self.g, self.gate, self.h, self.half_n = g, gate, h, half_n
        self.hp, self.j, self.job, self.k = hp, j, job, k
        self.key_at, self.keys, self.layer, self.live = key_at, keys, layer, live
        self.m, self.m_n, self.mixer, self.norm = m, m_n, mixer, norm
        self.o_use, self.outs, self.part, self.s_use = o_use, outs, part, s_use
        self.slot, self.src, self.t = slot, src, t
        self.t_use, self.t_uses, self.tile, self.turn = t_use, t_uses, tile, turn
        self.u, self.up, self.what = u, up, what


class Schedule:

    def __init__(self):
        self.steps = []
        self.counts = {}
        self.uses = {}
        self.tile = 0
        self.half = 0
        self.background = []
        self.due = []
        self.lagged = []
        self.section = None
        self.bn = 0

    def count(self, kind):
        n = self.counts.get(kind, 0)
        self.counts[kind] = n + 1
        return n

    def use(self, bank):
        n = self.uses.get(bank, 0)
        self.uses[bank] = n + 1
        return n

    def add(self, kind, **fields):
        step = Step(kind=kind, n=self.count(kind), **fields)
        self.steps.append(step)
        return step

    def add_after_split(self, kind, **fields):
        step = Step(kind=kind, n=self.count(kind), **fields)
        self.lagged.append(step)
        return step

    def flush(self):
        self.steps += self.lagged
        self.lagged = []

    def split_ahead(self, t):
        if t + AHEAD < NT:
            self.add("split", t=t + AHEAD)

    def fill(self, slots=1):
        for _ in range(slots):
            if self.background:
                self.background.pop(0)()

    def drain(self):
        if self.background:
            self.flush()
        while self.background:
            self.fill()

    def later(self, parts, add_step):
        self.due.append([parts, add_step])

    def turn_due(self):
        while self.due:
            self.due.pop(0)[1]()

    def part_done(self):
        for entry in self.due:
            entry[0] -= 1
        while self.due and self.due[0][0] <= 0:
            self.due.pop(0)[1]()

    def product(self, what, src, n, blocks=KC, parts=(3, 3, 2), **fields):
        kind = TILES[self.tile][0]
        assert kind == what, (kind, what, self.tile)
        first_half = blocks < KC and self.half == 0
        job = Step(kind="job", n=self.use("G"), tile=self.tile, src=src, cols=n, blocks=blocks, what=what,
                   first_half=first_half, half_n=self.count("half") if first_half else None, **fields)
        base = 0 if blocks == KC else 4 * self.half
        if base == 0:
            self.split_ahead(self.tile)
        self.flush()
        at = 0
        for part in (parts if blocks == KC else (2, 2)):
            self.add("product", job=job, at=at, part=part, base=base)
            at += part
            self.part_done()
            self.fill()
        if blocks == KC:
            self.tile += 1
        else:
            self.tile, self.half = self.tile + self.half, 1 - self.half
        return job


def schedule_layer(s, layer, h_norm):
    live = BOTH if layer == 0 else SEQ
    blocks = live // P
    groups = []
    first = {"h": h_norm}

    def src():
        return dict(src="h", norm=first.pop("h", None))

    def proj(what, n):
        return s.product(what, n=n, **src())

    def key(name, g):
        g.k_job = s_add_evac(proj(name, BOTH), "key", g)

    def value(name, g):
        job = proj(name, BOTH)
        g.v_evac = s.add_after_split("value_rows", job=job, g=g)

        def turn():
            g.v_turn = s.add("value_turn", evac=g.v_evac, g=g, m=s.use("M"))

        s.later(2, turn)

    def query(name, g):
        g.q_job = s_add_evac(proj(name, live), "query", g)

    def s_add_evac(job, what, g):
        return s.add_after_split("evacuate", job=job, what=what, g=g)

    def gate(name, g):
        job = proj(name, live)
        g.gate = s.add_after_split("gate", job=job, g=g, cols=live)

    def new_group(branch, c):
        g = Step(kind="group", n=s.count("group"), branch=branch, c=c, layer=layer, live=live, blocks=blocks)
        g.slot = g.n % 2
        groups.append(g)
        return g

    def rest():
        pass

    def softmax_units(g):
        units = []
        for hp in range(2):
            for b in range(blocks):
                x = b < 2
                units.append(Step(kind="unit", n=s.count("unit"), g=g, hp=hp, b=b, keys=BOTH if x else SEQ,
                                  key_at=0 if x else SEQ, bias=x and g.branch == "na"))
        for u in units:
            u.bias_n = s.count("biased") if u.bias else None
            u.last = u is units[-1]
        g.units = units
        g.last_unit = units[-1]

        def slot(i):
            def run():
                if i < len(units):
                    u = units[i]
                    u.s_use = s.use("S")
                    s.add("scores", u=u)
                if 0 <= i - 1 < len(units):
                    u = units[i - 1]
                    u.t_use = s.use("T")
                    s.add("turn_probs", u=u)
                if 0 <= i - 2 < len(units):
                    u = units[i - 2]
                    u.o_use = s.use("O")
                    s.add("values", u=u)
            return run

        slots = [slot(i) for i in range(len(units) + 2)]
        if len(units) < 8:
            slots = [x for run in slots[:-2] for x in (run, rest)] + slots[-2:]
        return slots + [rest, lambda: turn_out(g)]

    def turn_out(g):
        g.out = s.add("turn_out", g=g, m=s.use("M"))

    def retention_units(g):
        def decay():
            g.decay = s.add("decay", g=g)

        def slot(j):
            def run():
                cols = live if j >= 2 else SEQ
                st = s.add("ret_scores", g=g, j=j, cols=cols, s_use=s.use("S"))
                g.last_scores = st
            return run

        def out():
            g.ret_out = s.add("ret_out", g=g, o_use=s.use("O"), bn_at=s.bn)
            s.bn += 2 * blocks + 1

        return [decay, rest, rest] + [slot(j) for j in range(4)] + [out, rest, rest, rest, lambda: turn_out(g)]

    for c in range(4):
        g = new_group("na", c)
        g.bias = s.add("bias", g=g)
        key("nk", g)
        value("nv", g)
        query("nq", g)
        gate("ng", g)
        s.drain()
        s.background = softmax_units(g)

    ada = [(section, k) for section in ADA_BESIDE for k in range(KC)] if layer == 0 else []
    slots = list(ADA_SLOTS) if ada else [0] * len(ADA_SLOTS)

    def ada_tiles():
        count = slots.pop(0)
        for section, k in ada[:count]:
            ada_tile(s, section, k)
        del ada[:count]

    for h in range(4):
        g = new_group("ret", h)
        key("rk", g)
        ada_tiles()
        value("rv", g)
        ada_tiles()
        query("rq", g)
        ada_tiles()
        gate("rg", g)
        ada_tiles()
        s.drain()
        s.background = retention_units(g)

    merged = {"mg": [None, None]}

    def merge(branch, q, last_out):
        br = ("na", "ret", "gqa").index(branch)
        mg = []
        for dc in (2 * q, 2 * q + 1):
            job = proj("mg", live)
            mg.append(s.add_after_split("merge_gate", job=job, slot=dc % 2, before=merged["mg"][dc % 2], cols=live))
            if branch == "na":
                ada_tiles()
        if branch == "gqa":
            s.drain()
        for i, dc in enumerate((2 * q, 2 * q + 1)):
            job = s.product(f"w_{branch}_o", n=live, src=f"o_{branch}", blocks=4, norm=None, parts=None,
                            outs=last_out)
            st = s.add("merge", job=job, dc=dc, br=br, gate=mg[i], cols=live,
                       add_n=s.count("add") if br else None, m_n=s.count("m") if br == 2 else None)
            merged["mg"][dc % 2] = st

    na = [g for g in groups if g.branch == "na"]
    ret = [g for g in groups if g.branch == "ret"]
    for q in range(4):
        merge("na", q, na[-1])
    s.drain()
    kv = new_group("gqa_kv", 0)

    def norm_job(name, g, what, n):
        job = proj(name, n)
        evac = s.add_after_split("head_evacuate", job=job, what=what, g=g, cols=n)

        def norm():
            st = s.add("head_norm", job=job, what=what, g=g, cols=n, m=s.use("M"), evac=evac,
                       rows=s.count("rows"))
            s.later(2 if layer else 1, lambda: spread(st))

        def spread(st):
            st.spread = s.add("head_spread", norm=st, g=g, what=what, cols=n, m=s.use("M"))
            s.later(1, lambda: rotate(st))

        def rotate(st):
            rot = s.add("rotate", norm=st, g=g, what=what, m=s.use("M"))
            if what == "key":
                g.k_rot = rot
            else:
                g.q_rot = rot

        s.later(3 if layer else 2, norm)

    norm_job("gk", kv, "key", BOTH)
    ada_tiles()
    value("gv", kv)
    ada_tiles()
    for c in range(4):
        g = new_group("gqa", c)
        g.kv = kv
        norm_job("gq", g, "query", live)
        gate("gg", g)
        for q in {0: [], 1: [0], 2: [1], 3: [2]}[c]:
            merge("ret", q, ret[-1])
        s.drain()
        s.background = [rest, rest, rest] * (c == 0) + softmax_units(g)
        if c == 3:
            merge("ret", 3, ret[-1])
    gqa = [g for g in groups if g.branch == "gqa"]
    for q in range(4):
        merge("gqa", q, gqa[-1])
    s.drain()
    norm = new_norm(s, live if layer == 0 else SEQ)
    for dc in range(KC):
        job = s.product("w_out", n=live, src="m", norm=None)
        up = s.add("gated_residual", job=job, dc=dc, layer=layer, cols=live)
        square(s, norm, dc, 1, up, after_split=True)
    if layer == 0:
        norm.cols = BOTH
    return norm


def ada_tile(s, section, k):
    if k == 0:
        s.section = Step("section", s.count("section"), layer=section[0], c=section[1],
                         t_uses=[s.use("T"), s.use("T")])
    s.split_ahead(s.tile)
    s.add("ada_tile", tile=s.tile, u=s.section, k=k)
    s.tile += 1
    if k == KC - 1:
        done = s.section
        done.tile = s.tile - 1
        s.add("ada_rows", u=done)

        def turn():
            done.m = s.use("M")
            s.add("ada_turn", u=done)

        s.later(2, turn)


def new_norm(s, cols, how=None, weight=None):
    return Step("norm", s.count("norm"), cols=cols, how=how, layer=weight, units=[], chunks=[])


def rms(s, norm):
    s.flush()
    norm.m, norm.rows = s.use("M"), s.count("rows")
    s.add("rms", norm=norm)
    norm.m_spread = s.use("M")


def square(s, norm, k, chunks, up, after_split=False):
    add = s.add_after_split if after_split else s.add
    last = k + chunks == KC
    i = len(norm.units)
    st = add("square", norm=norm, k=k, blocks=chunks, up=up, first=i == 0, last=last, slot=i % 2,
             before=norm.units[i - 2] if i >= 3 else None,
             add_n=s.count("sq_add") if i and not last else None)
    norm.units.append(st)


def follow(s, norm, q, ups, after_split=False):
    if norm.how == "h":
        for k in (2 * q, 2 * q + 1):
            add = s.add_after_split if after_split else s.add
            norm.chunks.append(add("split_x", norm=norm, k=k, up=ups[k], h=s.count("h")))
    square(s, norm, 2 * q, 2, ups[2 * q + 1], after_split)


def normed(s, norm, k):
    split = norm.how == "ada"
    st = s.add("normed", norm=norm, k=k, f=s.count("f") if split or norm.how == "out" else None,
               h=s.count("h") if split else None, t_use=s.use("T") if norm.how == "out" else None)
    norm.chunks.append(st)
    return st


def build_schedule():
    s = Schedule()
    for t in range(AHEAD):
        s.add("split", t=t)
    for k in range(KC):
        ada_tile(s, ADA_FIRST[0], k)
    ups = [s.add("turn_in", k=k, t_use=s.use("T")) for k in range(KC)]
    s.turn_due()
    norm = new_norm(s, BOTH)
    for k in range(KC):
        square(s, norm, k, 1, ups[k])
        ada_tile(s, ADA_FIRST[1], k)
    rms(s, norm)
    s.turn_due()
    for layer in range(DEPTH):
        if layer:
            rms(s, norm)
        norm.how, norm.layer = "ada", layer
        s.add("ada_scale", layer=layer)
        for k in range(KC):
            normed(s, norm, k)
        norm = schedule_layer(s, layer, norm)
    norm.how, norm.layer = "residual", ("final_norm_w", 0)
    rms(s, norm)
    before, norm = norm, new_norm(s, SEQ, "h", ("ffn1_norm", 0))
    for q in range(KC // 2):
        ups = [normed(s, before, k) for k in (2 * q, 2 * q + 1)]
        follow(s, norm, q, [None] * (2 * q) + ups)
    for layer in range(DEPTH):
        norm = schedule_ffn(s, norm, "h", ("mix_norm", layer))
        mixer = schedule_recurrent if layer == 0 else schedule_spatial
        norm = mixer(s, norm, ("ffn2_norm", layer))
        norm = schedule_ffn(s, norm, *((("h", ("ffn1_norm", 1))) if layer == 0 else ("out", ("final_norm", 0))))
    rms(s, norm)
    for k in range(KC):
        normed(s, norm, k)
    s.add("store")
    assert s.tile == NT
    return s


def schedule_ffn(s, norm, how, weight):
    norm.m, norm.rows = s.use("M"), s.count("rows")
    norm.m_spread = s.use("M")
    ffn = s.add("ffn", t=s.tile, norm=norm, job=s.uses["G"], s_use=s.uses["S"])
    s.tile += 3 * FC
    after = new_norm(s, SEQ, how, weight)
    ups = []
    for q in range(KC // 2 + 1):
        if q < KC // 2:
            ups += [s.add("ffn_residual", u=ffn, k=q)] * 2
        if q:
            follow(s, after, q - 1, ups)
    return after


def schedule_recurrent(s, norm, weight):
    def gates(c):
        return lambda: s.add("rec_gates", c=c, s_use=s.use("S"))

    for n in range(KC):
        job = s.product("rec_r", n=SEQ, src="h", norm=norm if n == 0 else None)
        if n == 0:
            rms(s, norm)
        s.add("conv", job=job, c=n, norm=norm)
        s.later(3, gates(n))
    for n in range(KC):
        job = s.product("rec_y", n=SEQ, src="h", norm=None)
        s.add("rec_y", job=job, c=n)
        if n < 4:
            s.add_after_split("rec_decay", c=2 * n)
            s.add_after_split("rec_decay", c=2 * n + 1)
        if n == 4:
            for c in range(KC):
                s.add_after_split("rec_root", c=c)
        if n >= 4:
            for c in (2 * n - 8, 2 * n - 7):
                s.add_after_split("rec_scan", c=c)
        if n >= 5:
            for c in (2 * n - 10, 2 * n - 9):
                s.add_after_split("rec_out", c=c)
    s.flush()
    for c in (6, 7):
        s.add("rec_out", c=c)
    return mixer_out(s, "rec_o", 0, weight)


def schedule_spatial(s, norm, weight):
    turns = []

    def turn(c):
        turns.append(s.add("sg_turn", c=c, t_use=s.use("T")))

    def mix(c):
        s.add("sg_mix", c=c, turn=turns[c], s_use=s.use("S"))

    vnorm = new_norm(s, SEQ, "v", ("sg_v_norm", 0))
    for n in range(KC):
        job = s.product("sg_v", n=SEQ, src="h", norm=norm if n == 0 else None)
        if n == 0:
            rms(s, norm)
        s.add("sg_v", job=job, c=n, norm=norm)
        up = s.add_after_split("sg_gelu", c=n)
        square(s, vnorm, n, 1, up, after_split=True)
        if n == 4:
            s.add("spatial_weights", t_uses=[s.use("T"), s.use("T")])
    for n in range(KC):
        job = s.product("sg_u", n=SEQ, src="h", norm=None)
        if n == 0:
            rms(s, vnorm)
        s.add("sg_u", job=job, c=n)
        s.add_after_split("sg_u_gelu", job=job, c=n)
        normed(s, vnorm, n)
        if n >= 1:
            turn(n - 1)
        if n >= 2:
            mix(n - 2)
    s.flush()
    turn(KC - 1)
    mix(KC - 2)
    mix(KC - 1)
    return mixer_out(s, "sg_o", 1, weight)


def mixer_out(s, what, mixer, weight):
    norm = new_norm(s, SEQ, "h", weight)
    ups = []
    for n in range(KC):
        job = s.product(what, n=SEQ, src="mix", norm=None, mixer=mixer)
        ups.append(s.add("plain_residual", job=job, dc=n))
        if n % 2:
            follow(s, norm, n // 2, ups, after_split=n < KC - 1)
    return norm


def ffn_tile(which, i):
    if which == "o":
        return 3 * i + 4 if i < FC - 1 else 3 * FC - 1
    return (0 if i == 0 else 3 * i - 1) + (which == "u")


def block_kernel(nc, weights, params, consts, tokens, rpb, gate_a, gate_x, spatial, spatial_b, out):
    schedule = build_schedule()
    steps = schedule.steps
    ctx = ExitStack()
    with ctx:
        def sb(name, shape, dt=F32, stack=None):
            return (stack or ctx).enter_context(nc.sbuf_tensor(name, shape, dt))

        def sem(name):
            return ctx.enter_context(nc.semaphore(name))

        x = sb("x", [P, KC, BOTH])
        raw = sb("raw", [P, RAW, D])
        w_hi = sb("w_hi", [P, SPLIT, D], F32R)
        w_lo = sb("w_lo", [P, SPLIT, D], F32R)
        h_hi = sb("h_hi", [P, KC, BOTH], F32R)
        h_lo = sb("h_lo", [P, KC, BOTH], F32R)
        par = sb("par", [P, NPARAM])
        con = sb("con", [P, NCONST])
        c_silu = sb("c_silu", [P, KC, 2])
        c_split = sb("c_split", [P, KC, 4], F32R)
        ada = sb("ada", [P, DEPTH, 24, 2])
        ada_a = sb("ada_a", [P, KC, 2])
        eps = sb("eps", [P, 1])
        neg_half = sb("neg_half", [P, 1])
        stats = sb("stats", [P, 2, 8])
        log_g = sb("log_g", [P, 3, 16])
        gn_half = sb("gn_half", [P, 8])
        q_norm = sb("q_norm", [P, 2])
        lam = sb("lam", [P, 3, KC])
        square = sb("square", [P, 2, BOTH])
        rstd = sb("rstd", [P, BOTH])
        scaled = sb("scaled", [P, 2, BOTH])

        def P_(name, width=None):
            at = PARAM_AT[name]
            return par[:, at:at + (width or dict(PARAMS)[name])]

        def C_(name):
            at = CONST_AT[name]
            return con[:, at:at + dict(CONSTS)[name]]

        hybrid = ExitStack()

        def hb(name, shape, dt=F32, stack=None):
            return sb(name, shape, dt, stack or hybrid)

        o_hi = {"a": hb("oa_hi", [P, 4, BOTH], F32R)}
        o_lo = {"a": hb("oa_lo", [P, 4, BOTH], F32R)}
        m = hb("m", [P, KC, BOTH])
        tok = m[:, :, :].rearrange("p a b -> p (a b)").rearrange("p (t d) -> p t d", t=4)
        bias = hb("bias", [P, 2, 2, 6 * GRID_W])
        branch_gate = hb("branch_gate", [P, 2, BOTH])
        out_rows = hb("out_rows", [P, 4, P])
        gated = rstd
        attention = ExitStack()
        o_hi["b"] = hb("ob_hi", [P, 4, BOTH], F32R, attention)
        o_lo["b"] = hb("ob_lo", [P, 4, BOTH], F32R, attention)
        q_s = hb("q_s", [P, 2, BOTH], stack=attention)
        k_s = hb("k_s", [P, 2, BOTH], stack=attention)
        v_s = hb("v_s", [P, 2, 4, P], stack=attention)
        shared = hb("shared", [P, 4 * 3 * P], stack=attention)
        decay_s = shared[:, :].rearrange("p (k c) -> p k c", k=4)
        k_g, v_g = shared[:, 0:BOTH], shared[:, BOTH:2 * BOTH].rearrange("p (t d) -> p t d", t=4)
        stage = hb("stage", [P, BOTH], stack=attention)
        head_rows = k_s
        attention.close()
        m_hi = hb("m_hi", [P, KC, BOTH], F32R, attention)
        m_lo = hb("m_lo", [P, KC, BOTH], F32R, attention)
        attention.close()
        hb("reserved", [P, 8 * BOTH + 6 * BOTH + 12 * P + BOTH])
        half_tanh, head_sq = scaled[:, 0, :], scaled[:, 1, :]
        merge_tanh = hb("merge_tanh", [P, 2, BOTH])
        ada_rows = [merge_tanh[0:4, :, :].rearrange("p a b -> p (a b)"),
                    bias[0:4, :, :, :].rearrange("p a b c -> p (a b c)")[:, 0:D]]
        work = hb("work", [P, 4, BOTH])
        probs, probs_t = work[:, 0:2, :], work[:, 2:4, :]
        abs_dif = hb("abs_dif", [P, 3 * P])
        row_stat = hb("row_stat", [P, 3, 4])
        bn = hb("bn", [P, 4, 6])
        mean_var = hb("mean_var", [P, 4, 2])
        ret_rs = hb("ret_rs", [P, 4])
        hybrid.close()
        branch_sum = square
        sum_sq = scaled[:, 0, :]
        row_mean, row_rstd = stats[:, 0, :], stats[:, 1, :]

        silu_g = sb("silu_g", [P, 2, SEQ])
        hidden = sb("hidden", [P, 2, SEQ])
        hid_hi = sb("hid_hi", [P, 2, SEQ], F32R)
        hid_lo = sb("hid_lo", [P, 2, SEQ], F32R)
        mix_hi = sb("mix_hi", [P, KC, SEQ], F32R)
        mix_lo = sb("mix_lo", [P, KC, SEQ], F32R)
        mix_t = sb("mix_t", [P, 2, SEQ])
        rows_out = sb("rows_out", [P, 2, D])
        mixer = ExitStack()
        r_pad = sb("r_pad", [P, KC, SEQ + 3], stack=mixer)
        r_conv = sb("r_conv", [P, KC, SEQ], stack=mixer)
        g_a = sb("g_a", [P, KC, SEQ], stack=mixer)
        g_x = sb("g_x", [P, KC, SEQ], stack=mixer)
        y_act = sb("y_act", [P, KC, SEQ], stack=mixer)
        th = sb("th", [P, KC, SEQ], stack=mixer)
        gate_w = sb("gate_w", [P, 2, KC, P], stack=mixer)
        mixer.close()
        sg_v = sb("sg_v", [P, KC, SEQ], stack=mixer)
        sg_u = sb("sg_u", [P, KC, SEQ], stack=mixer)
        sg_vt = sb("sg_vt", [P, 2, SEQ], stack=mixer)
        ws = sb("ws", [P, KC, P], stack=mixer)
        ws_t = sb("ws_t", [P, KC, P], stack=mixer)
        ws_b = sb("ws_b", [P, KC, P], stack=mixer)
        mixer.close()

        bank = [ctx.enter_context(nc.psum_tensor(f"bank{i}", [P, 512], F32)) for i in range(8)]
        G, S, T, O, M = bank[0:2], bank[2:4], bank[4:6], bank[6], bank[7]

        raw_landed = [sem(f"raw_landed{i}") for i in range(RAW)]
        g_free = [sem("g_free0"), sem("g_free1")]
        s_free = [sem("s_free0"), sem("s_free1")]
        t_free = [sem("t_free0"), sem("t_free1")]
        bias_landed = [sem("bias_landed0"), sem("bias_landed1")]
        hi_ready = sem("hi_ready")
        lo_ready = sem("lo_ready")
        tile_used = sem("tile_used")
        half_used = sem("half_used")
        s_full = sem("s_full")
        t_full = sem("t_full")
        o_full = sem("o_full")
        o_free = sem("o_free")
        m_full = sem("m_full")
        m_free = sem("m_free")
        par_landed = sem("par_landed")
        con_landed = sem("con_landed")
        tok_landed = sem("tok_landed")
        set_up_dve = sem("set_up_dve")
        set_up_act = sem("set_up_act")
        set_up_pool = sem("set_up_pool")
        squared = sem("squared")
        sq_added = sem("sq_added")
        rstd_rows = sem("rstd_rows")
        f_ready = sem("f_ready")
        h_hi_ready = sem("h_hi_ready")
        h_lo_ready = sem("h_lo_ready")
        renormed = sem("renormed")
        a_ready = sem("a_ready")
        bias_ready = sem("bias_ready")
        biased = sem("biased")
        max_ready = sem("max_ready")
        sum_ready = sem("sum_ready")
        th_ready = sem("th_ready")
        head_copied = sem("head_copied")
        decay_exp = sem("decay_exp")
        decay_ready = sem("decay_ready")
        decay_cut = sem("decay_cut")
        bn_step = sem("bn_step")
        ret_pow = sem("ret_pow")
        o_hi_ready = sem("o_hi_ready")
        o_lo_ready = sem("o_lo_ready")
        cos_ready = sem("cos_ready")
        rot_done = sem("rot_done")
        added = sem("added")
        m_hi_ready = sem("m_hi_ready")
        m_lo_ready = sem("m_lo_ready")
        gate_scaled = sem("gate_scaled")
        silu_ready = sem("silu_ready")
        silu_scaled = sem("silu_scaled")
        hid_ready = sem("hid_ready")
        hid_hi_ready = sem("hid_hi_ready")
        hid_lo_ready = sem("hid_lo_ready")
        ffn_out = sem("ffn_out")
        ffn_added = sem("ffn_added")
        mix_zero = sem("mix_zero")
        mix_landed = sem("mix_landed")
        mix_step = sem("mix_step")
        conv_step = sem("conv_step")
        gates_ready = sem("gates_ready")
        gated_ready = sem("gated_ready")
        decays = sem("decays")
        a_squared = sem("a_squared")
        root_in = sem("root_in")
        root_out = sem("root_out")
        bx_ready = sem("bx_ready")
        scanned = sem("scanned")
        y_ready = sem("y_ready")
        mix_ready = sem("mix_ready")
        mix_hi_ready = sem("mix_hi_ready")
        mix_lo_ready = sem("mix_lo_ready")
        v_rows = sem("v_rows")
        u_ready = sem("u_ready")
        v_normed = sem("v_normed")
        ws_cut = sem("ws_cut")
        rows_stored = sem("rows_stored")

        def evacuated(job):
            return g_free[job.n % 2], job.n // 2 + 1

        def complete(job):
            return (half_used, job.half_n + 1) if job.first_half else (tile_used, job.tile + 1)

        def s_out(use):
            return s_free[use % 2], use // 2 + 1

        def t_out(use):
            return t_free[use % 2], use // 2 + 1

        def residual_ready(up, k):
            if up.kind == "turn_in":
                return t_out(up.t_use)
            if up.kind in ("gated_residual", "plain_residual"):
                return evacuated(up.job)
            if up.kind == "normed":
                return renormed, k + 1
            if up.kind == "sg_gelu":
                return v_rows, up.c + 1
            return ffn_added, up.n + 1

        def square_of(st):
            n = st.blocks * st.norm.cols
            return sum_sq[:, 0:n] if st.first else square[:, st.slot, 0:n]

        def rstd_of(norm):
            return scaled[:, 1, 0:SEQ] if norm.how == "v" else rstd[:, 0:norm.cols]

        def g_buf(g, which):
            if which == "q":
                return q_s[:, g.slot, :]
            if g.branch in ("gqa", "gqa_kv"):
                return k_g[:, :] if which == "k" else v_g[:, :, :]
            return k_s[:, g.slot, :] if which == "k" else v_s[:, g.slot, :, :]

        def o_of(branch):
            return "b" if branch == "ret" else "a"

        def norm_weight(norm, k):
            name, row = norm.layer
            at = PARAM_AT[name] + KC * row + k
            return par[:, at:at + 1]

        def key_blocks(u):
            return range(u.key_at // P, u.key_at // P + u.keys // P)

        Q_SCALE = {"na": DH ** -0.5, "ret": 1.0}
        K_SCALE = {"na": 1.0, "ret": float(np.float32(P) ** np.float32(-0.5))}
        DECAY = 3 * P

        ffn_bank = [M, T[0], T[1], O]
        y_jobs = [st.job for st in steps if st.kind == "rec_y"]
        v_jobs = [st.job for st in steps if st.kind == "sg_v"]

        block = ctx.enter_context(nc.Block())

        @block.sync
        def _(sp):
            for t in range(RAW):
                sp.dma_start(raw[:, t, :], weights[t, :, :]).then_inc(raw_landed[t], 16)
            full = NT // RAW
            with sp.Fori(0, full - 1) as r:
                for i in range(RAW):
                    sp.wait_ge(lo_ready, r * RAW + (i + 1))
                    sp.dma_start(raw[:, i, :], weights[r * RAW + (RAW + i), :, :]).then_inc(raw_landed[i], 16)
            for t in range(full * RAW, NT):
                sp.wait_ge(lo_ready, t - RAW + 1)
                sp.dma_start(raw[:, t % RAW, :], weights[t, :, :]).then_inc(raw_landed[t % RAW], 16)
            t_uses = schedule.uses["T"]
            sp.wait_ge(t_free[0], (t_uses + 1) // 2)
            sp.wait_ge(t_free[1], t_uses // 2)
            sp.dma_start(out.rearrange("(t p) d -> p t d", p=P), rows_out[:, :, :]).then_inc(rows_stored, 16)
            sp.wait_ge(rows_stored, 16)

        @block.gpsimd
        def _(pool):
            pool.memset(eps[:, :], EPS).then_inc(set_up_pool, 1)
            pool.memset(neg_half[:, :], -0.5).then_inc(set_up_pool, 1)
            reader = [None, None]

            def bias_step(st):
                g = st.g
                slot = g.c % 2
                if reader[slot] is not None:
                    pool.wait_ge(biased, reader[slot] + 1)
                pool.dma_start(bias[:, slot, :, :], rpb[g.layer, g.c]).then_inc(bias_landed[slot], 16)
                pool.wait_ge(con_landed, 16)
                pool.wait_ge(bias_landed[slot], 16 * (st.n // 2 + 1))
                b = bias[:, slot, :, :].rearrange("p h (r c) -> p (h r) c", r=6)
                window = C_("window").unsqueeze(1).to_broadcast([P, 12, GRID_W])
                pool.tensor_tensor(b, b, window, ALU.add).then_inc(bias_ready, 1)

            def decay_step(st):
                n = st.n
                pool.wait_ge(decay_exp, 4 * n + 4)
                fwd, bwd, cross, cross_b = (decay_s[:, i, :] for i in range(4))
                pool.affine_select(out=fwd, in_=fwd, compare_op=ALU.is_ge, fill=0.0, base=-P,
                                   pattern=[[1, DECAY]], channel_multiplier=-1).then_inc(decay_cut, 1)
                pool.affine_select(out=bwd, in_=bwd, compare_op=ALU.is_ge, fill=0.0, base=P,
                                   pattern=[[-1, DECAY]], channel_multiplier=1).then_inc(decay_cut, 1)
                pool.tensor_tensor(cross, cross, cross_b, ALU.add).then_inc(decay_ready, 1)
                pool.wait_ge(decay_cut, 2 * n + 2)
                pool.tensor_tensor(fwd, fwd, bwd, ALU.add).then_inc(decay_ready, 1)

            def ret_out_step(st):
                nb = st.g.blocks
                pool.wait_ge(bn_step, st.bn_at + 2 * nb + 1)
                half = neg_half[:, 0:1].to_broadcast([P, nb])
                pool.tensor_tensor(ret_rs[:, 0:nb], ret_rs[:, 0:nb], half, ALU.pow).then_inc(ret_pow, 1)

            def rotate_step(st):
                pool.wait_ge(m_free, st.norm.spread.m + 1)
                dst = g_buf(st.g, "k" if st.what == "key" else "q")
                pool.tensor_tensor(head_rows[:, st.n % 2, 0:SEQ], dst[:, 0:SEQ], C_("cos"), ALU.mult).then_inc(cos_ready, 1)

            def merge_step(st):
                if st.br == 0:
                    return
                pool.wait_ge(*evacuated(st.job))
                v = m[:, st.dc, 0:st.cols]
                pool.tensor_tensor(v, v, branch_sum[:, st.dc % 2, 0:st.cols], ALU.add).then_inc(added, 1)

            def row_rstd_of(m, n):
                pool.wait_ge(m_free, m + 1)
                pool.tensor_tensor(row_rstd[:, 0:n], row_mean[:, 0:n], neg_half[:, 0:1].to_broadcast([P, n]), ALU.pow)\
                    .then_inc(rstd_rows, 1)

            def rms_step(st):
                row_rstd_of(st.norm.m, st.norm.cols // P)

            def head_norm_step(st):
                row_rstd_of(st.m, 2 * st.cols // P)

            def square_step(st):
                if st.first or st.last:
                    return
                pool.wait_ge(squared, st.n + 1)
                n = st.blocks * st.norm.cols
                if st.add_n:
                    pool.wait_ge(sq_added, st.add_n)
                pool.tensor_tensor(sum_sq[:, 0:n], sum_sq[:, 0:n], square_of(st), ALU.add).then_inc(sq_added, 1)

            def ffn_step(st):
                mixer_parameters(st)
                f = st.n
                row_rstd_of(st.norm.m, SEQ // P)
                pool.wait_ge(m_free, st.norm.m_spread + 1)

                def scale_silu(i, r=None):
                    cnt = 0 if r is None else r * ROUND
                    pool.wait_ge(silu_ready, cnt + (FC * f + i + 1))
                    v = silu_g[:, i % 2, :]
                    pool.tensor_tensor(v, v, rstd[:, 0:SEQ], ALU.mult).then_inc(silu_scaled, 1)

                scale_silu(0)
                scale_silu(1)
                with pool.Fori(0, (FC - 2) // ROUND) as r:
                    for i in range(2, ROUND + 2):
                        scale_silu(i, r)
                if f == 2:
                    pool.wait_ge(mix_landed, 6 * 16)
                    pool.affine_select(out=ws[:, :, :], in_=ws[:, :, :], compare_op=ALU.is_ge, fill=0.0, base=0,
                                       pattern=[[0, KC], [-1, P]], channel_multiplier=1).then_inc(ws_cut, 1)

            def mixer_parameters(st):
                if st.n % 2:
                    return
                pool.wait_ge(h_lo_ready, st.norm.chunks[KC - 1].h + 1)
                if st.n == 0:
                    pool.memset(gate_w[:, :, :, :], 0.0).then_inc(mix_zero, 1)
                    pool.wait_ge(mix_zero, 1)
                    for i, w in enumerate((gate_a, gate_x)):
                        halves = w.rearrange("(n two) i j -> two i n j", two=2)
                        for j in range(2):
                            at = slice(DH * j, DH * j + DH)
                            pool.dma_start(gate_w[at, i, :, at], halves[j]).then_inc(mix_landed, 16)
                else:
                    pool.dma_start(ws[:, :, :], spatial.rearrange("h p q -> p h q")).then_inc(mix_landed, 16)
                    rows = spatial_b.rearrange("h p -> (h p)").partition_broadcast(P)
                    pool.dma_start(ws_b[:, :, :].rearrange("p h q -> p (h q)"), rows).then_inc(mix_landed, 16)

            def rec_gates_step(st):
                pool.wait_ge(*s_out(st.s_use))
                v = g_x[:, st.c, :]
                pool.tensor_tensor(v, v, r_conv[:, st.c, :], ALU.mult).then_inc(gated_ready, 1)

            def rec_decay_step(st):
                pool.wait_ge(decays, 2 * st.c + 2)
                if st.c >= 2:
                    pool.wait_ge(root_in, st.c - 1)
                pool.tensor_tensor(mix_t[:, st.c % 2, :], g_a[:, st.c, :], g_a[:, st.c, :], ALU.mult)\
                    .then_inc(a_squared, 1)

            def rec_root_step(st):
                pool.wait_ge(root_out, st.n + 1)
                pool.wait_ge(gated_ready, st.n + 1)
                v = g_x[:, st.c, :]
                pool.tensor_tensor(v, v, th[:, st.c, :], ALU.mult).then_inc(bx_ready, 1)

            run = {"square": square_step, "rms": rms_step, "head_norm": head_norm_step, "bias": bias_step, "decay": decay_step, "ret_out": ret_out_step, 
                   "rotate": rotate_step, "merge": merge_step,
                   "ffn": ffn_step, "rec_gates": rec_gates_step, "rec_decay": rec_decay_step, "rec_root": rec_root_step}
            for st in steps:
                if st.kind == "scores" and st.u.bias:
                    reader[st.u.g.c % 2] = st.u.bias_n
                if st.kind in run:
                    run[st.kind](st)

        @block.scalar
        def _(act):
            act.dma_start(par[:, :], params).then_inc(par_landed, 16)
            act.dma_start(con[:, :], consts).then_inc(con_landed, 16)
            rows = tokens.rearrange("(t p) d -> p t d", p=P)
            for i in range(2):
                act.dma_start(tok[:, 2 * i:2 * i + 2, :], rows[:, 2 * i:2 * i + 2, :]).then_inc(tok_landed, 16)
            act.wait_ge(par_landed, 16)
            nc.scalar.activation(c_silu[:, :, 0], P_("c"), ACT.Silu).then_inc(set_up_act, 1)
            nc.scalar.activation(c_silu[:, :, 1], P_("c_ctx"), ACT.Silu).then_inc(set_up_act, 1)
            act.wait_ge(set_up_act, 2)
            nc.scalar.activation(c_split[:, :, 0:2], c_silu[:, :, :], ACT.Copy).then_inc(set_up_act, 1)
            nc.scalar.activation(log_g[:, 0, :], P_("decay"), ACT.Exp).then_inc(set_up_act, 1)
            nc.scalar.activation(lam[:, 0, :], P_("rec_lambda"), ACT.Abs).then_inc(set_up_act, 1)
            act.wait_ge(set_up_act, 5)
            nc.scalar.activation(lam[:, 1, :], lam[:, 0, :], ACT.Exp, scale=-1.0).then_inc(set_up_act, 1)
            act.wait_ge(set_up_act, 6)
            act.wait_ge(set_up_dve, 1)
            nc.scalar.activation(lam[:, 0, :], lam[:, 1, :], ACT.Ln, bias=lam[:, 2, 0:1]).then_inc(set_up_act, 1)
            last = {"gate": None, "decay": None}

            def split_step(st):
                split(st.t, None)

            def ada_rows_step(st):
                u = st.u
                if u.n:
                    act.wait_ge(m_full, last["section"].m + 1)
                last["section"] = u
                for j, use in enumerate(u.t_uses):
                    if j == 0:
                        act.wait_ge(t_full, use + 1)
                    else:
                        act.wait_ge(tile_used, u.tile + 1)
                    nc.scalar.activation(ada_rows[u.n >= len(ADA_FIRST)][:, 512 * j:512 * j + 512],
                                         T[use % 2][0:4, :], ACT.Copy).then_inc(t_free[use % 2], 1)

            def split(t, r):
                if r is None and t >= NT:
                    return
                base, landed = (0, 0) if r is None else (r * (3 * ROUND), r * (16 * 3 * ROUND // RAW))
                act.wait_ge(raw_landed[t % RAW], landed + 16 * (t // RAW + 1))
                if t >= SPLIT:
                    act.wait_ge(tile_used, base + (t - SPLIT + 1))
                nc.scalar.activation(w_hi[:, t % SPLIT, :], raw[:, t % RAW, :], ACT.Copy).then_inc(hi_ready, 1)

            def turn_in_step(st):
                if st.k % 2:
                    return
                act.wait_ge(t_full, st.t_use + 1)
                nc.scalar.activation(x[:, st.k, :], T[st.t_use % 2][:, :], ACT.Copy).then_inc(t_free[st.t_use % 2], 1)

            def square_step(st):
                act.wait_ge(*residual_ready(st.up, st.k))
                if st.before is not None:
                    act.wait_ge(sq_added, st.before.add_n + 1)
                c, n = st.norm.cols, st.blocks
                src = sg_v[:, st.k:st.k + n, :] if st.norm.how == "v" else x[:, st.k:st.k + n, 0:c]
                nc.scalar.activation(square_of(st).rearrange("p (a b) -> p a b", a=n), src, ACT.Square)\
                    .then_inc(squared, 1)

            def split_x_step(st):
                act.wait_ge(*residual_ready(st.up, st.k))
                nc.scalar.activation(h_hi[:, st.k, 0:SEQ], x[:, st.k, 0:SEQ], ACT.Copy, scale=norm_weight(st.norm, st.k))\
                    .then_inc(h_hi_ready, 1)

            def normed_step(st):
                norm, k = st.norm, st.k
                if norm.how == "out":
                    act.wait_ge(t_full, st.t_use + 1)
                    nc.scalar.activation(rows_out[:, :, P * k:P * k + P],
                                         T[st.t_use % 2][:, 0:SEQ].rearrange("p (t d) -> p t d", t=2), ACT.Copy)\
                        .then_inc(t_free[st.t_use % 2], 1)
                if norm.how != "ada":
                    return
                act.wait_ge(f_ready, st.f + 1)
                for j in range(2):
                    at = slice(SEQ * j, SEQ * j + SEQ)
                    ins = nc.scalar.activation(h_hi[:, k, at], scaled[:, k % 2, at], ACT.Identity,
                                               bias=ada[:, norm.layer, k, j:j + 1])
                ins.then_inc(h_hi_ready, 1)

            def evacuate_step(st):
                g, n = st.g, st.job.cols
                act.wait_ge(*complete(st.job))
                dst = g_buf(g, "q" if st.what == "query" else "k")
                scale = (Q_SCALE if st.what == "query" else K_SCALE)[g.branch]
                nc.scalar.activation(dst[:, 0:n], G[st.job.n % 2][:, 0:n], ACT.Copy, scale=scale)\
                    .then_inc(g_free[st.job.n % 2], 1)

            def value_rows_step(st):
                act.wait_ge(*complete(st.job))
                nc.scalar.activation(stage[:, :], G[st.job.n % 2][:, :], ACT.Copy).then_inc(g_free[st.job.n % 2], 1)

            def gate_step(st):
                act.wait_ge(*complete(st.job))
                if last["gate"] is not None:
                    act.wait_ge(*evacuated(last["gate"].job))
                last["gate"] = st
                nc.scalar.activation(half_tanh[:, 0:st.cols], G[st.job.n % 2][:, 0:st.cols], ACT.Tanh, scale=0.5)\
                    .then_inc(th_ready, 1)

            def merge_gate_step(st):
                act.wait_ge(*complete(st.job))
                if st.before is not None:
                    act.wait_ge(*evacuated(st.before.job))
                nc.scalar.activation(merge_tanh[:, st.slot, 0:st.cols], G[st.job.n % 2][:, 0:st.cols], ACT.Tanh,
                                     scale=0.5).then_inc(g_free[st.job.n % 2], 1)

            def merge_step(st):
                if st.br < 2:
                    return
                act.wait_ge(added, st.add_n + 1)
                nc.scalar.activation(m_hi[:, st.dc, 0:st.cols], m[:, st.dc, 0:st.cols], ACT.Copy, scale=0.5)\
                    .then_inc(m_hi_ready, 1)

            def scores_step(st):
                u = st.u
                act.wait_ge(max_ready, u.n + 1)
                nc.scalar.activation(probs[:, u.n % 2, 0:u.keys], S[u.s_use % 2][:, 0:u.keys], ACT.Exp,
                                     bias=row_stat[:, 0, u.n % 4:u.n % 4 + 1],
                                     accum_out=row_stat[:, 1, u.n % 4:u.n % 4 + 1]).then_inc(s_free[u.s_use % 2], 1)

            def turn_probs_step(st):
                u = st.u
                act.wait_ge(t_full, u.t_use + 1)
                nc.scalar.activation(probs_t[:, u.n % 2, 0:u.keys], T[u.t_use % 2][:, 0:u.keys], ACT.Copy)\
                    .then_inc(t_free[u.t_use % 2], 1)

            def turn_out_step(st):
                g = st.g
                act.wait_ge(m_free, st.m + 1)
                nc.scalar.activation(o_hi[o_of(g.branch)][:, g.c, 0:g.live], gated[:, 0:g.live], ACT.Copy)\
                    .then_inc(o_hi_ready, 1)

            def decay_step(st):
                g = st.g
                if last["decay"] is not None:
                    act.wait_ge(*s_out(last["decay"].last_scores.s_use))
                last["decay"] = g
                if st.n == 0:
                    act.wait_ge(con_landed, 16)
                    nc.scalar.activation(abs_dif[:, :], C_("dif"), ACT.Abs).then_inc(set_up_act, 1)
                f, b = g.layer * 8 + g.c, g.layer * 8 + 4 + g.c
                act.wait_ge(set_up_dve, 5)
                act.wait_ge(set_up_act, 8)

                def lg(kind, i):
                    return log_g[:, kind, i:i + 1]

                nc.scalar.activation(decay_s[:, 0, :], abs_dif[:, :], ACT.Exp, scale=lg(0, f)).then_inc(decay_exp, 1)
                nc.scalar.activation(decay_s[:, 1, :], abs_dif[:, :], ACT.Exp, scale=lg(0, b)).then_inc(decay_exp, 1)
                nc.scalar.activation(decay_s[:, 2, :], C_("dif"), ACT.Exp, scale=lg(0, f), bias=lg(2, f))\
                    .then_inc(decay_exp, 1)
                nc.scalar.activation(decay_s[:, 3, :], C_("dif"), ACT.Exp, scale=lg(1, b), bias=lg(2, b))\
                    .then_inc(decay_exp, 1)

            def head_evacuate_step(st):
                n = st.cols
                act.wait_ge(*complete(st.job))
                if st.n >= 1:
                    act.wait_ge(rot_done, st.n)
                nc.scalar.activation(head_rows[:, st.n % 2, 0:n], G[st.job.n % 2][:, 0:n], ACT.Copy)\
                    .then_inc(head_copied, 1)
                nc.scalar.activation(head_sq[:, 0:n], G[st.job.n % 2][:, 0:n], ACT.Square)\
                    .then_inc(g_free[st.job.n % 2], 1)

            def ffn_step(st):
                f, t0 = st.n, st.t

                def silu(i, r=None):
                    cnt = 0 if r is None else r * ROUND
                    act.wait_ge(gate_scaled, cnt + (FC * f + i + 1))
                    nc.scalar.activation(silu_g[:, i % 2, :], silu_g[:, i % 2, :], ACT.Silu).then_inc(silu_ready, 1)

                def hid(i, r=None):
                    cnt = 0 if r is None else r * ROUND
                    act.wait_ge(hid_ready, cnt + (FC * f + i + 1))
                    nc.scalar.activation(hid_hi[:, i % 2, :], hidden[:, i % 2, :], ACT.Copy).then_inc(hid_hi_ready, 1)

                def round_(i, r=None):
                    a = t0 + AHEAD + 3 * i
                    split(a + 2, r)
                    hid(i, r)
                    split(a + 3, r)
                    silu(i + 1, r)
                    split(a + 4, r)

                split(t0 + AHEAD, None)
                split(t0 + AHEAD + 1, None)
                silu(0)
                round_(0)
                peeled = ROUND if t0 + 3 * FC == NT else 0
                with act.Fori(0, (FC - 2 - peeled) // ROUND) as r:
                    for i in range(1, ROUND + 1):
                        round_(i, r)
                for i in range(FC - 1 - peeled, FC - 1):
                    round_(i)
                hid(FC - 1)
                split(t0 + 3 * FC - 1 + AHEAD, None)

            def rec_gates_step(st):
                act.wait_ge(s_full, st.s_use + 1)
                b = S[st.s_use % 2]
                at_a, at_x = PARAM_AT["rec_gate_a_b"] + st.c, PARAM_AT["rec_gate_x_b"] + st.c
                nc.scalar.activation(g_a[:, st.c, :], b[:, 0:SEQ], ACT.Sigmoid, bias=par[:, at_a:at_a + 1])\
                    .then_inc(gates_ready, 1)
                nc.scalar.activation(g_x[:, st.c, :], b[:, SEQ:BOTH], ACT.Sigmoid, bias=par[:, at_x:at_x + 1])\
                    .then_inc(s_free[st.s_use % 2], 1)

            def rec_decay_step(st):
                act.wait_ge(gates_ready, st.c + 1)
                act.wait_ge(set_up_dve, 10)
                scale = lam[:, 0, st.c:st.c + 1]
                nc.scalar.activation(th[:, st.c, :], g_a[:, st.c, :], ACT.Tanh, scale=scale).then_inc(decays, 1)
                act.wait_ge(decays, 2 * st.c + 1)
                nc.scalar.activation(g_a[:, st.c, :], g_a[:, st.c, :], ACT.Exp, scale=scale).then_inc(decays, 1)

            def rec_root_step(st):
                act.wait_ge(root_in, st.n + 1)
                nc.scalar.activation(th[:, st.c, :], th[:, st.c, :], ACT.Sqrt, scale=-1.0).then_inc(root_out, 1)

            def rec_out_step(st):
                act.wait_ge(*evacuated(y_jobs[st.c]))
                nc.scalar.activation(y_act[:, st.c, :], y_act[:, st.c, :], ACT.Gelu_apprx_tanh).then_inc(y_ready, 1)
                mix_split(st.c, st.n)

            def mix_split(c, n):
                act.wait_ge(mix_ready, n + 1)
                nc.scalar.activation(mix_hi[:, c, :], mix_t[:, n % 2, :], ACT.Copy).then_inc(mix_hi_ready, 1)

            def sg_gelu_step(st):
                act.wait_ge(*evacuated(v_jobs[st.c]))
                v = sg_v[:, st.c, :]
                nc.scalar.activation(v, v, ACT.Gelu_apprx_tanh).then_inc(v_rows, 1)

            def sg_u_gelu_step(st):
                act.wait_ge(*evacuated(st.job))
                v = sg_u[:, st.c, :]
                nc.scalar.activation(v, v, ACT.Gelu_apprx_tanh).then_inc(u_ready, 1)

            def sg_turn_step(st):
                act.wait_ge(t_full, st.t_use + 1)
                nc.scalar.activation(sg_vt[:, st.c % 2, :], T[st.t_use % 2][:, 0:SEQ], ACT.Copy)\
                    .then_inc(t_free[st.t_use % 2], 1)

            def sg_mix_step(st):
                mix_split(st.c, KC + st.n)

            run = {"split": split_step, "ada_rows": ada_rows_step, "turn_in": turn_in_step, "square": square_step,
                   "normed": normed_step, "evacuate": evacuate_step, "value_rows": value_rows_step,
                   "gate": gate_step, "merge_gate": merge_gate_step, "merge": merge_step, "scores": scores_step,
                   "turn_probs": turn_probs_step, "turn_out": turn_out_step, "decay": decay_step,
                   "head_evacuate": head_evacuate_step, "ffn": ffn_step,
                   "rec_gates": rec_gates_step, "split_x": split_x_step, "rec_decay": rec_decay_step, "rec_root": rec_root_step,
                   "rec_out": rec_out_step, "sg_gelu": sg_gelu_step, "sg_u_gelu": sg_u_gelu_step, "sg_turn": sg_turn_step,
                   "sg_mix": sg_mix_step}
            for st in steps:
                if st.kind in run:
                    run[st.kind](st)

        @block.vector
        def _(dve):
            dve.memset(lam[:, 2, 0:1], 1.0).then_inc(set_up_dve, 1)
            dve.wait_ge(set_up_act, 4)
            dve.tensor_tensor(c_split[:, :, 2:4], c_silu[:, :, :], c_split[:, :, 0:2].bitcast(F32), ALU.subtract)\
                .then_inc(set_up_dve, 1)
            dve.tensor_scalar(log_g[:, 1, :], log_g[:, 0, :], 1.0, None, ALU.mult).then_inc(set_up_dve, 1)
            dve.tensor_scalar(log_g[:, 2, :], log_g[:, 0, :], -256.0, None, ALU.mult).then_inc(set_up_dve, 1)
            dve.wait_ge(set_up_dve, 4)
            dve.tensor_scalar(log_g[:, 0, :], log_g[:, 0, :], -1.0, None, ALU.mult).then_inc(set_up_dve, 1)
            dve.tensor_scalar(gn_half[:, :], P_("ret_gn_w"), 0.5, None, ALU.mult).then_inc(set_up_dve, 1)
            dve.tensor_scalar(q_norm[:, :], P_("q_norm_w"), DH ** -0.5, None, ALU.mult).then_inc(set_up_dve, 1)
            dve.wait_ge(set_up_act, 7)
            dve.tensor_scalar(lam[:, 1, :], P_("rec_lambda"), -1.0, 0.0, ALU.mult, ALU.max).then_inc(set_up_dve, 1)
            dve.wait_ge(set_up_dve, 8)
            dve.tensor_tensor(lam[:, 1, :], lam[:, 1, :], lam[:, 0, :], ALU.add).then_inc(set_up_dve, 1)
            dve.wait_ge(set_up_dve, 9)
            dve.tensor_scalar(lam[:, 0, :], lam[:, 1, :], -8.0, None, ALU.mult).then_inc(set_up_dve, 1)

            def split(t, r=None):
                if r is None and t >= NT:
                    return
                base = 0 if r is None else r * (3 * ROUND)
                dve.wait_ge(hi_ready, base + (t + 1))
                dve.tensor_tensor(w_lo[:, t % SPLIT, :], raw[:, t % RAW, :], w_hi[:, t % SPLIT, :].bitcast(F32),
                                  ALU.subtract).then_inc(lo_ready, 1)

            def turn_in_step(st):
                if st.k % 2 == 0:
                    return
                dve.wait_ge(t_full, st.t_use + 1)
                dve.tensor_copy(x[:, st.k, :], T[st.t_use % 2][:, :]).then_inc(t_free[st.t_use % 2], 1)

            def ada_turn_step(st):
                u = st.u
                at = PARAM_AT["ada_b"] + 24 * u.layer + KC * u.c
                dve.wait_ge(m_full, u.m + 1)
                dve.wait_ge(par_landed, 16)
                b = par[:, at:at + KC].unsqueeze(2).to_broadcast([P, KC, 2])
                dve.tensor_tensor(ada[:, u.layer, KC * u.c:KC * u.c + KC, :],
                                  M[:, 0:2 * KC].rearrange("p (k j) -> p k j", j=2), b, ALU.add).then_inc(m_free, 1)
                if u.c == 1:
                    ada_m[u.layer] = u.m + 1

            ada_m = [0, 0]

            def ada_scale_step(st):
                at = PARAM_AT["norm_w"] + KC * st.layer
                dve.wait_ge(m_free, ada_m[st.layer])
                for j in range(2):
                    dve.scalar_tensor_tensor(out=ada_a[:, :, j], in0=ada[:, st.layer, KC:2 * KC, j], scalar=1.0,
                                             in1=par[:, at:at + KC], op0=ALU.add, op1=ALU.mult).then_inc(a_ready, 1)

            def rms_step(st):
                norm = st.norm
                mean_rows_of(norm.m, norm.rows, norm.cols // P)
                dve.wait_ge(m_full, norm.m_spread + 1)
                dve.tensor_copy(rstd_of(norm), M[:, 0:norm.cols]).then_inc(m_free, 1)

            def mean_rows_of(m, rows, n):
                dve.wait_ge(m_full, m + 1)
                if rows:
                    dve.wait_ge(rstd_rows, rows)
                dve.tensor_scalar(row_mean[:, 0:n], M[:, 0:n], EPS, None, ALU.add).then_inc(m_free, 1)

            def split_x_step(st):
                k = st.k
                dve.wait_ge(*residual_ready(st.up, k))
                dve.wait_ge(h_hi_ready, st.h + 1)
                dve.scalar_tensor_tensor(out=h_lo[:, k, 0:SEQ], in0=x[:, k, 0:SEQ], scalar=norm_weight(st.norm, k),
                                         in1=h_hi[:, k, 0:SEQ].bitcast(F32), op0=ALU.mult, op1=ALU.subtract)\
                    .then_inc(h_lo_ready, 1)

            def scaled_product(st, dst, norm=None):
                if norm is not None:
                    dve.wait_ge(m_free, norm.m_spread + 1)
                dve.wait_ge(*complete(st.job))
                dve.tensor_tensor(dst, G[st.job.n % 2][:, 0:SEQ], rstd[:, 0:SEQ], ALU.mult)\
                    .then_inc(g_free[st.job.n % 2], 1)

            def rec_y_step(st):
                scaled_product(st, y_act[:, st.c, :])

            def sg_v_step(st):
                scaled_product(st, sg_v[:, st.c, :], st.norm)

            def sg_u_step(st):
                scaled_product(st, sg_u[:, st.c, :])

            def normed_step(st):
                norm, k, c = st.norm, st.k, st.norm.cols
                if k == 0:
                    dve.wait_ge(m_free, norm.m_spread + 1)
                if st.h is not None and k >= 2:
                    dve.wait_ge(h_lo_ready, st.h - 1)
                if norm.how == "ada":
                    if k == 0:
                        dve.wait_ge(a_ready, 2 * norm.layer + 2)
                    for j in range(2):
                        at = slice(SEQ * j, SEQ * j + SEQ)
                        ins = dve.scalar_tensor_tensor(out=scaled[:, k % 2, at], in0=x[:, k, at],
                                                       scalar=ada_a[:, k, j:j + 1], in1=rstd[:, at],
                                                       op0=ALU.mult, op1=ALU.mult)
                    ins.then_inc(f_ready, 1)
                elif norm.how == "out":
                    if k >= 2:
                        dve.wait_ge(t_full, st.t_use - 1)
                    dve.scalar_tensor_tensor(out=scaled[:, k % 2, 0:c], in0=x[:, k, 0:c], scalar=norm_weight(norm, k),
                                             in1=rstd[:, 0:c], op0=ALU.mult, op1=ALU.mult).then_inc(f_ready, 1)
                    return
                elif norm.how == "residual":
                    dve.scalar_tensor_tensor(out=x[:, k, 0:SEQ], in0=x[:, k, 0:SEQ], scalar=norm_weight(norm, k),
                                             in1=rstd[:, 0:SEQ], op0=ALU.mult, op1=ALU.mult).then_inc(renormed, 1)
                    return
                else:
                    dve.scalar_tensor_tensor(out=sg_v[:, k, :], in0=sg_v[:, k, :], scalar=norm_weight(norm, k),
                                             in1=rstd_of(norm), op0=ALU.mult, op1=ALU.mult).then_inc(v_normed, 1)
                    return

                if k >= 1:
                    h_low(norm.chunks[k - 1], c)
                if k == KC - 1:
                    h_low(st, c)

            def h_low(st, c):
                dve.wait_ge(h_hi_ready, st.h + 1)
                for j in range(2):
                    at = slice(SEQ * j, SEQ * j + SEQ)
                    ins = dve.scalar_tensor_tensor(out=h_lo[:, st.k, at], in0=scaled[:, st.k % 2, at],
                                                   scalar=ada[:, st.norm.layer, st.k, j:j + 1],
                                                   in1=h_hi[:, st.k, at].bitcast(F32), op0=ALU.add, op1=ALU.subtract)
                ins.then_inc(h_lo_ready, 1)

            def value_turn_step(st):
                dve.wait_ge(m_full, st.m + 1)
                dve.tensor_copy(g_buf(st.g, "v"), M[:, :].rearrange("p (t d) -> p t d", t=4)).then_inc(m_free, 1)

            def gate_step(st):
                th_count[0] += 1
                dve.wait_ge(th_ready, th_count[0])
                if turned[st.g.slot]:
                    dve.wait_ge(m_free, turned[st.g.slot])
                dve.scalar_tensor_tensor(out=branch_gate[:, st.g.slot, 0:st.cols], in0=half_tanh[:, 0:st.cols],
                                         scalar=1.0, in1=G[st.job.n % 2][:, 0:st.cols], op0=ALU.add, op1=ALU.mult)\
                    .then_inc(g_free[st.job.n % 2], 1)

            th_count = [0]
            turned = [0, 0]

            def merge_step(st):
                c = st.cols
                dve.wait_ge(*complete(st.job))
                dve.wait_ge(*evacuated(st.gate.job))
                if st.br and st.add_n >= 2:
                    dve.wait_ge(added, st.add_n - 1)
                dst = m[:, st.dc, 0:c] if st.br == 0 else branch_sum[:, st.dc % 2, 0:c]
                dve.scalar_tensor_tensor(out=dst, in0=merge_tanh[:, st.dc % 2, 0:c], scalar=1.0,
                                         in1=G[st.job.n % 2][:, 0:c], op0=ALU.add, op1=ALU.mult)\
                    .then_inc(g_free[st.job.n % 2], 1)
                if st.br == 2:
                    dve.wait_ge(m_hi_ready, st.m_n + 1)
                    dve.scalar_tensor_tensor(out=m_lo[:, st.dc, 0:c], in0=m[:, st.dc, 0:c], scalar=0.5,
                                             in1=m_hi[:, st.dc, 0:c].bitcast(F32), op0=ALU.mult,
                                             op1=ALU.subtract).then_inc(m_lo_ready, 1)

            def gated_residual_step(st):
                dve.wait_ge(*complete(st.job))
                halves = range(2 if st.cols == BOTH else 1)
                for j in halves:
                    at = slice(SEQ * j, SEQ * j + SEQ)
                    v = x[:, st.dc, at]
                    ins = dve.scalar_tensor_tensor(out=v, in0=G[st.job.n % 2][:, at],
                                                   scalar=ada[:, st.layer, 16 + st.dc, j:j + 1], in1=v,
                                                   op0=ALU.mult, op1=ALU.add)
                ins.then_inc(g_free[st.job.n % 2], 1)

            def plain_residual_step(st):
                dve.wait_ge(*complete(st.job))
                v = x[:, st.dc, 0:SEQ]
                dve.tensor_tensor(v, G[st.job.n % 2][:, 0:SEQ], v, ALU.add).then_inc(g_free[st.job.n % 2], 1)

            def scores_step(st):
                u = st.u
                s = S[u.s_use % 2]
                dve.wait_ge(s_full, u.s_use + 1)
                if u.bias:
                    dve.wait_ge(bias_ready, u.g.bias.n + 1)
                    row = (2 - 2 * u.b) * GRID_W
                    dve.tensor_tensor(s[:, 0:SEQ], s[:, 0:SEQ], bias[:, u.g.c % 2, u.hp, row:row + SEQ], ALU.add)\
                        .then_inc(biased, 1)
                    dve.wait_ge(biased, u.bias_n + 1)
                dve.tensor_reduce(row_stat[:, 0, u.n % 4:u.n % 4 + 1], s[:, 0:u.keys], AX_X, ALU.max, negate=True)\
                    .then_inc(max_ready, 1)

            def turn_probs_step(st):
                u = st.u
                dve.wait_ge(*s_out(u.s_use))
                dve.reciprocal(row_stat[:, 2, u.n % 4:u.n % 4 + 1], row_stat[:, 1, u.n % 4:u.n % 4 + 1])\
                    .then_inc(sum_ready, 1)

            def values_step(st):
                u = st.u
                dve.wait_ge(o_full, u.o_use + 1)
                dve.wait_ge(sum_ready, u.n + 1)
                dve.tensor_scalar(out_rows[:, u.b, DH * u.hp:DH * u.hp + DH], O[:, 0:DH],
                                  row_stat[:, 2, u.n % 4:u.n % 4 + 1], None, ALU.mult).then_inc(o_free, 1)

            def turn_out_step(st):
                g = st.g
                dve.wait_ge(m_full, st.m + 1)
                dve.wait_ge(*evacuated(g.gate.job))
                if st.n:
                    dve.wait_ge(o_lo_ready, st.n)
                turned[g.slot] = st.m + 1
                scale = gn_half[:, 4 * g.layer + g.c:4 * g.layer + g.c + 1] if g.branch == "ret" else 0.5
                dve.scalar_tensor_tensor(out=gated[:, 0:g.live], in0=M[:, 0:g.live], scalar=scale,
                                         in1=branch_gate[:, g.slot, 0:g.live], op0=ALU.mult, op1=ALU.mult)\
                    .then_inc(m_free, 1)
                o = o_of(g.branch)
                dve.wait_ge(o_hi_ready, st.n + 1)
                dve.tensor_tensor(o_lo[o][:, g.c, 0:g.live], gated[:, 0:g.live],
                                  o_hi[o][:, g.c, 0:g.live].bitcast(F32), ALU.subtract).then_inc(o_lo_ready, 1)

            def ret_scores_step(st):
                g, s = st.g, S[st.s_use % 2]
                dve.wait_ge(s_full, st.s_use + 1)
                dve.wait_ge(decay_ready, 2 * g.decay.n + 2)
                at = P * (1 - st.j % 2)
                own, cross = decay_s[:, 0, at:at + SEQ], decay_s[:, 2, at:at + SEQ]
                ins = dve.tensor_tensor(work[:, st.j, 0:SEQ], s[:, 0:SEQ], own if st.j < 2 else cross, ALU.mult)
                if st.cols == BOTH:
                    ins = dve.tensor_tensor(work[:, st.j, SEQ:BOTH], s[:, SEQ:BOTH], own, ALU.mult)
                ins.then_inc(s_free[st.s_use % 2], 1)

            def ret_out_step(st):
                nb = st.g.blocks
                dve.wait_ge(o_full, st.o_use + 1)
                for b in range(nb):
                    dve.bn_stats(bn[:, b, :], O[:, P * b:P * b + P]).then_inc(bn_step, 1)
                for b in range(nb):
                    dve.wait_ge(bn_step, st.bn_at + b + 1)
                    dve.bn_aggr(mean_var[:, b, :], bn[:, b, :]).then_inc(bn_step, 1)
                dve.wait_ge(bn_step, st.bn_at + 2 * nb)
                dve.tensor_scalar(ret_rs[:, 0:nb], mean_var[:, 0:nb, 1], EPS, None, ALU.add).then_inc(bn_step, 1)
                dve.wait_ge(ret_pow, st.n + 1)
                for b in range(nb):
                    ins = dve.tensor_scalar(out_rows[:, b, :], O[:, P * b:P * b + P],
                                            mean_var[:, b, 0:1], ret_rs[:, b:b + 1], ALU.subtract, ALU.mult)
                ins.then_inc(o_free, 1)

            def head_norm_step(st):
                mean_rows_of(st.m, st.rows, 2 * st.cols // P)

            def head_spread_step(st):
                n, norm = st.cols, st.norm
                dst = g_buf(st.g, "k" if st.what == "key" else "q")
                at = PARAM_AT["k_norm_w"] + st.g.layer
                w = par[:, at:at + 1] if st.what == "key" else q_norm[:, st.g.layer:st.g.layer + 1]
                dve.wait_ge(m_full, st.m + 1)
                dve.wait_ge(head_copied, norm.n + 1)
                dve.scalar_tensor_tensor(out=dst[:, 0:n], in0=head_rows[:, norm.n % 2, 0:n], scalar=w, in1=M[:, 0:n],
                                         op0=ALU.mult, op1=ALU.mult).then_inc(m_free, 1)

            def rotate_step(st):
                dst = g_buf(st.g, "k" if st.what == "key" else "q")
                dve.wait_ge(m_full, st.m + 1)
                dve.tensor_tensor(head_sq[:, 0:SEQ], M[:, 0:SEQ], C_("sin"), ALU.mult).then_inc(m_free, 1)
                dve.wait_ge(cos_ready, st.n + 1)
                dve.wait_ge(m_free, st.m + 1)
                dve.tensor_tensor(dst[:, 0:SEQ], head_rows[:, st.n % 2, 0:SEQ], head_sq[:, 0:SEQ], ALU.add).then_inc(rot_done, 1)

            def ffn_step(st):
                f, t0 = st.n, st.t

                def gate(i, r=None):
                    cnt, up = (0, 0) if r is None else (r * ROUND, r * (3 * ROUND))
                    dve.wait_ge(tile_used, up + (t0 + ffn_tile("g", i) + 1))
                    if i >= 2:
                        dve.wait_ge(hid_ready, cnt + (FC * f + i - 1))
                    dve.tensor_tensor(silu_g[:, i % 2, :], G[i % 2][:, 0:SEQ], rstd[:, 0:SEQ], ALU.mult)\
                        .then_inc(gate_scaled, 1)

                def mult(i, r=None):
                    cnt, up = (0, 0) if r is None else (r * ROUND, r * (3 * ROUND))
                    dve.wait_ge(silu_scaled, cnt + (FC * f + i + 1))
                    dve.wait_ge(tile_used, up + (t0 + ffn_tile("u", i) + 1))
                    if i >= 2:
                        dve.wait_ge(hid_lo_ready, cnt + (FC * f + i - 1))
                    dve.tensor_tensor(hidden[:, i % 2, :], silu_g[:, i % 2, :], S[i % 2][:, 0:SEQ], ALU.mult)\
                        .then_inc(hid_ready, 1)

                def low(i, r=None):
                    cnt = 0 if r is None else r * ROUND
                    dve.wait_ge(hid_hi_ready, cnt + (FC * f + i + 1))
                    dve.tensor_tensor(hid_lo[:, i % 2, :], hidden[:, i % 2, :], hid_hi[:, i % 2, :].bitcast(F32),
                                      ALU.subtract).then_inc(hid_lo_ready, 1)

                def round_(i, r=None):
                    a = t0 + AHEAD + 3 * i
                    split(a + 2, r)
                    low(i, r)
                    split(a + 3, r)
                    gate(i + 1, r)
                    mult(i + 1, r)
                    split(a + 4, r)

                split(t0 + AHEAD)
                rms_step(st)
                split(t0 + AHEAD + 1)
                dve.wait_ge(m_free, st.norm.m_spread + 1)
                gate(0)
                mult(0)
                round_(0)
                peeled = ROUND if t0 + 3 * FC == NT else 0
                with dve.Fori(0, (FC - 2 - peeled) // ROUND) as r:
                    for i in range(1, ROUND + 1):
                        round_(i, r)
                for i in range(FC - 1 - peeled, FC - 1):
                    round_(i)
                low(FC - 1)
                split(t0 + 3 * FC - 1 + AHEAD)

            def ffn_residual_step(st):
                q, ffn = st.k, st.u
                if q < 3:
                    dve.wait_ge(ffn_out, 3 * ffn.n + q + 1)
                else:
                    dve.wait_ge(tile_used, ffn.t + 3 * FC)
                v = x[:, 2 * q:2 * q + 2, 0:SEQ]
                dve.scalar_tensor_tensor(out=v, in0=ffn_bank[q][:, :].rearrange("p (c t) -> p c t", c=2),
                                         scalar=0.5, in1=v, op0=ALU.mult, op1=ALU.add).then_inc(ffn_added, 1)

            def conv_step_dve(st):
                c = st.c
                at = PARAM_AT["rec_conv_w"] + c
                w = [par[:, at + KC * i:at + KC * i + 1] for i in range(4)]
                b = PARAM_AT["rec_conv_b"] + c
                if c == 0:
                    dve.memset(r_pad[:, :, 0:3], 0.0).then_inc(mix_step, 1)
                scaled_product(st, r_pad[:, c, 3:], st.norm)
                dve.wait_ge(*evacuated(st.job))
                dve.wait_ge(mix_step, 1)
                dst = r_conv[:, c, :]
                dve.tensor_scalar(dst, r_pad[:, c, 0:SEQ], w[0], par[:, b:b + 1], ALU.mult, ALU.add)\
                    .then_inc(conv_step, 1)
                for i in range(1, 4):
                    dve.wait_ge(conv_step, 4 * c + i)
                    dve.scalar_tensor_tensor(out=dst, in0=r_pad[:, c, i:i + SEQ], scalar=w[i], in1=dst,
                                             op0=ALU.mult, op1=ALU.add).then_inc(conv_step, 1)

            def rec_decay_step(st):
                c = st.c
                dve.wait_ge(a_squared, c + 1)
                dve.scalar_tensor_tensor(out=th[:, c, :], in0=mix_t[:, c % 2, :], scalar=1.0, in1=th[:, c, :],
                                         op0=ALU.add, op1=ALU.mult).then_inc(root_in, 1)

            def rec_scan_step(st):
                c = st.c
                dve.wait_ge(bx_ready, c + 1)
                dve.wait_ge(decays, 2 * c + 2)
                dve.tensor_tensor_scan(r_conv[:, c, :], g_a[:, c, :], g_x[:, c, :], 0.0, ALU.mult, ALU.add)\
                    .then_inc(scanned, 1)

            def mix_low(c, n):
                dve.wait_ge(mix_hi_ready, n + 1)
                dve.tensor_tensor(mix_lo[:, c, :], mix_t[:, n % 2, :], mix_hi[:, c, :].bitcast(F32), ALU.subtract)\
                    .then_inc(mix_lo_ready, 1)

            def rec_out_step(st):
                c = st.c
                dve.wait_ge(y_ready, c + 1)
                dve.wait_ge(scanned, c + 1)
                if c >= 2:
                    dve.wait_ge(mix_lo_ready, st.n - 1)
                dve.tensor_tensor(mix_t[:, st.n % 2, :], y_act[:, c, :], r_conv[:, c, :], ALU.mult)\
                    .then_inc(mix_ready, 1)
                mix_low(c, st.n)

            def spatial_weights_step(st):
                for i in range(2):
                    dve.wait_ge(t_full, st.t_uses[i] + 1)
                    dve.tensor_copy(ws_t[:, 4 * i:4 * i + 4, :],
                                    T[st.t_uses[i] % 2][:, :].rearrange("p (h d) -> p h d", h=4))\
                        .then_inc(t_free[st.t_uses[i] % 2], 1)

            def sg_mix_step(st):
                c = st.c
                dve.wait_ge(s_full, st.s_use + 1)
                if c == 0:
                    dve.wait_ge(mix_landed, 6 * 16)
                if c >= 2:
                    dve.wait_ge(mix_lo_ready, KC + st.n - 1)
                q = mix_t[:, c % 2, :].rearrange("p (t d) -> p t d", t=2)
                s = S[st.s_use % 2][:, 0:SEQ].rearrange("p (t d) -> p t d", t=2)
                dve.tensor_tensor(q, s, ws_b[:, c, :].unsqueeze(1).to_broadcast([P, 2, P]), ALU.add)\
                    .then_inc(s_free[st.s_use % 2], 1)
                dve.wait_ge(*s_out(st.s_use))
                dve.wait_ge(u_ready, c + 1)
                dve.tensor_tensor(mix_t[:, c % 2, :], mix_t[:, c % 2, :], sg_u[:, c, :], ALU.mult)\
                    .then_inc(mix_ready, 1)
                mix_low(c, KC + st.n)

            run = {"split": lambda st: split(st.t), "turn_in": turn_in_step, "ada_turn": ada_turn_step,
                   "ada_scale": ada_scale_step, "rms": rms_step, "normed": normed_step, "value_turn": value_turn_step,
                   "split_x": split_x_step, "rec_y": rec_y_step, "sg_v": sg_v_step, "sg_u": sg_u_step,
                   "ffn_residual": ffn_residual_step, "gate": gate_step, "merge": merge_step, "gated_residual": gated_residual_step,
                   "plain_residual": plain_residual_step, "scores": scores_step, "turn_probs": turn_probs_step,
                   "values": values_step, "turn_out": turn_out_step, "ret_scores": ret_scores_step,
                   "ret_out": ret_out_step, "head_norm": head_norm_step, "head_spread": head_spread_step, "rotate": rotate_step, "ffn": ffn_step,
                   "conv": conv_step_dve, "rec_decay": rec_decay_step, "rec_scan": rec_scan_step,
                   "rec_out": rec_out_step, "spatial_weights": spatial_weights_step, "sg_mix": sg_mix_step}
            for st in steps:
                if st.kind in run:
                    run[st.kind](st)

        @block.tensor
        def _(pe):
            ident = C_("ident")

            def three(dst, w, hi, lo, start, stop, shared=False):
                slot, blk = w
                at = slice(P * blk, P * blk + P)
                nc.tensor.matmul(dst, w_hi[:, slot, at], hi, start=start, stop=False, skip_group_check=shared)
                nc.tensor.matmul(dst, w_hi[:, slot, at], lo, start=False, stop=False, skip_group_check=shared)
                return nc.tensor.matmul(dst, w_lo[:, slot, at], hi, start=False, stop=stop, skip_group_check=shared)

            def product_step(st):
                job = st.job
                n = job.cols
                dst = G[job.n % 2][:, 0:n]
                if st.at == 0:
                    pe.wait_ge(lo_ready, job.tile + 1)
                    if job.n >= 2:
                        pe.wait_ge(g_free[job.n % 2], job.n // 2)
                    if job.src.startswith("o_"):
                        pe.wait_ge(o_lo_ready, job.outs.out.n + 1)
                for i in range(st.at, st.at + st.part):
                    if job.src == "h":
                        if job.norm:
                            pe.wait_ge(h_lo_ready, job.norm.chunks[i].h + 1)
                        hi, lo = h_hi[:, i, 0:n], h_lo[:, i, 0:n]
                    elif job.src == "m":
                        if m_waited[0] < m_base(job) + i + 1:
                            m_waited[0] = m_base(job) + i + 1
                            pe.wait_ge(m_lo_ready, m_waited[0])
                        hi, lo = m_hi[:, i, 0:n], m_lo[:, i, 0:n]
                    elif job.src == "mix":
                        if mix_waited[0] < KC * job.mixer + i + 1:
                            mix_waited[0] = KC * job.mixer + i + 1
                            pe.wait_ge(mix_lo_ready, mix_waited[0])
                        hi, lo = mix_hi[:, i, :], mix_lo[:, i, :]
                    else:
                        o = o_of(job.src[2:])
                        hi, lo = o_hi[o][:, i, 0:n], o_lo[o][:, i, 0:n]
                    ins = three(dst, (job.tile % SPLIT, st.base + i), hi, lo, start=(i == 0), stop=(i == job.blocks - 1))
                if st.at + st.part == job.blocks:
                    ins.then_inc(half_used if job.first_half else tile_used, 1)

            def ada_tile_step(st):
                u, k, slot = st.u, st.k, st.tile % SPLIT
                pe.wait_ge(lo_ready, st.tile + 1)
                if k == 0:
                    pe.wait_ge(set_up_dve, 2)
                    for use in u.t_uses:
                        pe.wait_ge(t_free[use % 2], use // 2)
                for j, use in enumerate(u.t_uses):
                    dst, at = T[use % 2][0:4, :], slice(512 * j, 512 * j + 512)
                    nc.tensor.matmul(dst, c_split[:, k, :], w_hi[:, slot, at], start=(k == 0), stop=False)
                    ins = nc.tensor.matmul(dst, c_split[:, k, :], w_lo[:, slot, at], start=False, stop=(k == KC - 1))
                    if j == 0 and k == KC - 1:
                        ins.then_inc(t_full, 2)
                ins.then_inc(tile_used, 1)

            def ada_turn_step(st):
                u = st.u
                for use in u.t_uses:
                    pe.wait_ge(*t_out(use))
                pe.wait_ge(m_free, u.m)
                for k in range(KC):
                    ins = nc.tensor.matmul(M[:, 2 * k:2 * k + 2], ada_rows[u.n >= len(ADA_FIRST)][:, P * k:P * k + P], C_("parts")[0:4, :],
                                           start=True, stop=True)
                ins.then_inc(m_full, 1)

            m_waited, mix_waited = [0], [0]

            def m_base(job):
                return 0 if job.tile < TILES.index(("w_out", 1, 0)) else KC

            def turn_in_step(st):
                pe.wait_ge(con_landed, 16)
                pe.wait_ge(tok_landed, 32)
                if st.t_use >= 2:
                    pe.wait_ge(t_free[st.t_use % 2], st.t_use // 2)
                for b in range(4):
                    ins = nc.tensor.transpose(T[st.t_use % 2][:, P * b:P * b + P], tok[:, b, P * st.k:P * st.k + P], ident)
                ins.then_inc(t_full, 1)

            def rms_step(st):
                norm_mean(st.norm)
                norm_spread(st.norm)

            def norm_mean(norm):
                c, halves = norm.cols, norm.units[0].blocks
                pe.wait_ge(sq_added, norm.units[-2].add_n + 1)
                pe.wait_ge(squared, norm.units[-1].n + 1)
                squares = [v[:, c * j:c * j + c] for v in (sum_sq, square_of(norm.units[-1])) for j in range(halves)]
                if norm.m:
                    pe.wait_ge(m_free, norm.m)
                for b in range(c // P):
                    for v in squares:
                        ins = nc.tensor.matmul(M[:, b:b + 1], v[:, P * b:P * b + P], C_("ones"),
                                               start=v is squares[0], stop=v is squares[-1])
                ins.then_inc(m_full, 1)

            def norm_spread(norm):
                pe.wait_ge(rstd_rows, norm.rows + 1)
                pe.wait_ge(m_free, norm.m_spread)
                for b in range(norm.cols // P):
                    ins = nc.tensor.matmul(M[:, P * b:P * b + P], row_rstd[:, b:b + 1].to_broadcast([P, P]), ident,
                                           start=True, stop=True)
                ins.then_inc(m_full, 1)

            def normed_step(st):
                if st.norm.how != "out":
                    return
                pe.wait_ge(f_ready, st.f + 1)
                pe.wait_ge(t_free[st.t_use % 2], st.t_use // 2)
                for b in range(2):
                    ins = nc.tensor.transpose(T[st.t_use % 2][:, P * b:P * b + P],
                                              scaled[:, st.k % 2, P * b:P * b + P], ident)
                ins.then_inc(t_full, 1)

            def value_turn_step(st):
                pe.wait_ge(*evacuated(st.evac.job))
                pe.wait_ge(m_free, st.m)
                for b in range(4):
                    ins = nc.tensor.transpose(M[:, P * b:P * b + P], stage[:, P * b:P * b + P], ident)
                ins.then_inc(m_full, 1)

            def scores_step(st):
                u = st.u
                g = u.g
                if g.branch == "na":
                    pe.wait_ge(*evacuated(g.k_job.job))
                    pe.wait_ge(*evacuated(g.q_job.job))
                else:
                    pe.wait_ge(rot_done, g.q_rot.n + 1)
                if u.s_use >= 2:
                    pe.wait_ge(s_free[u.s_use % 2], u.s_use // 2)
                at = slice(DH * u.hp, DH * u.hp + DH)
                nc.tensor.matmul(S[u.s_use % 2][:, 0:u.keys], g_buf(g, "q")[at, P * u.b:P * u.b + P],
                                 g_buf(g, "k")[at, u.key_at:u.key_at + u.keys], start=True, stop=True)\
                    .then_inc(s_full, 1)

            def turn_probs_step(st):
                u = st.u
                pe.wait_ge(*s_out(u.s_use))
                if u.t_use >= 2:
                    pe.wait_ge(t_free[u.t_use % 2], u.t_use // 2)
                for j in range(u.keys // P):
                    ins = nc.tensor.transpose(T[u.t_use % 2][:, P * j:P * j + P], probs[:, u.n % 2, P * j:P * j + P],
                                              ident)
                ins.then_inc(t_full, 1)

            def values_step(st):
                u = st.u
                g = u.g.kv if u.g.branch == "gqa" else u.g
                pe.wait_ge(*t_out(u.t_use))
                if u.o_use:
                    pe.wait_ge(o_free, u.o_use)
                pe.wait_ge(m_free, g.v_turn.m + 1)
                v = g_buf(g, "v")
                blocks = list(key_blocks(u))
                for i, j in enumerate(blocks):
                    ins = nc.tensor.matmul(O[:, 0:DH], probs_t[:, u.n % 2, P * i:P * i + P],
                                           v[:, j, DH * u.hp:DH * u.hp + DH], start=(i == 0),
                                           stop=(i == len(blocks) - 1))
                ins.then_inc(o_full, 1)

            def turn_out_step(st):
                g = st.g
                pe.wait_ge(o_free, (g.ret_out.o_use if g.branch == "ret" else g.last_unit.o_use) + 1)
                pe.wait_ge(m_free, st.m)
                for b in range(g.blocks):
                    ins = nc.tensor.transpose(M[:, P * b:P * b + P], out_rows[:, b, :], ident)
                ins.then_inc(m_full, 1)

            def ret_scores_step(st):
                g = st.g
                pe.wait_ge(*evacuated(g.k_job.job))
                pe.wait_ge(*evacuated(g.q_job.job))
                if st.s_use >= 2:
                    pe.wait_ge(s_free[st.s_use % 2], st.s_use // 2)
                nc.tensor.matmul(S[st.s_use % 2][:, 0:st.cols], g_buf(g, "k")[:, P * st.j:P * st.j + P],
                                 g_buf(g, "q")[:, 0:st.cols], start=True, stop=True).then_inc(s_full, 1)

            def ret_out_step(st):
                g = st.g
                pe.wait_ge(*s_out(g.last_scores.s_use))
                pe.wait_ge(m_free, g.v_turn.m + 1)
                if st.o_use:
                    pe.wait_ge(o_free, st.o_use)
                v = g_buf(g, "v")
                for b in range(g.blocks):
                    keys = range(4) if b < 2 else range(2, 4)
                    for j in keys:
                        ins = nc.tensor.matmul(O[:, P * b:P * b + P], work[:, j, P * b:P * b + P], v[:, j, :],
                                               start=(j == keys[0]), stop=(j == 3))
                ins.then_inc(o_full, 1)

            def head_norm_step(st):
                pe.wait_ge(*evacuated(st.job))
                pe.wait_ge(m_free, st.m)
                for b in range(st.cols // P):
                    ins = nc.tensor.matmul(M[:, 2 * b:2 * b + 2], head_sq[:, P * b:P * b + P], C_("heads"), start=True,
                                           stop=True)
                ins.then_inc(m_full, 1)

            def head_spread_step(st):
                pe.wait_ge(rstd_rows, st.norm.rows + 1)
                pe.wait_ge(m_free, st.m)
                for b in range(st.cols // P):
                    for j in range(2):
                        w = row_rstd[:, 2 * b + j:2 * b + j + 1].to_broadcast([P, DH])
                        ins = nc.tensor.matmul(M[DH * j:DH * j + DH, P * b:P * b + P], w, ident, start=True, stop=True)
                ins.then_inc(m_full, 1)

            def rotate_step(st):
                pe.wait_ge(m_free, st.norm.spread.m + 1)
                pe.wait_ge(m_free, st.m)
                dst = g_buf(st.g, "k" if st.what == "key" else "q")
                nc.tensor.matmul(M[:, 0:SEQ], C_("swap"), dst[:, 0:SEQ], start=True, stop=True).then_inc(m_full, 1)

            def ffn_step(st):
                f, t0, norm = st.n, st.t, st.norm

                def up(i, which, r=None, first=False):
                    t = t0 + ffn_tile(which, i)
                    base, cnt = (0, 0) if r is None else (r * (3 * ROUND), r * ROUND)
                    pe.wait_ge(lo_ready, base + (t + 1))
                    if i < 2:
                        bank_free, uses = (g_free, st.job) if which == "g" else (s_free, st.s_use)
                        pe.wait_ge(bank_free[i], (uses + 1 - i) // 2)
                    else:
                        pe.wait_ge(gate_scaled if which == "g" else hid_ready, cnt + (FC * f + i - 1))
                    dst = (G if which == "g" else S)[i % 2][:, 0:SEQ]
                    for k in range(KC):
                        if first:
                            pe.wait_ge(h_lo_ready, norm.chunks[k].h + 1)
                        ins = three(dst, (t % SPLIT, k), h_hi[:, k, 0:SEQ], h_lo[:, k, 0:SEQ], k == 0, k == KC - 1)
                    ins.then_inc(tile_used, 1)

                def down(i, r=None, last=False):
                    t = t0 + ffn_tile("o", i)
                    base, cnt = (0, 0) if r is None else (r * (3 * ROUND), r * ROUND)
                    pe.wait_ge(lo_ready, base + (t + 1))
                    pe.wait_ge(hid_lo_ready, cnt + (FC * f + i + 1))
                    for dc in range(KC):
                        dst = ffn_bank[dc // 2][:, SEQ * (dc % 2):SEQ * (dc % 2) + SEQ]
                        ins = three(dst, (t % SPLIT, dc), hid_hi[:, i % 2, :], hid_lo[:, i % 2, :],
                                    i == 0 and dc % 2 == 0, last, shared=True)
                        if last and dc % 2 and dc < KC - 1:
                            ins.then_inc(ffn_out, 1)
                    ins.then_inc(tile_used, 1)

                def round_(i, r=None):
                    up(i + 1, "g", r)
                    up(i + 1, "u", r)
                    down(i, r)

                up(0, "g", first=True)
                norm_mean(norm)
                up(0, "u")
                norm_spread(norm)
                round_(0)
                with pe.Fori(0, (FC - 2) // ROUND) as r:
                    for i in range(1, ROUND + 1):
                        round_(i, r)
                down(FC - 1, last=True)

            def rec_gates_step(st):
                if st.c == 0:
                    pe.wait_ge(mix_landed, 64)
                pe.wait_ge(conv_step, 4 * st.c + 4)
                pe.wait_ge(s_free[st.s_use % 2], st.s_use // 2)
                s = S[st.s_use % 2]
                nc.tensor.matmul(s[:, 0:SEQ], gate_w[:, 0, st.c, :], r_conv[:, st.c, :], start=True, stop=True)
                nc.tensor.matmul(s[:, SEQ:BOTH], gate_w[:, 1, st.c, :], r_conv[:, st.c, :], start=True, stop=True)\
                    .then_inc(s_full, 1)

            def spatial_weights_step(st):
                pe.wait_ge(ws_cut, 1)
                pe.wait_ge(ffn_added, 4 * 3)
                for i in range(2):
                    u = st.t_uses[i]
                    pe.wait_ge(t_free[u % 2], u // 2)
                    for h in range(4):
                        ins = nc.tensor.transpose(T[u % 2][:, P * h:P * h + P], ws[:, 4 * i + h, :], ident)
                    ins.then_inc(t_full, 1)

            def sg_turn_step(st):
                pe.wait_ge(v_normed, st.c + 1)
                pe.wait_ge(t_free[st.t_use % 2], st.t_use // 2)
                for b in range(2):
                    ins = nc.tensor.transpose(T[st.t_use % 2][:, P * b:P * b + P], sg_v[:, st.c, P * b:P * b + P],
                                              ident)
                ins.then_inc(t_full, 1)

            def sg_mix_step(st):
                pe.wait_ge(*t_out(st.turn.t_use))
                pe.wait_ge(s_free[st.s_use % 2], st.s_use // 2)
                for b in range(2):
                    ins = nc.tensor.matmul(S[st.s_use % 2][:, P * b:P * b + P], sg_vt[:, st.c % 2, P * b:P * b + P],
                                           ws_t[:, st.c, :], start=True, stop=True)
                ins.then_inc(s_full, 1)

            run = {"product": product_step, "ada_tile": ada_tile_step, "ada_turn": ada_turn_step, "turn_in": turn_in_step, "rms": rms_step,
                   "normed": normed_step, "value_turn": value_turn_step, "scores": scores_step,
                   "turn_probs": turn_probs_step, "values": values_step, "turn_out": turn_out_step,
                   "ret_scores": ret_scores_step, "ret_out": ret_out_step, "head_norm": head_norm_step,
                   "head_spread": head_spread_step, "rotate": rotate_step, "ffn": ffn_step, "rec_gates": rec_gates_step,
                   "spatial_weights": spatial_weights_step, "sg_turn": sg_turn_step, "sg_mix": sg_mix_step}
            for st in steps:
                if st.kind in run:
                    run[st.kind](st)


def kernel(**inputs):
    from concourse import bacc
    from concourse.bass_utils import run_bass_kernel_spmd

    a = {name: np.ascontiguousarray(v) for name, v in inputs.items()}
    arrays = {
        "weights": lay_out_weights(a),
        "params": lay_out_params(a),
        "consts": shape_tables(),
        "tokens": np.concatenate([a["x"][0], a["ctx"][0]]),
        "rpb": lay_out_bias(a["na_rpb"]),
        "gate_a": a["rec_gate_a_w_2"][0],
        "gate_x": a["rec_gate_x_w_2"][0],
        "spatial": a["sg_w_s_2"][0],
        "spatial_b": a["sg_b_s_2"][0],
    }
    arrays = {name: np.ascontiguousarray(v) for name, v in arrays.items()}
    nc = bacc.Bacc("TRN2", target_bir_lowering=False, num_devices=1)
    args = [nc.dram_tensor(f"in_{n}", v.shape, F32, kind="ExternalInput").ap() for n, v in arrays.items()]
    args.append(nc.dram_tensor("out", (SEQ, D), F32, kind="ExternalOutput").ap())
    block_kernel(nc, *args)
    r = run_bass_kernel_spmd(nc, [{f"in_{n}": v for n, v in arrays.items()}], core_ids=[0])
    return r.results[0]["out"].reshape(1, SEQ, D)
```
